# Optimizing a Trainium2 kernel written in Bass

```python
import jax, jax.numpy as jnp
from jax import lax
import numpy as np

D_MODEL = 1024
BATCH = 1
SEQ = 256
DEPTH = 1

HEAD_DIM = 64
RWKV_HEADS = 8
RWKV_WIDTH = RWKV_HEADS * HEAD_DIM
DECAY_LORA = 64
AAA_LORA = 64
GATE_LORA = 128
RWKV_PROJ_WIDTH = 3 * RWKV_WIDTH + DECAY_LORA + AAA_LORA + GATE_LORA
GN_EPS = 64e-5
MOBA_HEADS = 8
MOBA_WIDTH = MOBA_HEADS * HEAD_DIM
MOBA_BLOCK = 256
MOBA_TOP_K = 3
MOBA_Q_CHUNK = 64
IN_WIDTH = RWKV_PROJ_WIDTH + 3 * MOBA_WIDTH + 2 * D_MODEL
N_EXPERTS = 32
EXPERT_TOP_K = 4
D_FF = D_MODEL
SWIGLU_LIMIT = 7.0
SWIGLU_ALPHA = 1.702
RMS_EPS = 1e-5
GATE_NEG = -1e30

kernel_name = "hybrid_rwkv7_moba_moe_adaln_block"

def rms_norm(x, g):
    xf = x.astype(jnp.float32)
    y = xf * lax.rsqrt(jnp.mean(xf * xf, axis=-1, keepdims=True) + RMS_EPS)
    return (y * g.astype(jnp.float32)).astype(x.dtype)

def rwkv7_mixer(p, mu, w0, w2, a0, a2, g2, k_k, k_a, r_k, ln_w, ln_b):
    B, T, _ = p.shape
    H, N = RWKV_HEADS, HEAD_DIM
    p_prev = jnp.pad(p, ((0, 0), (1, 0), (0, 0)))[:, :-1]
    ps = p + (p_prev - p) * mu
    cuts = [RWKV_WIDTH, 2 * RWKV_WIDTH, 3 * RWKV_WIDTH,
            3 * RWKV_WIDTH + DECAY_LORA, 3 * RWKV_WIDTH + DECAY_LORA + AAA_LORA]
    r, k, v, xw, xa, xg = jnp.split(ps, cuts, axis=-1)
    w = -jax.nn.softplus(-(w0 + jnp.tanh(xw) @ w2)) - 0.5
    a = jax.nn.sigmoid(a0 + xa @ a2)
    g = jax.nn.sigmoid(xg) @ g2
    f32 = jnp.float32
    kk = (k * k_k).astype(f32).reshape(B, T, H, N)
    kk = kk / jnp.maximum(jnp.sqrt(jnp.sum(kk * kk, axis=-1, keepdims=True)), 1e-12)
    k = k * (1 + (a - 1) * k_a)
    decay = jnp.exp(-jnp.exp(w.astype(f32))).reshape(B, T, H, N)
    r_h = r.astype(f32).reshape(B, T, H, N)
    k_h = k.astype(f32).reshape(B, T, H, N)
    v_h = v.astype(f32).reshape(B, T, H, N)
    a_h = a.astype(f32).reshape(B, T, H, N)
    vec_a = -kk
    vec_b = kk * a_h

    def step(S, inp):
        r_t, w_t, k_t, v_t, a_t, b_t = inp
        sa = jnp.einsum('bhij,bhj->bhi', S, a_t)
        S = S * w_t[:, :, None, :] + sa[..., None] * b_t[:, :, None, :] + v_t[..., None] * k_t[:, :, None, :]
        return S, jnp.einsum('bhij,bhj->bhi', S, r_t)

    xs = tuple(jnp.moveaxis(t, 1, 0) for t in (r_h, decay, k_h, v_h, vec_a, vec_b))
    _, y = lax.scan(step, jnp.zeros((B, H, N, N), f32), xs)
    y = jnp.moveaxis(y, 0, 1)
    mean = jnp.mean(y, axis=-1, keepdims=True)
    var = jnp.mean(jnp.square(y - mean), axis=-1, keepdims=True)
    y = ((y - mean) * lax.rsqrt(var + GN_EPS)).reshape(B, T, H * N)
    y = y * ln_w.astype(f32) + ln_b.astype(f32)
    bonus = jnp.sum(r_h * k_h * r_k.astype(f32), axis=-1, keepdims=True) * v_h
    y = y + bonus.reshape(B, T, H * N)
    return (y * g.astype(f32)).astype(p.dtype)

def moba_attention(q, k, v):
    B, T, H, Dh = q.shape
    BS, QC = MOBA_BLOCK, MOBA_Q_CHUNK
    NB = -(-T // BS)
    Tp = NB * BS
    pad = ((0, 0), (0, Tp - T), (0, 0), (0, 0))
    q, k, v = jnp.pad(q, pad), jnp.pad(k, pad), jnp.pad(v, pad)
    scale = Dh ** -0.5
    k_blk = k.reshape(B, NB, BS, H, Dh).transpose(0, 3, 1, 2, 4)
    v_blk = v.reshape(B, NB, BS, H, Dh).transpose(0, 3, 1, 2, 4)
    n_sel = min(MOBA_TOP_K, NB - 1)
    q_blk_id = jnp.arange(Tp) // BS
    if n_sel > 0:
        k_mean = jnp.mean(k_blk[:, :, :NB - 1].astype(jnp.float32), axis=3)
        gate = jnp.einsum('bthd,bhnd->bhtn', q.astype(jnp.float32), k_mean)
        past = jnp.arange(NB - 1)[None, :] < q_blk_id[:, None]
        gate = jnp.where(past, gate, GATE_NEG)
        _, sel_idx = lax.top_k(gate, n_sel)
    NC = Tp // QC
    q_c = q.reshape(B, NC, QC, H, Dh).transpose(1, 0, 3, 2, 4)
    b_ix = jnp.arange(B)[:, None, None, None]
    h_ix = jnp.arange(H)[None, :, None, None]
    key_off = jnp.arange(BS)

    def chunk(args):
        qc, ci = args
        start = ci * QC
        blk = start // BS
        q_off = start - blk * BS + jnp.arange(QC)
        k_own = lax.dynamic_index_in_dim(k_blk, blk, axis=2, keepdims=False)
        v_own = lax.dynamic_index_in_dim(v_blk, blk, axis=2, keepdims=False)
        s_own = jnp.einsum('bhqd,bhkd->bhqk', qc, k_own).astype(jnp.float32) * scale
        s_own = jnp.where(key_off[None, :] <= q_off[:, None], s_own, -jnp.inf)
        if n_sel == 0:
            p = jax.nn.softmax(s_own, axis=-1).astype(v.dtype)
            return jnp.einsum('bhqk,bhkd->bhqd', p, v_own)
        ic = lax.dynamic_slice_in_dim(sel_idx, start, QC, axis=2)
        k_sel = k_blk[b_ix, h_ix, ic]
        v_sel = v_blk[b_ix, h_ix, ic]
        s_sel = jnp.einsum('bhqd,bhqnkd->bhqnk', qc, k_sel).astype(jnp.float32) * scale
        s_sel = jnp.where((ic < blk)[..., None], s_sel, -jnp.inf)
        s = jnp.concatenate([s_sel.reshape(B, H, QC, n_sel * BS), s_own], axis=-1)
        p = jax.nn.softmax(s, axis=-1).astype(v.dtype)
        p_sel = p[..., :n_sel * BS].reshape(B, H, QC, n_sel, BS)
        p_own = p[..., n_sel * BS:]
        return (jnp.einsum('bhqnk,bhqnkd->bhqd', p_sel, v_sel)
                + jnp.einsum('bhqk,bhkd->bhqd', p_own, v_own))

    out = lax.map(chunk, (q_c, jnp.arange(NC)))
    out = out.transpose(1, 0, 3, 2, 4).reshape(B, Tp, H, Dh)
    return out[:, :T]

def moe_ffn(h, router_w, router_b, w_gate, b_gate, w_up, b_up, w_down, b_down):
    logits = (h @ router_w + router_b).astype(jnp.float32)
    top_v, top_i = lax.top_k(logits, EXPERT_TOP_K)
    top_w = jax.nn.softmax(top_v, axis=-1)
    comb = jnp.sum(jax.nn.one_hot(top_i, N_EXPERTS, dtype=jnp.float32) * top_w[..., None], axis=-2)
    comb = comb.astype(h.dtype)
    y = jnp.zeros_like(h)
    for e in range(N_EXPERTS):
        gt = jnp.minimum(h @ w_gate[e] + b_gate[e], SWIGLU_LIMIT)
        up = jnp.clip(h @ w_up[e] + b_up[e], -SWIGLU_LIMIT, SWIGLU_LIMIT)
        hid = (up + 1) * gt * jax.nn.sigmoid(SWIGLU_ALPHA * gt)
        y = y + comb[..., e:e + 1] * (hid @ w_down[e] + b_down[e])
    return y

def setup_inputs(seed: int = 0) -> dict:
    key = jax.random.key(seed)
    ks = jax.random.split(key, 32)
    D, F, E = D_MODEL, D_FF, N_EXPERTS
    nrm = lambda k, shape, s: jax.random.normal(k, shape, jnp.float32) * s
    return {
        "x": nrm(ks[0], (BATCH, SEQ, D), 1.0),
        "c": nrm(ks[1], (BATCH, D), 1.0),
        "w_ada": nrm(ks[2], (D, 6 * D), D ** -0.5),
        "b_ada": nrm(ks[3], (6 * D,), 0.02),
        "norm1_g": 1.0 + nrm(ks[4], (D,), 0.02),
        "w_in": nrm(ks[5], (D, IN_WIDTH), D ** -0.5),
        "rwkv_mu": jax.random.uniform(ks[6], (RWKV_PROJ_WIDTH,), jnp.float32),
        "rwkv_w0": jax.random.uniform(ks[7], (RWKV_WIDTH,), jnp.float32, -6.0, -1.0),
        "rwkv_w2": nrm(ks[8], (DECAY_LORA, RWKV_WIDTH), 0.1 * DECAY_LORA ** -0.5),
        "rwkv_a0": nrm(ks[9], (RWKV_WIDTH,), 0.5),
        "rwkv_a2": nrm(ks[10], (AAA_LORA, RWKV_WIDTH), 0.1 * AAA_LORA ** -0.5),
        "rwkv_g2": nrm(ks[11], (GATE_LORA, RWKV_WIDTH), GATE_LORA ** -0.5),
        "rwkv_k_k": 0.85 + nrm(ks[12], (RWKV_WIDTH,), 0.02),
        "rwkv_k_a": 1.0 + nrm(ks[13], (RWKV_WIDTH,), 0.02),
        "rwkv_r_k": nrm(ks[14], (RWKV_HEADS, HEAD_DIM), 0.1),
        "rwkv_ln_w": 1.0 + nrm(ks[15], (RWKV_WIDTH,), 0.02),
        "rwkv_ln_b": nrm(ks[16], (RWKV_WIDTH,), 0.02),
        "w_branch_a": nrm(ks[17], (RWKV_WIDTH, D), RWKV_WIDTH ** -0.5),
        "w_branch_b": nrm(ks[18], (MOBA_WIDTH, D), MOBA_WIDTH ** -0.5),
        "w_out": nrm(ks[19], (D, D), D ** -0.5),
        "norm2_g": 1.0 + nrm(ks[20], (D,), 0.02),
        "router_w": nrm(ks[21], (D, E), D ** -0.5),
        "router_b": nrm(ks[22], (E,), 0.01),
        "exp_w_gate": nrm(ks[23], (E, D, F), D ** -0.5),
        "exp_b_gate": nrm(ks[24], (E, F), 0.02),
        "exp_w_up": nrm(ks[25], (E, D, F), D ** -0.5),
        "exp_b_up": nrm(ks[26], (E, F), 0.02),
        "exp_w_down": nrm(ks[27], (E, F, D), F ** -0.5),
        "exp_b_down": nrm(ks[28], (E, D), 0.02),
        "normf_g": 1.0 + nrm(ks[29], (D,), 0.02),
    }

def reference(x, c, w_ada, b_ada, norm1_g, w_in, rwkv_mu, rwkv_w0, rwkv_w2, rwkv_a0, rwkv_a2,
              rwkv_g2, rwkv_k_k, rwkv_k_a, rwkv_r_k, rwkv_ln_w, rwkv_ln_b, w_branch_a, w_branch_b,
              w_out, norm2_g, router_w, router_b, exp_w_gate, exp_b_gate, exp_w_up, exp_b_up,
              exp_w_down, exp_b_down, normf_g):
    B, T, D = x.shape
    mod = (jax.nn.silu(c) @ w_ada + b_ada)[:, None, :]
    shift1, scale1, gate1, shift2, scale2, gate2 = jnp.split(mod, 6, axis=-1)
    cuts = [RWKV_PROJ_WIDTH, RWKV_PROJ_WIDTH + MOBA_WIDTH, RWKV_PROJ_WIDTH + 2 * MOBA_WIDTH,
            RWKV_PROJ_WIDTH + 3 * MOBA_WIDTH, RWKV_PROJ_WIDTH + 3 * MOBA_WIDTH + D]
    for _ in range(DEPTH):
        h = rms_norm(x, norm1_g) * (1 + scale1) + shift1
        proj = h @ w_in
        p_rwkv, q, k, v, g_a, g_b = jnp.split(proj, cuts, axis=-1)
        y_a = rwkv7_mixer(p_rwkv, rwkv_mu, rwkv_w0, rwkv_w2, rwkv_a0, rwkv_a2, rwkv_g2,
                          rwkv_k_k, rwkv_k_a, rwkv_r_k, rwkv_ln_w, rwkv_ln_b) @ w_branch_a
        heads = lambda t: t.reshape(B, T, MOBA_HEADS, HEAD_DIM)
        y_b = moba_attention(heads(q), heads(k), heads(v)).reshape(B, T, MOBA_WIDTH) @ w_branch_b
        mixed = (jax.nn.sigmoid(g_a) * y_a + jax.nn.sigmoid(g_b) * y_b) @ w_out
        x = x + gate1 * mixed
        h2 = rms_norm(x, norm2_g) * (1 + scale2) + shift2
        x = x + gate2 * moe_ffn(h2, router_w, router_b, exp_w_gate, exp_b_gate, exp_w_up,
                                exp_b_up, exp_w_down, exp_b_down)
    return rms_norm(x, normf_g)


_drawn_inputs = setup_inputs


def setup_inputs(seed=0):
    import zlib

    import numpy as np

    out = dict(_drawn_inputs(seed))
    spreads = {}
    factors = {'rwkv_w2': 3.357,
     'rwkv_ln_w': 10.514,
     'rwkv_ln_b': 11.446,
     'router_b': 9.14,
     'exp_b_gate': 8.0,
     'exp_b_up': 21.741,
     'exp_b_down': 8.0,
     'normf_g': 26.751,
     'norm2_g': 4.015}
    for name, (base, spread) in spreads.items():
        noise = np.random.default_rng([zlib.crc32(name.encode()), seed]).standard_normal(out[name].shape)
        drawn = base * np.exp(spread * noise) if base else spread * noise
        out[name] = __import__('jax').numpy.asarray(drawn.astype(out[name].dtype))
    for name, factor in factors.items():
        out[name] = (out[name] * factor).astype(out[name].dtype)
    return out
```

```python
from contextlib import ExitStack

import concourse.bass as bass
from concourse import mybir

F32 = mybir.dt.float32
BF16 = mybir.dt.bfloat16
I32 = mybir.dt.int32
U32 = mybir.dt.uint32
ALU = mybir.AluOpType
ACT = mybir.ActivationFunctionType
AX_X = mybir.AxisListType.X

P = 128
D = 1024
T = 256
TT = T // P
KC = D // P
HD = 64
RH = 8
HP = RH // 2
W = RH * HD
NE = 32
TOPK = 4
SLOTS = 64
PAIRS = NE // 2
MORE = T // SLOTS - 1
MAX_TURNS = T * TOPK // SLOTS
LIMIT = 7.0
ALPHA = 1.702
RMS_EPS = 1e-5
GN_EPS = 64e-5
NEG = -1e30
LAM = 0.6065306597126334
SCALE = HD ** -0.5
MID = HD - 1

VECS = [("c", 8), ("norm1_g", 8), ("rwkv_mu", 14), ("rwkv_w0", 4), ("rwkv_a0", 4), ("rwkv_k_k", 4),
        ("rwkv_k_a", 4), ("rwkv_r_k", 4), ("rwkv_ln_w", 4), ("rwkv_ln_b", 4)]
NVEC = sum(n for _, n in VECS)

UNITS = [("lora", 3 * W, 256), ("k", W, 512), ("r", 0, 512), ("v", 2 * W, 512),
         ("q", 1792, 512), ("km", 2304, 512), ("vm", 2816, 512),
         ("ga", 3328, 512), ("ga", 3840, 512), ("gb", 4352, 512), ("gb", 4864, 512)]
TILES = []
for _u, (_kind, _c0, _w) in enumerate(UNITS):
    if _kind == "vm":
        TILES += [("vm", _u, 0, c) for c in range(TT)]
    else:
        _at = {"r": 0, "k": 4, "v": 8, "lora": 12, "q": 0, "km": 4, "ga": 0, "gb": 8}[_kind]
        _at += 4 if _kind in ("ga", "gb") and UNITS[_u - 1][0] == _kind else 0
        TILES += [(_kind, _u, 128 * j, _at + j) for j in range(_w // 128)]
UNIT_END = {u: max(n for n, t in enumerate(TILES) if t[1] == u) for u in range(len(UNITS))}
COL_BANK = (0, 1, 6, 7)
ADA = 4
U_ADA1 = ADA + len(UNITS)
U_BRANCH = U_ADA1 + 8
U_OUT = U_BRANCH + 2
N_UNITS = U_OUT + 2
AFTER_LORA, AFTER_KK, AFTER_V, AFTER_SCORES, AFTER_PT, AFTER_PV = 10, 18, 22, 24, 28, 30


def place(h):
    return (h % 2) * HP + h // 2


def level_index(c, k, what, g):
    n = c * 34 + (k - 1) * 6
    if what == "T":
        return n + g
    return n + 2 + (2 * g + (what == "N") if k < 6 else g)


def block_kernel(nc, A, out, scratch, dbg=None):
    ctx = ExitStack()
    with ctx:
        def sb(name, n, dt=F32, parts=P):
            return ctx.enter_context(nc.sbuf_tensor(name, [parts, n], dt))

        ring = ctx.enter_context(nc.sbuf_tensor("ring", [P, 4, KC * D], F32))
        PS = ctx.enter_context(nc.psum_tensor("PS", [P, 8, 512], F32))

        lmask_t = sb("lmask_t", 1024)
        lmask = lmask_t[:, 0:896].rearrange("p (k t) -> p k t", k=7)
        lmask0L = lmask_t[:, 896:1024]
        ident_t = sb("ident_t", 128)
        blk_t = sb("blk_t", 128)
        ones_t = sb("ones_t", 128)
        ident, blk, ones = ident_t[:, :], blk_t[:, :], ones_t[:, :]
        maskU_t = sb("maskU_t", 256)
        maskU = maskU_t[:, :].rearrange("p (a t) -> p a t", a=2)
        maskL = sb("maskL", 128)[:, :]
        negmask = sb("negmask", 128)[:, :]
        iota64 = sb("iota64", 64)[:, :]
        iota32 = sb("iota32", 32)[:, :]
        x_sb = sb("x_sb", TT * D)
        x3 = x_sb[:, :].rearrange("p (a d) -> p a d", a=TT)
        colrows = sb("colrows", 128)
        cols = sb("cols", 64)
        scr = sb("scr", KC * 32)[:, :].rearrange("p (k m) -> p k m", k=KC)
        modrow = sb("modrow", 512)
        hT_t = sb("hT_t", KC * T)
        hT = hT_t[:, :].rearrange("p (k t) -> p k t", k=KC)
        PR_t = sb("PR_t", 14 * 257)
        PR = PR_t[:, :].rearrange("p (j t) -> p j t", j=14)
        QK_t = sb("QK_t", 8 * T)
        QK = QK_t[:, :].rearrange("p (j t) -> p j t", j=8)
        VM_t = sb("VM_t", TT * 512)
        VM = VM_t[:, :].rearrange("p (a d) -> p a d", a=TT)
        GAB_t = sb("GAB_t", 16 * T)
        GAB = GAB_t[:, :].rearrange("p (j t) -> p j t", j=16)
        WG = sb("WG", 1024)
        rw = sb("rw", KC * NE)[:, :].rearrange("p (k e) -> p k e", k=KC)
        rbias = sb("rbias", NE)[:, :]
        small = sb("small", 96)
        eye3 = sb("eye3", 32)
        selb_t = sb("selb", 2 * SLOTS, BF16)
        selb = selb_t[:, :].rearrange("p (b s) -> p b s", b=2)

        sh1c, s1c, sigc = small[:, 0:8], small[:, 8:16], small[:, 16:24]
        ss, rstd = small[:, 24:26], small[:, 26:28]
        decay_end = small[:, 28:32]
        mx, sums = small[:, 32:48], small[:, 48:64]
        eps_gn, eps_rms = small[:, 64:65], small[:, 65:66]
        ss2, rstd2, ss3, rstd3 = small[:, 66:68], small[:, 68:70], small[:, 70:72], small[:, 72:74]
        dsum = small[:, 76:80]
        off, v = {}, 0
        for name, n in VECS:
            off[name] = v
            v += n

        def col(name, j, n=1):
            return cols[:, off[name] + j:off[name] + j + n]

        def over(ap, n):
            return ap.unsqueeze(2).broadcast_to([ap.shape[0], ap.shape[1], n])

        def unit(u):
            return ring[:, (u % 4) // 2, (u % 2) * 4096:(u % 2) * 4096 + 4096]

        TMP = ring[:, 2:4, :].rearrange("p a n -> p (a n)")
        heads = lambda a: a.rearrange("p (h t) -> p h t", h=RH)
        pairs = lambda a: a.rearrange("p (q t) -> p q t", q=HP)
        XS, Nm, Mm = (heads(TMP[:, 1024 * i:1024 * i + 1024]) for i in range(3))
        BK = TMP[:, 3072:7168].rearrange("p (h j a t) -> p h j a t", h=RH, j=2, a=2)
        TL = BK[:, :, 0, 0, :]
        AR = TMP[:, 7168:9216].rearrange("p (q c a t) -> p q c a t", q=HP, c=TT, a=2)
        Bf, K2f, SIGf, Af, KKf, Gf, VTf = (TMP[:, 9216 + 1024 * i:10240 + 1024 * i] for i in range(7))
        VT = VTf.rearrange("p (c d) -> p c d", c=TT)
        Rs, Us = KKf[:, 0:512], KKf[:, 512:1024]
        S1 = SIGf[:, 0:256].rearrange("p (q d) -> p q d", q=HP)
        YTf = Af
        bada0 = TMP[:, 0:512]
        xn = TMP[:, 7168:9216].rearrange("p (a d) -> p a d", a=TT)
        same = TMP[:, 2048:3072].rearrange("p (k t) -> p k t", k=8)
        Cf, Ccf, E1f, E2f, DIFf, NRMf, SQf = (TMP[:, 1024 * i:1024 * i + 1024] for i in range(7))
        att = TMP[:, 0:3072].rearrange("p (h t) -> p h t", h=RH)
        PT = TMP[:, 3072:6144].rearrange("p (b h t) -> p b h t", b=3, h=RH)
        w2, a2, g2 = WG[0:64, 0:512], WG[64:128, 0:512], WG[:, 512:1024]
        Btok, Ktok = WG[:, 0:512], WG[:, 512:1024]
        YB = QK[:, 0:4, :]
        gate1b = QK_t[:, 1024:2048]
        scale2b, shift2b = VM_t[:, :], WG[:, :]
        bada12 = hT_t[:, 0:1024].rearrange("p (r n) -> p r n", r=2)
        modrow12 = hT_t[:, 1024:2048].rearrange("p (r n) -> p r n", r=2)
        YF = PR[:, 0:4, 1:257]
        BON = PR[:, 4:8, 1:257]
        norm2b = PR_t[:, 2056:3080]
        zT = hT

        h2 = hT_t[:, :].rearrange("p (a d) -> p a d", a=TT)
        h2T = GAB_t[:, 0:2048].rearrange("p (k t) -> p k t", k=KC)
        gate2b, normfb = GAB_t[:, 0:1024], GAB_t[:, 1024:2048]
        xe = GAB_t[:, 2048:4096].rearrange("p (b k s) -> p b k s", b=2, k=KC)
        biasraw = GAB_t[0:NE, 2048:4096]
        bias3 = WG[:, :].bitcast(BF16)
        bdown = lmask_t[0:NE, 0:1024]
        combT = modrow[0:NE, 0:T]
        OUTe = PR_t[:, 0:1024]
        t1, sg, hid, u_sb = (PR_t[:, 1024 + 512 * i:1536 + 512 * i] for i in range(4))
        hidT = PR_t[:, 3072:3584].rearrange("p (q s) -> p q s", q=4)
        L2, M8 = QK_t[:, 0:64].rearrange("p (a e) -> p a e", a=2), QK_t[:, 64:80].rearrange("p (a e) -> p a e", a=2)
        IX = QK_t[:, 80:96].bitcast(U32).rearrange("p (a e) -> p a e", a=2)
        IXF, EX = (QK_t[:, o:o + 8].rearrange("p (a e) -> p a e", a=2) for o in (96, 104))
        SM = QK_t[:, 112:114]
        OH = QK_t[:, 128:384].rearrange("p (a k e) -> p a k e", a=2, k=TOPK)
        MSK = QK_t[:, 384:448].rearrange("p (a e) -> p a e", a=2)
        COMB, POS = (QK_t[:, o:o + 68].rearrange("p (a e) -> p a e", a=2) for o in (448, 516))
        CNT = QK_t[:, 584:616]
        P1 = QK_t[:, 656:1168].rearrange("p (b a s) -> p b a s", b=2, a=TT)
        PW = QK_t[:, 1168:1680].rearrange("p (b a s) -> p b a s", b=2, a=TT)
        OVP, OVC = QK_t[:, 1680:1682], QK_t[:, 1682:1684]
        TAKEN, RANK = QK_t[:, 1684:1780], QK_t[:, 1780:1876]
        TURN3 = QK_t[:, 1876:1924].rearrange("p (l t) -> p l t", t=MORE)
        TURN_E, TURN_BASE = QK_t[:, 1924:1940], QK_t[:, 1940:1956]
        TURN_EI, N_TURNS = QK_t[:, 1956:1972].bitcast(I32), QK_t[:, 1972:1973].bitcast(I32)
        LISTING = PR_t[:, 2048:3584].rearrange("p (l t e) -> p l t e", l=MAX_TURNS, t=MORE)
        PWT = VM_t[:, 0:512].rearrange("p (b t) -> p b t", b=2)

        sem = {}
        for n in """consts_ready x_loaded vecs_loaded bada_loaded lora_loaded router_loaded
                    cols_done cols_ready sigc_ready scr_ready ss_ready rms_ready xn_ready xT_done hT_dve hT_act
                    mod_done modrow_ready modcols_done modcols_read
                    unit_free tile_done tile_read lora_shifted lora_act kk_sq norm_ready kkn_read centred decays
                    v_shifted ar_ready bon_ready att_centred att_exp att_ready yb_ready
                    auxa_full auxa_free auxb_full auxb_free
                    x_full x_read bk_full bk_read n_init m_init level_done level_read
                    r_full r_read u_full u_read y_full y_read s_full s_read
                    gn_mean gn_c gn_var gn_std yf_ready
                    bada12_loaded mod12_done mod12_ready scratch_written mod_bcast norm2_loaded
                    z_full z_read mix_done x1_ready ss2_ready rms2_ready h2_ready h2T_full h2T_read
                    logits_full top_ready top_exp chosen_ready comb_ready pos_full combT_full combT_ready bias_loaded bias_ready late_loaded
                    pool_chain dve_chain act_chain
                    gathering_ready weighted_ready pt_full pt_read gather_full gather_read out_read out_read_b combined sel_ready
                    gate_done up_half_done up_done down_done t1_ready sg_ready up_read hid_ready hidT_full hidT_read
                    prologue turns_listed
                    ov_onehot ov_gather ov_copied ov_gate ov_t1 ov_sg ov_up ov_hid ov_hidT ov_hidTc ov_down
                    ov_out ov_comb ov_sel ov_place ov_gathering ov_uread ov_weights
                    y_ready ss3_ready rms3_ready result_ready result_stored""".split():
            sem[n] = ctx.enter_context(nc.semaphore(n))
        unit_full = [ctx.enter_context(nc.semaphore(f"unit_full{i}")) for i in range(4)]
        w_full = [ctx.enter_context(nc.semaphore(f"w_full{i}")) for i in range(4)]

        AUX = ["zw", "za", "g", "kk", "vt", "s0", "s1a", "s1b", "pt0", "pt1", "pt2", "pv", "tok", "bonus"]

        def aux(name):
            n = AUX.index(name)
            full, free = ("auxa_full", "auxa_free") if n % 2 == 0 else ("auxb_full", "auxb_free")
            b = 0 if n % 2 == 0 else 2
            return PS[:, b:b + 2, :].rearrange("p a n -> p (a n)"), sem[full], sem[free], n // 2

        block = ctx.enter_context(nc.Block())

        @block.sync
        def _(sp):
            sp.dma_start(x3[:, :, :], A["x"][0].rearrange("(a p) d -> p a d", p=P)).then_inc(sem["x_loaded"], 16)
            row = 0
            for name, n in VECS:
                src = A[name]
                if name == "c":
                    src = src[0]
                elif name == "rwkv_r_k":
                    src = src.rearrange("h n -> (h n)")
                sp.dma_start(colrows[row:row + n, :], src.rearrange("(a b) -> a b", b=P)).then_inc(sem["vecs_loaded"], 16)
                row += n
            for g in range(4):
                src = A["b_ada"][512 * g:512 * g + 512].rearrange("(a n) -> a n", a=1)
                sp.dma_start(bada0[32 * g:32 * g + 32, :], src.broadcast_to([32, 512])).then_inc(sem["bada_loaded"], 16)

            def load_unit(u):
                if u >= 4:
                    sp.wait_ge(sem["unit_free"], u - 3)
                full = unit_full[u % 4]
                if u < ADA or U_ADA1 <= u < U_BRANCH:
                    c = u if u < ADA else u - U_ADA1 + ADA
                    src = A["w_ada"][:, 512 * c:512 * c + 512].rearrange("(k p) n -> p k n", p=P)
                    dst = unit(u).rearrange("p (k n) -> p k n", k=KC)
                elif u < U_ADA1:
                    _, c0, w = UNITS[u - ADA]
                    src = A["w_in"][:, c0:c0 + w].rearrange("(k p) n -> p k n", p=P)
                    dst = unit(u)[:, 0:KC * w].rearrange("p (k n) -> p k n", k=KC)
                elif u < U_OUT:
                    src = A["w_branch_a" if u == U_BRANCH else "w_branch_b"].rearrange("(k p) n -> p k n", p=P)
                    dst = unit(u).rearrange("p (k n) -> p k n", k=4)
                else:
                    h = u - U_OUT
                    src = A["w_out"][512 * h:512 * h + 512, :].rearrange("(k p) n -> p k n", p=P)
                    dst = unit(u).rearrange("p (k n) -> p k n", k=4)
                sp.dma_start(dst, src).then_inc(full, 16)

            for u in range(ADA):
                load_unit(u)
            sp.dma_start(w2, A["rwkv_w2"]).then_inc(sem["lora_loaded"], 16)
            sp.dma_start(a2, A["rwkv_a2"]).then_inc(sem["lora_loaded"], 16)
            sp.dma_start(g2, A["rwkv_g2"]).then_inc(sem["lora_loaded"], 16)
            sp.dma_start(rw, A["router_w"].rearrange("(k p) e -> p k e", p=P)).then_inc(sem["router_loaded"], 16)
            sp.dma_start(rbias, A["router_b"].rearrange("(a e) -> a e", a=1).broadcast_to([P, NE])).then_inc(sem["router_loaded"], 16)
            for u in range(ADA, N_UNITS):
                load_unit(u)

            WEIGHTS = [A["exp_w_gate"], A["exp_w_up"], A["exp_w_down"]]
            DONE = [sem["gate_done"], sem["up_done"], sem["down_done"]]

            def load_matrix(e, kind, slot):
                sp.dma_start(ring[:, slot, :].rearrange("p (k n) -> p k n", k=KC),
                             WEIGHTS[kind][bass.ds(e, 1), :, :].rearrange("a (k p) n -> p (a k) n", p=P)).then_inc(w_full[slot], 16)

            sp.wait_ge(sem["yf_ready"], 1)
            load_matrix(0, 2, 2)
            load_matrix(1, 0, 3)
            sp.wait_ge(sem["unit_free"], N_UNITS)
            load_matrix(0, 0, 0)
            load_matrix(0, 1, 1)
            with sp.Fori(0, 7) as i:
                for q in range(4, 16):
                    sp.wait_ge(DONE[(q - 4) % 3], 4 * i + (q - 4) // 3 + 1)
                    load_matrix(4 * i + q // 3, q % 3, q % 4)
            for m in range(88, 96):
                sp.wait_ge(DONE[(m - 4) % 3], (m - 4) // 3 + 1)
                load_matrix(m // 3, m % 3, m % 4)

            def load_turn(c, used):
                e = sp.value_load(TURN_EI[0:1, bass.ds(c, 1)], min_val=0, max_val=NE - 1)
                for kind in range(3):
                    s, n = used[kind]
                    sp.wait_ge(s, n)
                    sp.dma_start(ring[:, kind, :].rearrange("p (k n) -> p k n", k=KC),
                                 WEIGHTS[kind][bass.ds(e, 1), :, :].rearrange("a (k p) n -> p (a k) n", p=P)).then_inc(w_full[kind], 16)

            sp.wait_ge(sem["turns_listed"], 1)
            turns = sp.value_load(N_TURNS[0:1, 0:1], min_val=0, max_val=MAX_TURNS)
            with sp.If(turns > 0):
                load_turn(0, ((DONE[2], NE - 1), (DONE[0], NE), (DONE[1], NE)))
                with sp.If(turns > 1):
                    with sp.Fori(1, turns) as c:
                        load_turn(c, ((sem["ov_gate"], c), (sem["ov_up"], c), (sem["ov_down"], c)))

            sp.wait_ge(sem["result_ready"], 1)
            sp.dma_start(out[0, 0:P, :], x3[:, 0, :]).then_inc(sem["result_stored"], 16)
            sp.wait_ge(sem["result_ready"], 2)
            sp.dma_start(out[0, P:T, :], x3[:, 1, :]).then_inc(sem["result_stored"], 16)
            sp.wait_ge(sem["result_stored"], 32)

        @block.gpsimd
        def _(pool):
            n = [0]

            def link(ins):
                n[0] += 1
                ins.then_inc(sem["pool_chain"], 1)
                pool.wait_ge(sem["pool_chain"], n[0])

            link(nc.gpsimd.memset(same, 1.0))
            for i in range(7):
                b = 1 << i
                v = same[:, i, :].rearrange("p (n b) -> p n b", b=b)
                link(nc.gpsimd.affine_select(out=v, in_=v, compare_op=ALU.is_ge, fill=0.0, base=0,
                                             pattern=[[-b, P // b], [0, b]], channel_multiplier=1))
                link(nc.gpsimd.affine_select(out=v, in_=v, compare_op=ALU.is_ge, fill=0.0, base=b - 1,
                                             pattern=[[b, P // b], [0, b]], channel_multiplier=-1))
            link(nc.gpsimd.tensor_copy(ident, same[:, 0, :]))
            link(nc.gpsimd.tensor_copy(blk, same[:, 6, :]))
            link(nc.gpsimd.tensor_copy(ones, same[:, 7, :]))
            for m, base, f, p in ((maskU[:, 0, :], -1, 1, -1), (maskU[:, 1, :], 0, 1, -1), (maskL, -1, -1, 1)):
                link(nc.gpsimd.affine_select(out=m, in_=ones, compare_op=ALU.is_ge, fill=0.0, base=base,
                                             pattern=[[f, P]], channel_multiplier=p))
            link(nc.gpsimd.memset(negmask, 0.0))
            link(nc.gpsimd.affine_select(out=negmask, in_=negmask, compare_op=ALU.is_ge, fill=NEG, base=0,
                                         pattern=[[-1, P]], channel_multiplier=1))
            link(nc.gpsimd.tensor_tensor(lmask, same[:, 1:8, :], same[:, 0:7, :], ALU.subtract))
            link(nc.gpsimd.tensor_tensor(lmask0L, lmask[:, 0, :], maskL, ALU.mult))
            link(nc.gpsimd.tensor_tensor(lmask, lmask, maskU[:, 0:1, :].broadcast_to([P, 7, P]), ALU.mult))
            link(nc.gpsimd.iota(iota64, pattern=[[1, 64]], base=0, channel_multiplier=0,
                                allow_small_or_imprecise_dtypes=True))
            nc.gpsimd.iota(iota32, pattern=[[1, 32]], base=0, channel_multiplier=0,
                           allow_small_or_imprecise_dtypes=True).then_inc(sem["consts_ready"], 1)

            for c in range(TT):
                pool.wait_ge(sem["bk_read"], HP * (c + 1))
                if c:
                    pool.wait_ge(sem["u_full"], 1)
                link(nc.gpsimd.tensor_tensor(Nm, BK[:, :, 0, 0, :], lmask[:, 0:1, :].broadcast_to([P, RH, P]), ALU.mult))
                nc.gpsimd.tensor_tensor(Nm, Nm, ident.unsqueeze(1).broadcast_to([P, RH, P]), ALU.add).then_inc(sem["n_init"], 1)

            pool.wait_ge(sem["tile_done"], len(TILES))
            for g in range(8):
                src = A["b_ada"][2048 + 512 * g:2560 + 512 * g].rearrange("(a n) -> a n", a=1)
                pool.dma_start(bada12[32 * (g % 4):32 * (g % 4) + 32, g // 4, :],
                               src.broadcast_to([32, 512])).then_inc(sem["bada12_loaded"], 16)
            pool.wait_ge(sem["mod12_ready"], 2)
            for r in range(2):
                pool.dma_start(scratch[4 * r:4 * r + 4, :], modrow12[0:P:32, r, :]).then_inc(sem["scratch_written"], 16)
            pool.wait_ge(sem["scratch_written"], 32)
            pool.wait_ge(sem["s_full"], 1)
            pool.wait_ge(sem["auxb_full"], AUX.index("pv") // 2 + 1)
            for dst, r in ((gate1b, 0), (shift2b, 2), (scale2b, 4)):
                src = scratch[r:r + 2, :].rearrange("(o a) n -> o (a n)", o=1)
                pool.dma_start(dst, src.broadcast_to([P, D])).then_inc(sem["mod_bcast"], 16)
            pool.wait_ge(sem["yf_ready"], 1)
            pool.dma_start(norm2b, A["norm2_g"].rearrange("(a n) -> a n", a=1).broadcast_to([P, D])).then_inc(sem["norm2_loaded"], 16)
            pool.wait_ge(sem["z_read"], KC)
            pool.dma_start(biasraw[:, 0:D], A["exp_b_gate"]).then_inc(sem["bias_loaded"], 16)
            pool.dma_start(biasraw[:, D:2 * D], A["exp_b_up"]).then_inc(sem["bias_loaded"], 16)
            pool.dma_start(bdown, A["exp_b_down"]).then_inc(sem["bias_loaded"], 16)
            pool.wait_ge(sem["logits_full"], 1)
            pool.dma_start(gate2b, scratch[6:8, :].rearrange("(o a) n -> o (a n)", o=1).broadcast_to([P, D])).then_inc(sem["late_loaded"], 16)
            pool.dma_start(normfb, A["normf_g"].rearrange("(a n) -> a n", a=1).broadcast_to([P, D])).then_inc(sem["late_loaded"], 16)

            pool.wait_ge(sem["bias_ready"], 1)
            with pool.Fori(0, PAIRS) as p:
                for k in range(2):
                    e = 2 * p + k
                    if k == 0:
                        pool.wait_ge(sem["gather_full"], p + 1)
                    nc.gpsimd.tensor_copy(selb[0:96, k, :], eye3[0:96, bass.ds(e, 1)].broadcast_to([96, SLOTS])).then_inc(sem["sel_ready"], 1)

            def select_expert(c):
                e = pool.value_load(TURN_EI[0:1, bass.ds(c, 1)], min_val=0, max_val=NE - 1)
                nc.gpsimd.tensor_copy(selb[0:96, 0, :], eye3[0:96, bass.ds(e, 1)].broadcast_to([96, SLOTS])).then_inc(sem["ov_sel"], 1)

            pool.wait_ge(sem["turns_listed"], 1)
            turns = pool.value_load(N_TURNS[0:1, 0:1], min_val=0, max_val=MAX_TURNS)
            with pool.If(turns > 0):
                pool.wait_ge(sem["up_done"], NE)
                select_expert(0)
                with pool.If(turns > 1):
                    with pool.Fori(1, turns) as c:
                        pool.wait_ge(sem["ov_up"], c)
                        select_expert(c)

        @block.scalar
        def _(act):
            n = [0]

            def link(ins):
                n[0] += 1
                ins.then_inc(sem["act_chain"], 1)
                act.wait_ge(sem["act_chain"], n[0])

            act.wait_ge(sem["ss_ready"], 1)
            nc.scalar.activation(rstd, ss, ACT.Sqrt).then_inc(sem["rms_ready"], 1)
            act.wait_ge(sem["cols_ready"], 1)
            nc.scalar.activation(sigc, col("c", 0, 8), ACT.Sigmoid).then_inc(sem["sigc_ready"], 1)

            act.wait_ge(sem["modcols_read"], 1)
            for k in range(4, KC):
                act.wait_ge(sem["xT_done"], k // 2 + 1)
                nc.scalar.activation(hT[:, k, :], PS[:, 2 + k // 2, (k % 2) * T:(k % 2) * T + T], ACT.Identity,
                                     bias=sh1c[:, k:k + 1], scale=s1c[:, k:k + 1]).then_inc(sem["hT_act"], 1)

            def read_tiles(a, b):
                for i in range(a, b):
                    kind, u, c0, j = TILES[i]
                    act.wait_ge(sem["tile_done"], i + 1)
                    src = PS[:, 4 + i % 4, 0:T]
                    if kind in ("r", "k", "v", "lora"):
                        dst, f = PR[:, j, 1:257], ACT.Copy
                    elif kind in ("q", "km"):
                        dst, f = QK[:, j, :], ACT.Copy
                    elif kind == "vm":
                        src, dst, f = PS[:, 4 + i % 4, :], VM[:, j, :], ACT.Copy
                    else:
                        dst, f = GAB[:, j, :], ACT.Sigmoid
                    nc.scalar.activation(dst, src, f).then_inc(sem["tile_read"], 1)

            def read_aux(name, dst, f=ACT.Copy, biases=None, **kw):
                ps, full, free, uses = aux(name)
                act.wait_ge(full, uses + 1)
                if biases is None:
                    last = nc.scalar.activation(dst, ps, f, **kw)
                else:
                    for q in range(HP):
                        last = nc.scalar.activation(dst[:, T * q:T * q + T], ps[:, T * q:T * q + T], f, bias=biases(q))
                last.then_inc(free, 1)

            read_tiles(0, 6)
            act.wait_ge(sem["lora_shifted"], 1)
            nc.scalar.activation(PR[0:64, 12, 1:257], PR[0:64, 12, 1:257], ACT.Tanh)
            nc.scalar.activation(PR[:, 13, 1:257], PR[:, 13, 1:257], ACT.Sigmoid).then_inc(sem["lora_act"], 1)
            read_tiles(6, 14)
            read_aux("zw", SIGf, ACT.Sigmoid, lambda q: col("rwkv_w0", q))
            read_aux("za", Af, ACT.Sigmoid, lambda q: col("rwkv_a0", q))
            read_tiles(14, 18)
            read_aux("g", Gf)
            ps, full, free, uses = aux("kk")
            act.wait_ge(full, uses + 1)
            nc.scalar.activation(NRMf, ps, ACT.Sqrt).then_inc(free, 1)
            read_tiles(18, 22)
            read_aux("vt", VTf)
            read_tiles(22, 24)
            act.wait_ge(sem["centred"], 1)
            nc.scalar.activation(E1f, Ccf, ACT.Exp, scale=-LAM)
            nc.scalar.activation(NRMf, DIFf, ACT.Exp, scale=-LAM)
            nc.scalar.activation(decay_end, dsum, ACT.Exp, scale=-LAM)
            nc.scalar.activation(E2f, Ccf, ACT.Exp, scale=LAM).then_inc(sem["decays"], 1)
            read_tiles(24, 26)
            act.wait_ge(sem["att_centred"], 1)
            nc.scalar.activation(att, att, ACT.Exp, scale=SCALE).then_inc(sem["att_exp"], 1)
            read_tiles(26, 28)
            for b in range(3):
                read_aux(f"pt{b}", PT[:, b].rearrange("p h t -> p (h t)"))
            read_tiles(28, 30)
            read_aux("pv", QK_t[:, 0:1024])
            read_aux("tok", WG[:, :])
            at = 30
            for c in range(TT):
                act.wait_ge(sem["r_full"], c + 1)
                nc.scalar.activation(Rs.rearrange("p (i n) -> p i n", i=2), PS[:, 0:2, 0:T], ACT.Copy).then_inc(sem["r_read"], 1)
                to = min(at + 6, len(TILES))
                read_tiles(at, to)
                at = to
                act.wait_ge(sem["u_full"], c + 1)
                nc.scalar.activation(Us, PS[:, 0, :], ACT.Copy).then_inc(sem["u_read"], 1)
                act.wait_ge(sem["y_full"], c + 1)
                nc.scalar.activation(YTf.rearrange("p (q t) -> p q t", q=HP)[:, :, P * c:P * c + P],
                                     PS[:, 2, :].rearrange("p (q t) -> p q t", q=HP), ACT.Copy).then_inc(sem["y_read"], 1)
            act.wait_ge(sem["gn_var"], 1)
            nc.scalar.activation(SIGf, PS[:, 2:4, :].rearrange("p a n -> p (a n)"), ACT.Sqrt, bias=eps_gn, scale=1.0 / HD).then_inc(sem["gn_std"], 1)

            act.wait_ge(sem["ss2_ready"], 1)
            nc.scalar.activation(rstd2, ss2, ACT.Sqrt).then_inc(sem["rms2_ready"], 1)
            for b in range(4):
                act.wait_ge(sem["h2T_full"], b + 1)
                nc.scalar.activation(h2T[:, 2 * b:2 * b + 2, :].rearrange("p k t -> p (k t)"), PS[:, b, :], ACT.Copy).then_inc(sem["h2T_read"], 1)
            act.wait_ge(sem["top_ready"], 1)
            nc.scalar.activation(EX, EX, ACT.Exp).then_inc(sem["top_exp"], 1)
            act.wait_ge(sem["combT_full"], 1)
            nc.scalar.activation(combT, PS[0:NE, 2, 0:T], ACT.Copy).then_inc(sem["combT_ready"], 1)

            act.sem_inc(sem["hidT_read"], 1)
            act.sem_inc(sem["out_read"], 1)
            with act.Fori(0, PAIRS // 2) as i:
                for pp in range(2):
                    p = 2 * i + pp
                    act.wait_ge(sem["pt_full"], p + 1)
                    nc.scalar.activation(PWT[:, pp, :], PS[:, 0, 0:T], ACT.Copy).then_inc(sem["pt_read"], 1)
                    act.wait_ge(sem["gather_full"], p + 1)
                    nc.scalar.activation(xe[:, pp].rearrange("p k s -> p (k s)"), PS[:, 1:3, :].rearrange("p a n -> p (a n)"), ACT.Copy).then_inc(sem["gather_read"], 1)
                    for k in range(2):
                        e = 2 * p + k
                        act.wait_ge(sem["t1_ready"], e + 1)
                        nc.scalar.activation(sg, t1, ACT.Sigmoid, scale=ALPHA).then_inc(sem["sg_ready"], 1)
                        for h in range(2):
                            act.wait_ge(sem["hidT_full"], 2 * e + h + 1)
                            nc.scalar.activation(hidT[:, 2 * h:2 * h + 2, :].rearrange("p q s -> p (q s)"),
                                                 PS[:, 0, T * h:T * h + T], ACT.Copy).then_inc(sem["hidT_read"], 1)
                        act.wait_ge(sem["down_done"], e + 1)
                        nc.scalar.activation(OUTe[64 * k:64 * k + 64, 0:512], PS[0:64, 3, :], ACT.Copy).then_inc(sem["out_read"], 1)
            act.wait_ge(sem["turns_listed"], 1)
            turns = act.value_load(N_TURNS[0:1, 0:1], min_val=0, max_val=MAX_TURNS)
            with act.If(turns > 0):
                with act.Fori(0, turns) as c:
                    act.wait_ge(sem["ov_gather"], c + 1)
                    nc.scalar.activation(PWT[:, 0, :], PS[:, 0, 0:T], ACT.Copy)
                    nc.scalar.activation(xe[:, 0].rearrange("p k s -> p (k s)"), PS[:, 1:3, :].rearrange("p a n -> p (a n)"), ACT.Copy).then_inc(sem["ov_copied"], 1)
                    act.wait_ge(sem["ov_t1"], c + 1)
                    nc.scalar.activation(sg, t1, ACT.Sigmoid, scale=ALPHA).then_inc(sem["ov_sg"], 1)
                    act.wait_ge(sem["ov_hidT"], c + 1)
                    nc.scalar.activation(hidT.rearrange("p q s -> p (q s)"), PS[:, 0, :], ACT.Copy).then_inc(sem["ov_hidTc"], 1)
            act.wait_ge(sem["ss3_ready"], 1)
            nc.scalar.activation(rstd3, ss3, ACT.Sqrt).then_inc(sem["rms3_ready"], 1)

        @block.vector
        def _(dve):
            n = [0]
            V = nc.vector

            def link(ins):
                n[0] += 1
                ins.then_inc(sem["dve_chain"], 1)
                dve.wait_ge(sem["dve_chain"], n[0])

            b4 = lambda name: over(col(name, 0, 4), T)
            r4, k4, v4 = PR[:, 0:4, 1:257], PR[:, 4:8, 1:257], PR[:, 8:12, 1:257]

            V.memset(PR[:, :, 0:1], 0.0)
            V.memset(eps_gn, GN_EPS)

            dve.wait_ge(sem["x_loaded"], 16)
            for a in range(TT):
                link(V.tensor_tensor_reduce(out=xn[:, a, :], in0=x3[:, a, :], in1=x3[:, a, :], scale=1.0, scalar=0.0,
                                            op0=ALU.mult, op1=ALU.add, accum_out=ss[:, a:a + 1]))
            V.tensor_scalar(ss, ss, 1.0 / D, RMS_EPS, ALU.mult, ALU.add).then_inc(sem["ss_ready"], 1)
            dve.wait_ge(sem["rms_ready"], 1)
            link(V.reciprocal(rstd, rstd))
            for a in range(TT):
                V.tensor_scalar(xn[:, a, :], x3[:, a, :], rstd[:, a:a + 1], None, ALU.mult).then_inc(sem["xn_ready"], 1)
            dve.wait_ge(sem["cols_done"], 1)
            V.tensor_copy(cols[:, 0:NVEC], PS[:, 0, 0:NVEC]).then_inc(sem["cols_ready"], 1)
            dve.wait_ge(sem["cols_ready"], 1)
            dve.wait_ge(sem["sigc_ready"], 1)
            V.tensor_tensor(scr, over(col("c", 0, 8), 32), over(sigc, 32), ALU.mult).then_inc(sem["scr_ready"], 1)
            dve.wait_ge(sem["mod_done"], 1)
            dve.wait_ge(sem["bada_loaded"], 64)
            V.tensor_tensor(modrow[:, :], PS[:, 1, :], bada0, ALU.add).then_inc(sem["modrow_ready"], 1)
            dve.wait_ge(sem["modcols_done"], 1)
            for g in range(2):
                V.tensor_copy(sh1c[:, 4 * g:4 * g + 4], PS[:, COL_BANK[g], 64:68])
                last = V.scalar_tensor_tensor(out=s1c[:, 4 * g:4 * g + 4], in0=PS[:, COL_BANK[2 + g], 64:68], scalar=1.0,
                                              in1=col("norm1_g", 4 * g, 4), op0=ALU.add, op1=ALU.mult)
            last.then_inc(sem["modcols_read"], 1)
            dve.wait_ge(sem["modcols_read"], 1)
            for k in range(4):
                dve.wait_ge(sem["xT_done"], k // 2 + 1)
                V.tensor_scalar(hT[:, k, :], PS[:, 2 + k // 2, (k % 2) * T:(k % 2) * T + T], s1c[:, k:k + 1],
                                sh1c[:, k:k + 1], ALU.mult, ALU.add).then_inc(sem["hT_dve"], 1)

            def shift(j0, nj, signal=None):
                dif = DIFf[:, 0:T * nj].rearrange("p (j t) -> p j t", j=nj)
                link(V.tensor_tensor(dif, PR[:, j0:j0 + nj, 0:T], PR[:, j0:j0 + nj, 1:257], ALU.subtract))
                for j in range(nj):
                    ins = V.scalar_tensor_tensor(out=PR[:, j0 + j, 1:257], in0=dif[:, j, :], scalar=col("rwkv_mu", j0 + j),
                                                 in1=PR[:, j0 + j, 1:257], op0=ALU.mult, op1=ALU.add)
                if signal:
                    ins.then_inc(sem[signal], 1)
                else:
                    link(ins)

            dve.wait_ge(sem["tile_read"], 2)
            shift(12, 2, "lora_shifted")
            dve.wait_ge(sem["lora_shifted"], 1)
            dve.wait_ge(sem["tile_read"], 6)
            shift(4, 4)
            link(V.tensor_tensor(pairs(KKf), k4, b4("rwkv_k_k"), ALU.mult))
            V.tensor_tensor(SQf, KKf, KKf, ALU.mult).then_inc(sem["kk_sq"], 1)
            dve.wait_ge(sem["tile_read"], 10)
            shift(0, 4)
            dve.wait_ge(sem["tile_read"], 14)
            shift(8, 4, "v_shifted")
            dve.wait_ge(sem["v_shifted"], 1)
            dve.wait_ge(sem["auxb_free"], 1)
            link(V.scalar_tensor_tensor(out=pairs(DIFf), in0=pairs(Af), scalar=-1.0, in1=b4("rwkv_k_a"), op0=ALU.add, op1=ALU.mult))
            link(V.scalar_tensor_tensor(out=k4, in0=pairs(DIFf), scalar=1.0, in1=k4, op0=ALU.add, op1=ALU.mult))
            dve.wait_ge(sem["auxa_free"], 1)
            for q in range(2 * HP):
                last = V.tensor_tensor_scan(Cf[:, P * q:P * q + P], ones, SIGf[:, P * q:P * q + P], 0.0, ALU.mult, ALU.add)
            link(last)
            C8 = Cf.rearrange("p (j t) -> p j t", t=P)
            link(V.tensor_tensor(Ccf.rearrange("p (j t) -> p j t", t=P), C8,
                                 C8[:, :, MID:MID + 1].broadcast_to([P, 2 * HP, P]), ALU.subtract))
            C4 = Ccf.rearrange("p (q c t) -> p q c t", q=HP, c=TT)
            R4 = Cf.rearrange("p (q c t) -> p q c t", q=HP, c=TT)
            V.tensor_tensor(dsum.unsqueeze(2), C4[:, :, 0, P - 1:P], R4[:, :, 1, MID:MID + 1], ALU.add)
            link(V.tensor_tensor(DIFf, Ccf, SIGf, ALU.subtract))
            dve.wait_ge(sem["auxb_free"], 2)
            link(V.tensor_scalar(NRMf, NRMf, 1e-12, None, ALU.max))
            link(V.reciprocal(NRMf, NRMf))
            link(V.tensor_tensor(KKf, KKf, NRMf, ALU.mult))
            V.tensor_tensor(Bf, KKf, Af, ALU.mult).then_inc(sem["centred"], 1)
            dve.wait_ge(sem["centred"], 1)
            dve.wait_ge(sem["decays"], 1)
            c4 = lambda a: a.rearrange("p (q c t) -> p q c t", q=HP, c=TT)
            for c in range(TT):
                V.tensor_tensor(AR[:, :, c, 1, :], PR[:, 0:4, 1 + P * c:1 + P * c + P], c4(E1f)[:, :, c, :], ALU.mult)
                V.scalar_tensor_tensor(out=AR[:, :, c, 0, :], in0=c4(KKf)[:, :, c, :], scalar=-1.0, in1=c4(NRMf)[:, :, c, :],
                                       op0=ALU.mult, op1=ALU.mult)
            V.tensor_tensor(pairs(K2f), k4, pairs(E2f), ALU.mult)
            V.tensor_tensor(Bf, Bf, E2f, ALU.mult).then_inc(sem["ar_ready"], 1)
            dve.wait_ge(sem["ar_ready"], 1)
            link(V.tensor_tensor(r4, r4, k4, ALU.mult))
            V.tensor_tensor(r4, r4, b4("rwkv_r_k"), ALU.mult).then_inc(sem["bon_ready"], 1)

            ps, full, free, uses = aux("s0")
            dve.wait_ge(full, uses + 1)
            V.tensor_tensor(att[:, :, 0:P], heads(ps), negmask.unsqueeze(1).broadcast_to([P, RH, P]), ALU.add).then_inc(free, 1)
            for name, h0 in (("s1a", 0), ("s1b", 4)):
                ps, full, free, uses = aux(name)
                s = ps.rearrange("p (i q t) -> p i q t", i=2, q=2)
                dst = att.rearrange("p (i q) t -> p i q t", i=2)[:, :, h0 // 2:h0 // 2 + 2, :]
                dve.wait_ge(full, uses + 1)
                V.tensor_copy(dst[:, :, :, P:2 * P], s[:, :, :, 0:P])
                for i in range(2):
                    last = V.tensor_tensor(dst[:, i, :, 2 * P:3 * P], s[:, i, :, P:T], negmask.unsqueeze(1).broadcast_to([P, 2, P]), ALU.add)
                last.then_inc(free, 1)
            dve.wait_ge(sem["auxb_free"], 4)
            dve.wait_ge(sem["auxa_free"], 4)
            parts = ((att[:, :, 0:P], 0, P), (att[:, :, P:3 * P], RH, 2 * P))
            for a, m, w in parts:
                last = V.tensor_reduce(mx[:, m:m + RH], a, AX_X, ALU.max)
            link(last)
            for a, m, w in parts:
                last = V.tensor_tensor(a, a, over(mx[:, m:m + RH], w), ALU.subtract)
            last.then_inc(sem["att_centred"], 1)
            dve.wait_ge(sem["att_exp"], 1)
            for a, m, w in parts:
                last = V.tensor_reduce(sums[:, m:m + RH], a, AX_X, ALU.add)
            link(last)
            link(V.reciprocal(sums, sums))
            for a, m, w in parts:
                last = V.tensor_tensor(a, a, over(sums[:, m:m + RH], w), ALU.mult)
            last.then_inc(sem["att_ready"], 1)

            ps, full, free, uses = aux("bonus")
            dve.wait_ge(full, uses + 1)
            V.tensor_tensor(BON, pairs(ps), v4, ALU.mult).then_inc(free, 1)

            steps = 0
            for c in range(TT):
                for q in range(HP):
                    u = HP * c + q
                    dve.wait_ge(sem["bk_full"], u + 1)
                    V.tensor_tensor(BK[:, 2 * q:2 * q + 2].rearrange("p h j a t -> p (h j) (a t)"),
                                    PS[:, 0:2, :].rearrange("p h (j t) -> p (h j) t", j=2),
                                    maskU_t[:, :].unsqueeze(1).broadcast_to([P, 4, T]), ALU.mult).then_inc(sem["bk_read"], 1)
                    dve.wait_ge(sem["x_full"], u + 1)
                    V.tensor_tensor(XS[:, 2 * q:2 * q + 2, :], PS[:, 2:4, 0:P],
                                    maskL.unsqueeze(1).broadcast_to([P, 2, P]), ALU.mult).then_inc(sem["x_read"], 1)
                dve.wait_ge(sem["x_read"], HP * (c + 1))
                link(V.tensor_tensor(Mm, XS, lmask0L.unsqueeze(1).broadcast_to([P, RH, P]), ALU.mult))
                V.tensor_tensor(Mm, Mm, ident.unsqueeze(1).broadcast_to([P, RH, P]), ALU.add).then_inc(sem["m_init"], 1)
                dve.wait_ge(sem["n_init"], c + 1)
                for k in range(1, 7):
                    seq = [("T", 0), ("T", 1)] + [(w, g) for g in range(2) for w in ("MN" if k < 6 else "N")]
                    for what, g in seq:
                        assert steps == level_index(c, k, what, g)
                        dve.wait_ge(sem["level_done"], steps + 1 + (what == "M"))
                        hs = slice(4 * g, 4 * g + 4)
                        ps = PS[:, 2 * g + (what == "N"), :].rearrange("p (h t) -> p h t", h=4)
                        if what == "T":
                            ins = V.tensor_tensor(TL[:, hs, :], ps, lmask[:, k:k + 1, :].broadcast_to([P, 4, P]), ALU.mult)
                        else:
                            m = Mm if what == "M" else Nm
                            ins = V.tensor_tensor(m[:, hs, :], m[:, hs, :], ps, ALU.add)
                        ins.then_inc(sem["level_read"], 1)
                        steps += 1
                if c == 0:
                    dve.wait_ge(sem["s_full"], 1)
                    V.tensor_tensor(S1, PS[:, 3, 0:T].rearrange("p (q d) -> p q d", q=HP), over(decay_end, HD), ALU.mult).then_inc(sem["s_read"], 1)

            for r in range(2):
                dve.wait_ge(sem["mod12_done"], r + 1)
                dve.wait_ge(sem["bada12_loaded"], 128)
                V.tensor_tensor(modrow12[:, r, :], PS[:, 4 + r, :], bada12[:, r, :], ALU.add).then_inc(sem["mod12_ready"], 1)

            dve.wait_ge(sem["gn_mean"], 1)
            YC, SQ2 = KKf, Bf
            link(V.scalar_tensor_tensor(out=YC, in0=PS[:, 0:2, :].rearrange("p a n -> p (a n)"), scalar=-1.0 / HD, in1=YTf,
                                        op0=ALU.mult, op1=ALU.add))
            V.tensor_tensor(SQ2, YC, YC, ALU.mult).then_inc(sem["gn_c"], 1)
            dve.wait_ge(sem["gn_std"], 1)
            link(V.reciprocal(SIGf, SIGf))
            link(V.tensor_tensor(YC, YC, SIGf, ALU.mult))
            link(V.tensor_tensor(pairs(YC), pairs(YC), b4("rwkv_ln_w"), ALU.mult))
            link(V.tensor_tensor(pairs(YC), pairs(YC), b4("rwkv_ln_b"), ALU.add))
            link(V.tensor_tensor(pairs(YC), pairs(YC), BON, ALU.add))
            V.tensor_tensor(YF, pairs(YC), pairs(Gf), ALU.mult).then_inc(sem["yf_ready"], 1)

            dve.wait_ge(sem["scratch_written"], 32)
            za, zb = PR_t[:, 1028:1284], PR_t[:, 1284:1540]
            dve.wait_ge(sem["yf_ready"], 1)
            for m in range(KC):
                dve.wait_ge(sem["z_full"], m + 1)
                V.tensor_tensor(za, PS[:, m % 4, 0:T], GAB[:, m, :], ALU.mult)
                link(V.tensor_tensor(zb, PS[:, m % 4, T:2 * T], GAB[:, 8 + m, :], ALU.mult))
                V.tensor_tensor(zT[:, m, :], za, zb, ALU.add).then_inc(sem["z_read"], 1)
                dve.wait_ge(sem["z_read"], m + 1)

            dve.wait_ge(sem["mod_bcast"], 48)
            dve.wait_ge(sem["norm2_loaded"], 16)
            link(V.scalar_tensor_tensor(out=scale2b, in0=scale2b, scalar=1.0, in1=norm2b, op0=ALU.add, op1=ALU.mult))
            mixed = PR_t[:, 0:2048].rearrange("p (a d) -> p a d", a=TT)
            dve.wait_ge(sem["mix_done"], 1)
            for a in range(TT):
                for h in range(2):
                    s = slice(512 * h, 512 * h + 512)
                    last = V.tensor_tensor(mixed[:, a, s], PS[:, 4 + 2 * a + h, :], gate1b[:, s], ALU.mult)
            link(last)
            link(V.tensor_tensor(x_sb[:, :], x_sb[:, :], PR_t[:, 0:2048], ALU.add))
            for a in range(TT):
                link(V.tensor_tensor_reduce(out=h2[:, a, :], in0=x3[:, a, :], in1=x3[:, a, :], scale=1.0, scalar=0.0,
                                            op0=ALU.mult, op1=ALU.add, accum_out=ss2[:, a:a + 1]))
            V.tensor_scalar(ss2, ss2, 1.0 / D, RMS_EPS, ALU.mult, ALU.add).then_inc(sem["ss2_ready"], 1)
            dve.wait_ge(sem["rms2_ready"], 1)
            link(V.reciprocal(rstd2, rstd2))
            for a in range(TT):
                link(V.scalar_tensor_tensor(out=h2[:, a, :], in0=x3[:, a, :], scalar=rstd2[:, a:a + 1], in1=scale2b,
                                            op0=ALU.mult, op1=ALU.mult))
                V.tensor_tensor(h2[:, a, :], h2[:, a, :], shift2b, ALU.add).then_inc(sem["h2_ready"], 1)

            for j in range(3):
                V.tensor_copy(eye3[32 * j:32 * j + 32, :], ident[0:32, 0:32])
            dve.wait_ge(sem["bias_loaded"], 48)
            dve.wait_ge(sem["h2_ready"], 2)
            for j in range(3):
                ins = V.tensor_copy(bias3[32 * j:32 * j + 32, :], biasraw)
                if j < 2:
                    link(ins)
                    link(V.tensor_tensor(biasraw, biasraw, bias3[32 * j:32 * j + 32, :], ALU.subtract))
            ins.then_inc(sem["bias_ready"], 1)

            dve.wait_ge(sem["logits_full"], 1)
            dve.wait_ge(sem["router_loaded"], 32)
            link(V.tensor_tensor(L2, PS[:, 0, 0:64].rearrange("p (a e) -> p a e", a=2), rbias.unsqueeze(1).broadcast_to([P, 2, NE]), ALU.add))
            for a in range(TT):
                link(V.max(M8[:, a, :], L2[:, a, :]))
                link(V.max_index(IX[:, a, :], M8[:, a, :], L2[:, a, :]))
            V.tensor_copy(IXF, IX[:, :, 0:TOPK])
            V.memset(COMB, 0.0)
            V.tensor_tensor(EX, M8[:, :, 0:TOPK], M8[:, :, 0:1].broadcast_to([P, 2, TOPK]), ALU.subtract).then_inc(sem["top_ready"], 1)
            dve.wait_ge(sem["top_ready"], 1)
            for a in range(TT):
                last = V.tensor_tensor(OH[:, a], iota32.unsqueeze(1).broadcast_to([P, TOPK, NE]), over(IXF[:, a, :], NE), ALU.is_equal)
            link(last)
            V.tensor_reduce(MSK, OH.rearrange("p a k e -> p a e k"), AX_X, ALU.add).then_inc(sem["chosen_ready"], 1)
            dve.wait_ge(sem["top_exp"], 1)
            link(V.tensor_reduce(SM, EX, AX_X, ALU.add))
            link(V.reciprocal(SM, SM))
            link(V.tensor_tensor(EX, EX, over(SM, TOPK), ALU.mult))
            for a in range(TT):
                last = V.tensor_tensor(OH[:, a], OH[:, a], over(EX[:, a, :], NE), ALU.mult)
            link(last)
            V.tensor_reduce(COMB[:, :, 0:NE], OH.rearrange("p a k e -> p a e k"), AX_X, ALU.add).then_inc(sem["comb_ready"], 1)
            dve.wait_ge(sem["pos_full"], 1)
            link(V.memset(POS, 0.0))
            link(V.scalar_tensor_tensor(out=POS[:, :, 0:NE], in0=PS[:, 1, 0:64].rearrange("p (a e) -> p a e", a=2), scalar=1.0,
                                        in1=MSK, op0=ALU.add, op1=ALU.mult))
            link(V.tensor_scalar(POS, POS, -1.0, None, ALU.add))
            V.tensor_copy(CNT, PS[:, 1, 64:96])
            V.memset(PWT[:, 1, :], 0.0)
            V.memset(OUTe, 0.0).then_inc(sem["prologue"], 1)

            def one_hot(b, p):
                pos = POS[:, :, bass.ds(2 * p, 2)].unsqueeze(3).broadcast_to([P, TT, 2, SLOTS])
                comb = COMB[:, :, bass.ds(2 * p, 2)].unsqueeze(3).broadcast_to([P, TT, 2, SLOTS])
                gathering = P1[:, b].rearrange("p a (k s) -> p a k s", k=2)
                weighted = PW[:, b].rearrange("p a (k s) -> p a k s", k=2)
                for a in range(TT):
                    last = V.tensor_tensor(gathering[:, a], iota64.unsqueeze(1).broadcast_to([P, 2, SLOTS]), pos[:, a], ALU.is_equal)
                last.then_inc(sem["gathering_ready"], 1)
                dve.wait_ge(sem["gathering_ready"], p + 1)
                for a in range(TT):
                    last = V.tensor_tensor(weighted[:, a], gathering[:, a], comb[:, a], ALU.mult)
                last.then_inc(sem["weighted_ready"], 1)

            one_hot(0, 0)

            for t in range(MORE):
                last = V.tensor_scalar(TAKEN[:, NE * t:NE * t + NE], CNT, float(SLOTS * (t + 1)), None, ALU.is_gt)
            link(last)
            link(V.tensor_tensor_scan(RANK, ones[:, 0:MORE * NE], TAKEN, 0.0, ALU.mult, ALU.add))
            V.tensor_copy(N_TURNS, RANK[:, MORE * NE - 1:MORE * NE])
            link(V.tensor_tensor(TAKEN, TAKEN, RANK, ALU.mult))
            link(V.tensor_scalar(TAKEN, TAKEN, -1.0, None, ALU.add))
            flat = LISTING.rearrange("p l t e -> p l (t e)")
            link(V.tensor_tensor(flat, over(iota64[:, 0:MAX_TURNS], MORE * NE), TAKEN.unsqueeze(1).broadcast_to([P, MAX_TURNS, MORE * NE]), ALU.is_equal))
            link(V.tensor_reduce(TURN3, LISTING, AX_X, ALU.add))
            link(V.scalar_tensor_tensor(out=TURN_BASE, in0=TURN3[:, :, 1], scalar=2.0, in1=TURN3[:, :, 0], op0=ALU.mult, op1=ALU.add))
            link(V.scalar_tensor_tensor(out=TURN_BASE, in0=TURN3[:, :, 2], scalar=3.0, in1=TURN_BASE, op0=ALU.mult, op1=ALU.add))
            link(V.tensor_scalar(TURN_BASE, TURN_BASE, float(SLOTS), None, ALU.mult))
            for t in range(MORE):
                last = V.tensor_tensor(LISTING[:, :, t, :], LISTING[:, :, t, :], iota32.unsqueeze(1).broadcast_to([P, MAX_TURNS, NE]), ALU.mult)
            link(last)
            link(V.tensor_reduce(TURN_E, flat, AX_X, ALU.add))
            V.tensor_copy(TURN_EI, TURN_E).then_inc(sem["turns_listed"], 1)

            dve.sem_inc(sem["up_read"], 1)
            dve.sem_inc(sem["out_read_b"], 1)
            with dve.Fori(0, PAIRS // 2) as i:
                for pp in range(2):
                    p = 2 * i + pp
                    for k in range(2):
                        e = 2 * p + k
                        dve.wait_ge(sem["gate_done"], e + 1)
                        V.tensor_scalar(t1, PS[:, 0, :], LIMIT, None, ALU.min).then_inc(sem["t1_ready"], 1)
                        dve.wait_ge(sem["sg_ready"], e + 1)
                        V.tensor_tensor(t1, t1, sg, ALU.mult)
                        for h in range(2):
                            s = slice(T * h, T * h + T)
                            dve.wait_ge(sem["up_done" if h else "up_half_done"], e + 1)
                            V.tensor_scalar(u_sb[:, s], PS[:, 1 + h, 0:T], LIMIT, -LIMIT, ALU.min, ALU.max).then_inc(sem["up_read"], 1)
                            dve.wait_ge(sem["up_read"], 2 * e + h + 2)
                            V.scalar_tensor_tensor(out=hid[:, s], in0=u_sb[:, s], scalar=1.0, in1=t1[:, s],
                                                   op0=ALU.add, op1=ALU.mult).then_inc(sem["hid_ready"], 1)
                        if k == 1:
                            one_hot(1 - pp, p + 1)
                        dve.wait_ge(sem["down_done"], e + 1)
                        V.tensor_copy(OUTe[64 * k:64 * k + 64, 512:1024], PS[64:128, 3, :]).then_inc(sem["out_read_b"], 1)

            turns = dve.value_load(N_TURNS[0:1, 0:1], min_val=0, max_val=MAX_TURNS)
            with dve.If(turns > 0):
                dve.wait_ge(sem["weighted_ready"], PAIRS + 1)
                V.memset(P1[:, 0], 0.0)
                V.memset(PW[:, 0], 0.0)
                with dve.Fori(0, turns) as c:
                    e = dve.value_load(TURN_EI[0:1, bass.ds(c, 1)], min_val=0, max_val=NE - 1)
                    V.tensor_copy(OVC, COMB[:, :, bass.ds(e, 1)].rearrange("p a o -> p (a o)"))
                    V.tensor_tensor(OVP, POS[:, :, bass.ds(e, 1)].rearrange("p a o -> p (a o)"),
                                    TURN_BASE[:, bass.ds(c, 1)].broadcast_to([P, TT]), ALU.subtract).then_inc(sem["ov_place"], 1)
                    dve.wait_ge(sem["ov_place"], c + 1)
                    for a in range(TT):
                        last = V.tensor_tensor(P1[:, 0, a, 0:SLOTS], iota64, OVP[:, a:a + 1].broadcast_to([P, SLOTS]), ALU.is_equal)
                    last.then_inc(sem["ov_gathering"], 1)
                    dve.wait_ge(sem["ov_gathering"], c + 1)
                    for a in range(TT):
                        last = V.tensor_scalar(PW[:, 0, a, 0:SLOTS], P1[:, 0, a, 0:SLOTS], OVC[:, a:a + 1], None, ALU.mult)
                    last.then_inc(sem["ov_onehot"], 1)
                    dve.wait_ge(sem["ov_gate"], c + 1)
                    V.tensor_scalar(t1, PS[:, 0, :], LIMIT, None, ALU.min).then_inc(sem["ov_t1"], 1)
                    dve.wait_ge(sem["ov_sg"], c + 1)
                    V.tensor_tensor(t1, t1, sg, ALU.mult)
                    dve.wait_ge(sem["ov_up"], c + 1)
                    V.tensor_scalar(u_sb.rearrange("p (h n) -> p h n", h=2), PS[:, 1:3, 0:T], LIMIT, -LIMIT, ALU.min, ALU.max).then_inc(sem["ov_uread"], 1)
                    dve.wait_ge(sem["ov_uread"], c + 1)
                    V.scalar_tensor_tensor(out=hid, in0=u_sb, scalar=1.0, in1=t1, op0=ALU.add, op1=ALU.mult).then_inc(sem["ov_hid"], 1)
                    dve.wait_ge(sem["ov_down"], c + 1)
                    V.tensor_copy(OUTe[0:64, 0:512], PS[0:64, 3, :])
                    V.tensor_copy(OUTe[0:64, 512:1024], PS[64:128, 3, :]).then_inc(sem["ov_out"], 1)

            dve.wait_ge(sem["y_ready"], 1)
            dve.wait_ge(sem["late_loaded"], 32)
            gy = GAB_t[:, 2048:4096]
            for a in range(TT):
                for h in range(2):
                    s = slice(512 * h, 512 * h + 512)
                    last = V.tensor_tensor(gy[:, D * a + 512 * h:D * a + 512 * h + 512], PS[:, 4 + 2 * a + h, :], gate2b[:, s], ALU.mult)
            link(last)
            link(V.tensor_tensor(x_sb[:, :], x_sb[:, :], gy, ALU.add))
            for a in range(TT):
                link(V.tensor_tensor_reduce(out=gy[:, D * a:D * a + D], in0=x3[:, a, :], in1=x3[:, a, :], scale=1.0, scalar=0.0,
                                            op0=ALU.mult, op1=ALU.add, accum_out=ss3[:, a:a + 1]))
            V.tensor_scalar(ss3, ss3, 1.0 / D, RMS_EPS, ALU.mult, ALU.add).then_inc(sem["ss3_ready"], 1)
            dve.wait_ge(sem["rms3_ready"], 1)
            link(V.reciprocal(rstd3, rstd3))
            for a in range(TT):
                V.scalar_tensor_tensor(out=x3[:, a, :], in0=x3[:, a, :], scalar=rstd3[:, a:a + 1], in1=normfb,
                                       op0=ALU.mult, op1=ALU.mult).then_inc(sem["result_ready"], 1)

        @block.tensor
        def _(pe):
            M = nc.tensor

            pe.wait_ge(sem["consts_ready"], 1)
            pe.wait_ge(sem["vecs_loaded"], 16 * len(VECS))
            M.transpose(PS[:, 0, 0:NVEC], colrows[0:NVEC, :], ident[0:NVEC, 0:NVEC]).then_inc(sem["cols_done"], 1)
            for b in range(4):
                for k in (2 * b, 2 * b + 1):
                    for a in range(TT):
                        pe.wait_ge(sem["xn_ready"], a + 1)
                        c0 = (k % 2) * T + a * P
                        last = M.transpose(PS[:, 2 + b, c0:c0 + P], xn[:, a, P * k:P * k + P], ident)
                last.then_inc(sem["xT_done"], 1)

            def modulate(units, bank, done):
                for u in units:
                    pe.wait_ge(unit_full[u % 4], 16 * (u // 4 + 1))
                for k in range(KC):
                    for g, u in enumerate(units):
                        w = unit(u).rearrange("p (k n) -> p k n", k=KC)
                        last = M.matmul(PS[32 * g:32 * g + 32, bank, :], scr[:, k, :], w[:, k, :], start=(k == 0), stop=(k == KC - 1),
                                        tile_position=(0, 32 * g))
                last.then_inc(sem[done], 1)
                pe.wait_ge(sem[done], 1 + (units[0] - U_ADA1) // 4 if units[0] else 1)
                pe.sem_inc(sem["unit_free"], 4)

            pe.wait_ge(sem["scr_ready"], 1)
            modulate(range(0, ADA), 1, "mod_done")
            pe.wait_ge(sem["modrow_ready"], 1)
            for j in range(16):
                g = j // 4
                last = M.matmul(PS[:, COL_BANK[g], 64 + j % 4:65 + j % 4], modrow[32 * g:32 * g + 1, P * (j % 4):P * (j % 4) + P],
                                ones[32 * g:32 * g + 1, 0:1], start=True, stop=True, tile_position=(32 * g, 0))
            last.then_inc(sem["modcols_done"], 1)

            def tile(i):
                kind, u, c0, j = TILES[i]
                if i == 0:
                    pe.wait_ge(sem["hT_dve"], 4)
                    pe.wait_ge(sem["hT_act"], 4)
                n = u + ADA
                pe.wait_ge(unit_full[n % 4], 16 * (n // 4 + 1))
                if i >= 4:
                    pe.wait_ge(sem["tile_read"], i - 3)
                w = unit(n)[:, 0:KC * UNITS[u][2]].rearrange("p (k n) -> p k n", k=KC)
                for k in range(KC):
                    if kind == "vm":
                        last = M.matmul(PS[:, 4 + i % 4, :], hT[:, k, P * j:P * j + P], w[:, k, :], start=(k == 0), stop=(k == KC - 1))
                    else:
                        last = M.matmul(PS[:, 4 + i % 4, 0:T], w[:, k, c0:c0 + P], hT[:, k, :], start=(k == 0), stop=(k == KC - 1))
                last.then_inc(sem["tile_done"], 1)
                if i == UNIT_END[u]:
                    pe.wait_ge(sem["tile_done"], i + 1)
                    pe.sem_inc(sem["unit_free"], 1)

            def begin(name):
                ps, full, free, uses = aux(name)
                if uses:
                    pe.wait_ge(free, uses)
                return ps, full

            def run(i, to):
                for j in range(i, to):
                    tile(j)

            run(0, AFTER_LORA)
            pe.wait_ge(sem["lora_loaded"], 48)
            pe.wait_ge(sem["lora_act"], 1)
            pe.wait_ge(sem["hT_act"], 4)
            for name, w, x in (("zw", w2, PR[0:64, 12, 1:257]), ("za", a2, PR[64:128, 12, 1:257])):
                ps, full = begin(name)
                for q in range(HP):
                    last = M.matmul(ps[:, T * q:T * q + T], w[:, P * q:P * q + P], x, start=True, stop=True)
                last.then_inc(full, 1)
            run(AFTER_LORA, AFTER_KK)
            ps, full = begin("g")
            for q in range(HP):
                last = M.matmul(ps[:, T * q:T * q + T], g2[:, P * q:P * q + P], PR[:, 13, 1:257], start=True, stop=True)
            last.then_inc(full, 1)
            ps, full = begin("kk")
            pe.wait_ge(sem["kk_sq"], 1)
            for h in range(2):
                last = M.matmul(ps[:, 512 * h:512 * h + 512], blk, SQf[:, 512 * h:512 * h + 512], start=True, stop=True)
            last.then_inc(full, 1)
            run(AFTER_KK, AFTER_V)
            ps, full = begin("vt")
            pe.wait_ge(sem["v_shifted"], 1)
            for c in range(TT):
                for q in range(HP):
                    last = M.transpose(ps[:, 512 * c + P * q:512 * c + P * q + P], PR[:, 8 + q, 1 + P * c:1 + P * c + P], ident)
            last.then_inc(full, 1)
            run(AFTER_V, AFTER_SCORES)
            ps, full = begin("s0")
            pe.wait_ge(sem["tile_read"], AFTER_V)
            for h in range(RH):
                r = slice(64 * (h % 2), 64 * (h % 2) + 64)
                last = M.matmul(ps[:, P * place(h):P * place(h) + P], QK[r, h // 2, 0:P], QK[r, 4 + h // 2, 0:P], start=True, stop=True)
            last.then_inc(full, 1)
            for name, h0 in (("s1a", 0), ("s1b", 4)):
                ps, full = begin(name)
                for h in range(h0, h0 + 4):
                    r = slice(64 * (h % 2), 64 * (h % 2) + 64)
                    c0 = 512 * (h % 2) + T * ((h - h0) // 2)
                    last = M.matmul(ps[:, c0:c0 + T], QK[r, h // 2, P:T], QK[r, 4 + h // 2, :], start=True, stop=True)
                last.then_inc(full, 1)
            run(AFTER_SCORES, AFTER_PT)
            pe.wait_ge(sem["att_ready"], 1)
            for b in range(3):
                ps, full = begin(f"pt{b}")
                for h in range(RH):
                    last = M.transpose(ps[:, P * h:P * h + P], att[:, h, P * b:P * b + P], ident)
                last.then_inc(full, 1)
            run(AFTER_PT, AFTER_PV)
            ps, full = begin("pv")
            pe.wait_ge(sem["auxa_free"], AUX.index("pt2") // 2 + 1)
            pe.wait_ge(sem["tile_read"], AFTER_SCORES)
            for h in range(RH):
                r = slice(64 * (h % 2), 64 * (h % 2) + 64)
                c0 = T * (h // 2)
                v = slice(HD * h, HD * h + HD)
                M.matmul(ps[r, c0:c0 + P], VM[:, 0, v], PT[:, 0, place(h), :], start=True, stop=True)
                M.matmul(ps[r, c0 + P:c0 + T], VM[:, 0, v], PT[:, 1, place(h), :], start=True, stop=False)
                last = M.matmul(ps[r, c0 + P:c0 + T], VM[:, 1, v], PT[:, 2, place(h), :], start=False, stop=True)
            last.then_inc(full, 1)
            ps, full = begin("tok")
            pe.wait_ge(sem["ar_ready"], 1)
            for i, src in enumerate((Bf, K2f)):
                for q in range(HP):
                    last = M.transpose(ps[:, 512 * i + P * q:512 * i + P * q + P], src[:, T * q:T * q + P], ident)
            last.then_inc(full, 1)
            ps, full = begin("bonus")
            pe.wait_ge(sem["bon_ready"], 1)
            for q in range(HP):
                last = M.matmul(ps[:, T * q:T * q + T], blk, PR[:, q, 1:257], start=True, stop=True)
            last.then_inc(full, 1)
            at = AFTER_PV

            B4 = Bf.rearrange("p (q c t) -> p q c t", q=HP, c=TT)
            K4 = K2f.rearrange("p (q c t) -> p q c t", q=HP, c=TT)
            pe.wait_ge(sem["auxa_free"], 7)
            pe.wait_ge(sem["auxb_free"], 7)
            for c in range(TT):
                if c:
                    pe.wait_ge(sem["y_read"], c)
                    pe.wait_ge(sem["s_read"], c)
                for q in range(HP):
                    u = HP * c + q
                    if u:
                        pe.wait_ge(sem["bk_read"], u)
                    for i in range(2):
                        r = slice(64 * i, 64 * i + 64)
                        for j, src in enumerate((B4, K4)):
                            last = M.matmul(PS[:, i, T * j:T * j + T], src[r, q, c, :],
                                            AR[r, q, c].rearrange("p a t -> p (a t)"), start=True, stop=True)
                    last.then_inc(sem["bk_full"], 1)
                    if u:
                        pe.wait_ge(sem["x_read"], u)
                    for i in range(2):
                        r = slice(64 * i, 64 * i + 64)
                        last = M.matmul(PS[:, 2 + i, 0:P], AR[r, q, c, 0, :], B4[r, q, c, :], start=True, stop=True)
                    last.then_inc(sem["x_full"], 1)
                pe.wait_ge(sem["bk_read"], HP * (c + 1))
                for h in range(RH):
                    v = slice(HD * h, HD * h + HD)
                    r = slice(64 * (h % 2), 64 * (h % 2) + 64)
                    o = PS[:, h % 2, HD * (h // 2):HD * (h // 2) + HD]
                    last = M.matmul(o, BK[:, h, 1, 0, :], VT[:, c, v], start=True, stop=(c == 0))
                    if c:
                        last = M.matmul(o, AR[r, h // 2, c, 0, :], S1[r, h // 2, :], start=False, stop=True)
                last.then_inc(sem["r_full"], 1)
                pe.wait_ge(sem["x_read"], HP * (c + 1))
                pe.wait_ge(sem["r_read"], c + 1)
                pe.wait_ge(sem["n_init"], c + 1)
                pe.wait_ge(sem["m_init"], c + 1)
                for k in range(1, 7):
                    for g in range(2):
                        if k > 1:
                            pe.wait_ge(sem["level_read"], level_index(c, k - 1, "N", g) + 1)
                        for h in range(4 * g, 4 * g + 4):
                            last = M.matmul(PS[:, 2 * g, P * (h % 4):P * (h % 4) + P], XS[:, h, :], Nm[:, h, :], start=True, stop=True)
                        last.then_inc(sem["level_done"], 1)
                    if at < len(TILES):
                        tile(at)
                        at += 1
                    for g in range(2):
                        pe.wait_ge(sem["level_read"], level_index(c, k, "T", g) + 1)
                        for what in ("MN" if k < 6 else "N"):
                            for h in range(4 * g, 4 * g + 4):
                                lhsT, rhs = (TL, Mm) if what == "M" else (Mm, TL)
                                last = M.matmul(PS[:, 2 * g + (what == "N"), P * (h % 4):P * (h % 4) + P], lhsT[:, h, :], rhs[:, h, :],
                                                start=True, stop=True)
                            last.then_inc(sem["level_done"], 1)
                pe.wait_ge(sem["level_read"], level_index(c, 6, "N", 1) + 1)
                for h in range(RH):
                    v = slice(HD * h, HD * h + HD)
                    last = M.matmul(PS[:, 0, v], Nm[:, h, :], Rs[:, HD * place(h):HD * place(h) + HD], start=True, stop=True)
                last.then_inc(sem["u_full"], 1)
                pe.wait_ge(sem["u_read"], c + 1)
                for h in range(RH):
                    v = slice(HD * h, HD * h + HD)
                    r = slice(64 * (h % 2), 64 * (h % 2) + 64)
                    o = PS[r, 2, P * (h // 2):P * (h // 2) + P]
                    M.matmul(o, Us[:, v], BK[:, h, 0, 1, :], start=True, stop=False)
                    last = M.matmul(o, VT[:, c, v], BK[:, h, 1, 1, :], start=False, stop=(c == 0))
                    if c:
                        last = M.matmul(o, S1[r, h // 2, :], AR[r, h // 2, c, 1, :], start=False, stop=True)
                last.then_inc(sem["y_full"], 1)
                if c == 0:
                    for h in range(RH):
                        v = slice(HD * h, HD * h + HD)
                        o = PS[64 * (h % 2):64 * (h % 2) + 64, 3, HD * (h // 2):HD * (h // 2) + HD]
                        M.matmul(o, Btok[:, v], Us[:, v], start=True, stop=False)
                        last = M.matmul(o, Ktok[:, v], VT[:, 0, v], start=False, stop=True)
                    last.then_inc(sem["s_full"], 1)
            run(at, len(TILES))

            pe.wait_ge(sem["tile_read"], len(TILES))
            for r in range(2):
                modulate(range(U_ADA1 + 4 * r, U_ADA1 + 4 * r + 4), 4 + r, "mod12_done")

            pe.wait_ge(sem["y_read"], TT)
            for h in range(2):
                last = M.matmul(PS[:, h, :], blk, YTf[:, 512 * h:512 * h + 512], start=True, stop=True)
            last.then_inc(sem["gn_mean"], 1)
            pe.wait_ge(sem["gn_c"], 1)
            for h in range(2):
                last = M.matmul(PS[:, 2 + h, :], blk, Bf[:, 512 * h:512 * h + 512], start=True, stop=True)
            last.then_inc(sem["gn_var"], 1)

            for u in (U_BRANCH, U_BRANCH + 1):
                pe.wait_ge(unit_full[u % 4], 16 * (u // 4 + 1))
            pe.wait_ge(sem["yf_ready"], 1)
            for m in range(KC):
                if m >= 4:
                    pe.wait_ge(sem["z_read"], m - 3)
                for i, y in enumerate((YF, YB)):
                    w = unit(U_BRANCH + i).rearrange("p (k n) -> p k n", k=4)
                    for q in range(HP):
                        last = M.matmul(PS[:, m % 4, T * i:T * i + T], w[:, q, P * m:P * m + P], y[:, q, :], start=(q == 0), stop=(q == HP - 1))
                last.then_inc(sem["z_full"], 1)
            pe.wait_ge(sem["z_full"], KC)
            pe.sem_inc(sem["unit_free"], 2)
            pe.wait_ge(sem["mod12_ready"], 2)
            for k in range(KC):
                u = U_OUT + k // 4
                if k % 4 == 0:
                    pe.wait_ge(unit_full[u % 4], 16 * (u // 4 + 1))
                pe.wait_ge(sem["z_read"], k + 1)
                w = unit(u).rearrange("p (k n) -> p k n", k=4)
                for a in range(TT):
                    for h in range(2):
                        last = M.matmul(PS[:, 4 + 2 * a + h, :], zT[:, k, P * a:P * a + P], w[:, k % 4, 512 * h:512 * h + 512],
                                        start=(k == 0), stop=(k == KC - 1))
            last.then_inc(sem["mix_done"], 1)
            pe.wait_ge(sem["mix_done"], 1)
            pe.sem_inc(sem["unit_free"], 2)

            pe.wait_ge(sem["h2_ready"], 2)
            for b in range(4):
                for k in (2 * b, 2 * b + 1):
                    for a in range(TT):
                        c0 = (k % 2) * T + a * P
                        last = M.transpose(PS[:, b, c0:c0 + P], h2[:, a, P * k:P * k + P], ident)
                last.then_inc(sem["h2T_full"], 1)
            pe.wait_ge(sem["h2T_read"], 4)
            pe.wait_ge(sem["router_loaded"], 32)
            for a in range(TT):
                for k in range(KC):
                    last = M.matmul(PS[:, 0, NE * a:NE * a + NE], h2T[:, k, P * a:P * a + P], rw[:, k, :], start=(k == 0), stop=(k == KC - 1))
            last.then_inc(sem["logits_full"], 1)
            pe.wait_ge(sem["chosen_ready"], 1)
            strict = maskU[:, 0, :]
            M.matmul(PS[:, 1, 0:32], strict, MSK[:, 0, :], start=True, stop=True)
            M.matmul(PS[:, 1, 32:64], ones, MSK[:, 0, :], start=True, stop=False)
            M.matmul(PS[:, 1, 32:64], strict, MSK[:, 1, :], start=False, stop=True)
            M.matmul(PS[:, 1, 64:96], ones, MSK[:, 0, :], start=True, stop=False)
            M.matmul(PS[:, 1, 64:96], ones, MSK[:, 1, :], start=False, stop=True).then_inc(sem["pos_full"], 1)
            pe.wait_ge(sem["comb_ready"], 1)
            for a in range(TT):
                last = M.transpose(PS[0:NE, 2, P * a:P * a + P], COMB[:, a, 0:NE], ident)
            last.then_inc(sem["combT_full"], 1)
            pe.wait_ge(sem["combT_ready"], 1)
            pe.wait_ge(sem["bias_loaded"], 48)
            for a in range(TT):
                for h in range(2):
                    M.matmul(PS[:, 4 + 2 * a + h, :], combT[:, P * a:P * a + P], bdown[:, 512 * h:512 * h + 512], start=True, stop=True)

            def transpose_weights(b, done):
                for a in range(TT):
                    last = M.transpose(PS[:, 0, P * a:P * a + P], PW[:, b, a, :], ident)
                last.then_inc(sem[done], 1)

            def gather(b, done):
                for k in range(KC):
                    o = PS[:, 1 + k // 4, P * (k % 4):P * (k % 4) + P]
                    for a in range(TT):
                        last = M.matmul(o, h2[:, a, P * k:P * k + P], P1[:, b, a, :], start=(a == 0), stop=(a == TT - 1))
                last.then_inc(sem[done], 1)

            def combine(b, done):
                for a in range(TT):
                    for h in range(2):
                        last = M.matmul(PS[:, 4 + 2 * a + h, :], PWT[:, b, P * a:P * a + P], OUTe[:, 512 * h:512 * h + 512],
                                        start=False, stop=True, skip_group_check=True)
                last.then_inc(sem[done], 1)

            bias_of = {"gate": 0, "up": D}
            FILLS = 16 * 3 * NE // 4

            def project(what, slot, b, k, bank, c0, n, done, steps=range(KC + 1), sel=None):
                w = ring[:, slot, :].rearrange("p (k n) -> p k n", k=KC)
                for s in steps:
                    for h in range(2):
                        o = PS[64 * h:64 * h + 64, bank, 0:n]
                        if s < KC:
                            last = M.matmul(o, xe[:, b, s, 64 * k:64 * k + 64], w[:, s, 512 * h + c0:512 * h + c0 + n],
                                            start=(s == 0), stop=False, tile_position=(0, 64 * h))
                        else:
                            at = bias_of[what] + 512 * h + c0
                            last = M.matmul(o, selb[0:96, sel, :], bias3[0:96, at:at + n], start=False, stop=True, tile_position=(0, 64 * h))
                if done:
                    last.then_inc(sem[done], 1)

            def transpose_hidden(h):
                for q in (2 * h, 2 * h + 1):
                    last = M.transpose(PS[:, 0, P * q:P * q + P], hid[:, P * q:P * q + P], ident)
                return last

            def down(slot, qs, last_done):
                w = ring[:, slot, :].rearrange("p (k n) -> p k n", k=KC)
                for q in qs:
                    for f in range(2):
                        for h in range(2):
                            last = M.matmul(PS[64 * h:64 * h + 64, 3, :], hidT[:, q, 64 * f:64 * f + 64],
                                            w[:, 4 * f + q, 512 * h:512 * h + 512], start=(q == 0 and f == 0), stop=(q == 3 and f == 1),
                                            tile_position=(0, 64 * h))
                if last_done:
                    last.then_inc(sem[last_done], 1)

            pe.wait_ge(sem["prologue"], 1)
            with pe.Fori(0, PAIRS // 2) as i:
                for pp in range(2):
                    p = 2 * i + pp
                    pe.wait_ge(sem["weighted_ready"], p + 1)
                    pe.wait_ge(sem["hidT_read"], 4 * p + 1)
                    transpose_weights(pp, "pt_full")
                    pe.wait_ge(sem["up_read"], 4 * p + 1)
                    gather(pp, "gather_full")
                    pe.wait_ge(sem["out_read"], 2 * p + 1)
                    pe.wait_ge(sem["out_read_b"], 2 * p + 1)
                    combine(1 - pp, "combined")
                    pe.wait_ge(sem["gather_read"], p + 1)
                    for k in range(2):
                        e = 2 * p + k
                        m = 3 * (2 * pp + k)
                        fill = lambda j: 16 * (3 * i + j // 4 + 1)
                        pe.wait_ge(w_full[m % 4], fill(m))
                        if k:
                            pe.wait_ge(sem["hidT_read"], 4 * p + 3)
                        pe.wait_ge(sem["sel_ready"], e + 1)
                        project("gate", m % 4, pp, k, 0, 0, 512, "gate_done", sel=k)
                        pe.wait_ge(w_full[(m + 1) % 4], fill(m + 1))
                        if k:
                            pe.wait_ge(sem["up_read"], 4 * p + 3)
                        project("up", (m + 1) % 4, pp, k, 1, 0, T, "up_half_done", sel=k)
                        project("up", (m + 1) % 4, pp, k, 2, T, T, None, steps=range(0, 6), sel=k)
                        pe.wait_ge(sem["hid_ready"], 2 * e + 1)
                        transpose_hidden(0).then_inc(sem["hidT_full"], 1)
                        project("up", (m + 1) % 4, pp, k, 2, T, T, "up_done", steps=range(6, KC + 1), sel=k)
                        pe.wait_ge(w_full[(m + 2) % 4], fill(m + 2))
                        pe.wait_ge(sem["hidT_read"], 2 * e + 2)
                        if k:
                            pe.wait_ge(sem["out_read"], e + 1)
                            pe.wait_ge(sem["out_read_b"], e + 1)
                        down((m + 2) % 4, (0, 1), None)
                        pe.wait_ge(sem["hid_ready"], 2 * e + 2)
                        transpose_hidden(1).then_inc(sem["hidT_full"], 1)
                        pe.wait_ge(sem["hidT_read"], 2 * e + 3)
                        down((m + 2) % 4, (2, 3), "down_done")
            pe.wait_ge(sem["out_read"], NE + 1)
            pe.wait_ge(sem["out_read_b"], NE + 1)
            combine(1, "combined")

            turns = pe.value_load(N_TURNS[0:1, 0:1], min_val=0, max_val=MAX_TURNS)
            with pe.If(turns > 0):
                with pe.Fori(0, turns) as c:
                    pe.wait_ge(sem["ov_onehot"], c + 1)
                    transpose_weights(0, "ov_weights")
                    gather(0, "ov_gather")
                    pe.wait_ge(sem["ov_copied"], c + 1)
                    pe.wait_ge(sem["ov_sel"], c + 1)
                    pe.wait_ge(w_full[0], FILLS + 16 * (c + 1))
                    project("gate", 0, 0, 0, 0, 0, 512, "ov_gate", sel=0)
                    pe.wait_ge(w_full[1], FILLS + 16 * (c + 1))
                    project("up", 1, 0, 0, 1, 0, T, None, sel=0)
                    project("up", 1, 0, 0, 2, T, T, "ov_up", sel=0)
                    pe.wait_ge(sem["ov_hid"], c + 1)
                    transpose_hidden(0)
                    transpose_hidden(1).then_inc(sem["ov_hidT"], 1)
                    pe.wait_ge(w_full[2], FILLS + 16 * (c + 1))
                    pe.wait_ge(sem["ov_hidTc"], c + 1)
                    down(2, (0, 1, 2, 3), "ov_down")
                    pe.wait_ge(sem["ov_out"], c + 1)
                    combine(0, "ov_comb")
                    pe.wait_ge(sem["ov_comb"], c + 1)
            pe.wait_ge(sem["combined"], PAIRS + 1)
            pe.sem_inc(sem["y_ready"], 1)


_INS = ["x", "c", "w_ada", "b_ada", "norm1_g", "w_in", "rwkv_mu", "rwkv_w0", "rwkv_w2", "rwkv_a0", "rwkv_a2",
        "rwkv_g2", "rwkv_k_k", "rwkv_k_a", "rwkv_r_k", "rwkv_ln_w", "rwkv_ln_b", "w_branch_a", "w_branch_b",
        "w_out", "norm2_g", "router_w", "router_b", "exp_w_gate", "exp_b_gate", "exp_w_up", "exp_b_up",
        "exp_w_down", "exp_b_down", "normf_g"]


def kernel(**inputs):
    import concourse.bacc as bacc
    import numpy as np
    from concourse.bass_utils import run_bass_kernel_spmd

    nc = bacc.Bacc("TRN2", target_bir_lowering=False, num_devices=1)
    arrays, aps = {}, {}
    for name in _INS:
        a = np.ascontiguousarray(inputs[name])
        arrays[f"in_{name}"] = a
        aps[name] = nc.dram_tensor(f"in_{name}", a.shape, mybir.dt.from_np(a.dtype), kind="ExternalInput").ap()
    out = nc.dram_tensor("out_0", (1, T, D), F32, kind="ExternalOutput").ap()
    scratch = nc.dram_tensor("mod_rows", (8, 512), F32, kind="Internal").ap()
    block_kernel(nc, aps, out, scratch)
    r = run_bass_kernel_spmd(nc, [arrays], core_ids=[0])
    return r.results[0]["out_0"]
```

```python
from contextlib import ExitStack

import concourse.bass as bass
from concourse import mybir

F32 = mybir.dt.float32
BF16 = mybir.dt.bfloat16
I32 = mybir.dt.int32
U32 = mybir.dt.uint32
ALU = mybir.AluOpType
ACT = mybir.ActivationFunctionType
AX_X = mybir.AxisListType.X

P = 128
D = 1024
T = 256
TT = T // P
KC = D // P
HD = 64
RH = 8
HP = RH // 2
W = RH * HD
NE = 32
TOPK = 4
SLOTS = 64
PAIRS = NE // 2
MORE = T // SLOTS - 1
MAX_TURNS = T * TOPK // SLOTS
LIMIT = 7.0
ALPHA = 1.702
RMS_EPS = 1e-5
GN_EPS = 64e-5
NEG = -1e30
LAM = 0.6065306597126334
SCALE = HD ** -0.5
MID = HD - 1

VECS = [("c", 8), ("norm1_g", 8), ("rwkv_mu", 14), ("rwkv_w0", 4), ("rwkv_a0", 4), ("rwkv_k_k", 4),
        ("rwkv_k_a", 4), ("rwkv_r_k", 4), ("rwkv_ln_w", 4), ("rwkv_ln_b", 4)]
NVEC = sum(n for _, n in VECS)

LOADS = [("ada", 512 * c, 512) for c in range(4)]
LOADS += [("lora", 3 * W, 256), ("k", W, 512), ("r", 0, 512), ("v", 2 * W, 512), ("q", 1792, 512), ("km", 2304, 512), ("vm", 2816, 512)]
for _i, (_kind, _c) in enumerate((("ga", 3328), ("ga", 3840), ("gb", 4352), ("gb", 4864))):
    LOADS += [(_kind, _c, 512)] + [("ada", 2048 + 1024 * _i + 512 * _j, 512) for _j in range(2)]
LOADS += [("wb", 0, D), ("wa", 0, D), ("out", 0, D), ("out", 512, D)]
U_WB, U_WA, U_OUT, N_UNITS = (len(LOADS) - _n for _n in (4, 3, 2, 0))
TILES = []
_next = dict(r=0, k=4, v=8, lora=12, q=0, km=4, ga=0, gb=8, mod=0)
for _u in range(4, U_WB):
    _kind, _c0, _w = LOADS[_u]
    if _kind == "vm":
        TILES += [("vm", _u, 0, c) for c in range(TT)]
    elif _kind == "ada":
        if LOADS[_u - 1][0] == "ada":
            TILES.append(("mod", _u - 1, 0, _next["mod"]))
            _next["mod"] += 1
    else:
        TILES += [(_kind, _u, 128 * j, _next[_kind] + j) for j in range(_w // 128)]
        _next[_kind] += _w // 128
TILES += [("yb", U_WB, 128 * m, m) for m in range(KC)]
AT_CHUNK = (34, 41)
for _c, _i in enumerate(AT_CHUNK):
    TILES.insert(_i + 1, ("R", None, 0, _c))
AFTER_CHUNKS = AT_CHUNK[1] + 7
AFTER_LORA, AFTER_R, AFTER_Q, AFTER_K, AFTER_V, AFTER_PT, AFTER_PV = 10, 12, 18, 23, 24, 30, 31
BY_VECTOR = ("mod", "yb")


def tile_at(kind, j):
    return [n for n, t in enumerate(TILES) if t[0] == kind and t[3] == j][0]


def reads(i, by_vector=False):
    return sum((t[0] in BY_VECTOR) == by_vector for t in TILES[:i])


def place(h):
    return (h % 2) * HP + h // 2


def level_index(c, k, what, g):
    return c * 34 + (k - 1) * 6 + {"T": 0, "N": 2, "M": 4}[what] + g


def block_kernel(nc, A, out, scratch):
    ctx = ExitStack()
    with ctx:
        def sb(name, n, dt=F32, parts=P):
            return ctx.enter_context(nc.sbuf_tensor(name, [parts, n], dt))

        ring = ctx.enter_context(nc.sbuf_tensor("ring", [P, 4, KC * D], F32))
        PS = ctx.enter_context(nc.psum_tensor("PS", [P, 8, 512], F32))

        lmask_t = sb("lmask_t", 1024)
        lmask = lmask_t[:, 0:896].rearrange("p (k t) -> p k t", k=7)
        lmask0L = lmask_t[:, 896:1024]
        ident_t = sb("ident_t", 128)
        blk_t = sb("blk_t", 128)
        ones_t = sb("ones_t", 128)
        ident, blk, ones = ident_t[:, :], blk_t[:, :], ones_t[:, :]
        maskU_t = sb("maskU_t", 256)
        maskU = maskU_t[:, :].rearrange("p (a t) -> p a t", a=2)
        maskL = sb("maskL", 128)[:, :]
        negmask = sb("negmask", 128)[:, :]
        iota64 = sb("iota64", 64)[:, :]
        iota32 = sb("iota32", 32)[:, :]
        x_sb = sb("x_sb", TT * D)
        x3 = x_sb[:, :].rearrange("p (a d) -> p a d", a=TT)
        colrows = sb("colrows", 128)
        cols = sb("cols", 64)
        scr = sb("scr", KC * 32)[:, :].rearrange("p (k m) -> p k m", k=KC)
        modrow = sb("modrow", 1536)
        hT_t = sb("hT_t", KC * T)
        hT = hT_t[:, :].rearrange("p (k t) -> p k t", k=KC)
        PR_t = sb("PR_t", 14 * 257)
        PR = PR_t[:, :].rearrange("p (j t) -> p j t", j=14)
        QK_t = sb("QK_t", 8 * T)
        QK = QK_t[:, :].rearrange("p (j t) -> p j t", j=8)
        VM_t = sb("VM_t", TT * 512)
        VM = VM_t[:, :].rearrange("p (a d) -> p a d", a=TT)
        GAB_t = sb("GAB_t", 16 * T)
        GAB = GAB_t[:, :].rearrange("p (j t) -> p j t", j=16)
        WG = sb("WG", 1024)
        rw = sb("rw", KC * NE)[:, :].rearrange("p (k e) -> p k e", k=KC)
        rbias = sb("rbias", NE)[:, :]
        small = sb("small", 96)
        eye3 = sb("eye3", 32)
        selb_t = sb("selb", 2 * SLOTS, BF16)
        selb = selb_t[:, :].rearrange("p (b s) -> p b s", b=2)

        sh1c, s1c, sigc = small[:, 0:8], small[:, 8:16], small[:, 16:24]
        ss, rstd = small[:, 24:26], small[:, 26:28]
        decay_end = small[:, 28:32]
        mx, sums = small[:, 32:48], small[:, 48:64]
        eps_gn, eps_rms = small[:, 64:65], small[:, 65:66]
        ss2, rstd2, ss3, rstd3 = small[:, 66:68], small[:, 68:70], small[:, 70:72], small[:, 72:74]
        dsum = small[:, 76:80]
        ss2half = small[:, 80:84].rearrange("p (a h) -> p a h", a=TT)
        off, v = {}, 0
        for name, n in VECS:
            off[name] = v
            v += n

        def col(name, j, n=1):
            return cols[:, off[name] + j:off[name] + j + n]

        def over(ap, n):
            return ap.unsqueeze(2).broadcast_to([ap.shape[0], ap.shape[1], n])

        def unit(u):
            return ring[:, (u % 4) // 2, (u % 2) * 4096:(u % 2) * 4096 + 4096]

        TMP = ring[:, 2:4, :].rearrange("p a n -> p (a n)")
        heads = lambda a: a.rearrange("p (h t) -> p h t", h=RH)
        pairs = lambda a: a.rearrange("p (q t) -> p q t", q=HP)
        XS, Nm, Mm = (heads(TMP[:, 1024 * i:1024 * i + 1024]) for i in range(3))
        BK = TMP[:, 3072:7168].rearrange("p (h j a t) -> p h j a t", h=RH, j=2, a=2)
        TL = BK[:, :, 0, 0, :]
        ARz = TMP[:, 7168:9216].rearrange("p (q i a t) -> p q i a t", q=HP, i=2, a=2)
        Bf, K2f, SIGf, Af, KKf, Gf, VTf = (TMP[:, 9216 + 1024 * i:10240 + 1024 * i] for i in range(7))
        VT = VTf.rearrange("p (c d) -> p c d", c=TT)
        Rs, Us = KKf[:, 0:512], KKf[:, 512:1024]
        AR1 = SIGf.rearrange("p (q a t) -> p q a t", q=HP, a=2)
        S1 = modrow[:, 0:256].rearrange("p (q d) -> p q d", q=HP)
        YTf = Af
        bada0 = TMP[:, 0:512]
        xn = TMP[:, 7168:9216].rearrange("p (a d) -> p a d", a=TT)
        same = TMP[:, 2048:3072].rearrange("p (k t) -> p k t", k=8)
        Cf, Ccf, E1f, E2f, DIFf, NRMf, SQf = (TMP[:, 1024 * i:1024 * i + 1024] for i in range(7))
        att = TMP[:, 0:3072].rearrange("p (h t) -> p h t", h=RH)
        PT = TMP[:, 3072:6144].rearrange("p (b h t) -> p b h t", b=3, h=RH)
        w2, a2, g2 = WG[0:64, 0:512], WG[64:128, 0:512], WG[:, 512:1024]
        Btok, Ktok = WG[:, 0:512], WG[:, 512:1024]
        YB = QK[:, 0:4, :]
        Qz = (QK[:, 0:4, :], GAB[:, 8:12, :])
        gate1b = QK_t[:, 1024:2048]
        scale2b, shift2b = VM_t[:, :], WG[:, :]
        modrest = modrow[:, 512:1536].rearrange("p (v n) -> p v n", v=4)
        YF = PR[:, 0:4, 1:257]
        BON = PR[:, 4:8, 1:257]
        norm2b = PR_t[:, 2056:3080]
        zT = GAB[:, 0:8, :]

        h2 = hT_t[:, :].rearrange("p (a d) -> p a d", a=TT)
        h2T = GAB_t[:, 0:2048].rearrange("p (k t) -> p k t", k=KC)
        gate2b, normfb = GAB_t[:, 0:1024], GAB_t[:, 1024:2048]
        xe = GAB_t[:, 2048:4096].rearrange("p (b k s) -> p b k s", b=2, k=KC)
        biasraw = GAB_t[0:96, 2048:4096]
        bias3 = norm2b.bitcast(BF16)
        bdown = lmask_t[:, 0:1024]
        combT = modrow[:, 0:T]
        OUTe = PR_t[:, 0:1024]
        t1, u_sb, sg, hid = PR_t[:, 1024:1536], PR_t[:, 1536:2048], WG[:, 0:512], WG[:, 512:1024]
        hidT = PR_t[:, 3080:3592].rearrange("p (q s) -> p q s", q=4)
        L2, M8 = QK_t[:, 0:64].rearrange("p (a e) -> p a e", a=2), QK_t[:, 64:80].rearrange("p (a e) -> p a e", a=2)
        IX = QK_t[:, 80:96].bitcast(U32).rearrange("p (a e) -> p a e", a=2)
        IXF, EX = (QK_t[:, o:o + 8].rearrange("p (a e) -> p a e", a=2) for o in (96, 104))
        SM = QK_t[:, 112:114]
        OH = QK_t[:, 128:384].rearrange("p (a k e) -> p a k e", a=2, k=TOPK)
        MSK = QK_t[:, 384:448].rearrange("p (a e) -> p a e", a=2)
        COMB, POS = (QK_t[:, o:o + 68].rearrange("p (a e) -> p a e", a=2) for o in (448, 516))
        CNT = QK_t[:, 584:616]
        P1 = QK_t[:, 656:1168].rearrange("p (b a s) -> p b a s", b=2, a=TT)
        PW = QK_t[:, 1168:1680].rearrange("p (b a s) -> p b a s", b=2, a=TT)
        OVP, OVC = QK_t[:, 1680:1682], QK_t[:, 1682:1684]
        TAKEN, RANK = QK_t[:, 1684:1780], QK_t[:, 1780:1876]
        TURN3 = QK_t[:, 1876:1924].rearrange("p (l t) -> p l t", t=MORE)
        TURN_E, TURN_BASE = QK_t[:, 1924:1940], QK_t[:, 1940:1956]
        TURN_EI, N_TURNS = QK_t[:, 1956:1972].bitcast(I32), QK_t[:, 1972:1973].bitcast(I32)
        LISTING = modrow[:, 256:1024].rearrange("p (l t e) -> p l t e", l=MAX_TURNS // 2, t=MORE)
        PWT = VM_t[:, 0:512].rearrange("p (b t) -> p b t", b=2)

        sem = {}
        for n in """consts_ready x_loaded vecs_loaded bada_loaded lora_loaded router_loaded
                    ident_ready zeros_ready gate_folded comb_cleared cum_ready ar_next
                    cols_done cols_ready sigc_ready scr_ready ss_ready rms_ready xn_ready xT_done hT_dve hT_act
                    mod_done modrow_ready modcols_done modcols_read
                    unit_free tile_done tile_read lora_shifted lora_act kk_sq norm_ready kkn_read centred decays
                    v_shifted ar_ready bon_ready att_centred att_exp att_ready yb_ready
                    auxa_full auxa_free auxb_full auxb_free
                    x_full x_read bk_full bk_read n_init m_init level_done level_read
                    u_full u_read y_full y_read s_full s_read
                    gn_mean gn_c gn_var gn_std yf_ready
                    bada_rest_loaded mod_read yb_read scratch_written mod_bcast norm2_loaded
                    z_full z_read mix_done x1_ready ss2_ready rms2_ready h2_ready h2T_full h2T_read
                    logits_full top_ready top_exp scale2_ready chosen_ready comb_ready pos_full combT_full combT_ready bias_loaded bias_ready late_loaded
                    pool_chain dve_chain act_chain
                    gathering_ready weighted_ready pt_full pt_read gather_full gather_read out_read out_read_b combined sel_ready
                    gate_done up_half_done up_done down_done t1_ready sg_ready up_read hid_ready hidT_full hidT_read
                    prologue turns_listed
                    ov_onehot ov_gather ov_copied ov_gate ov_t1 ov_sg ov_up ov_hid ov_hidT ov_hidTc ov_down
                    ov_out ov_comb ov_sel ov_place ov_gathering ov_uread ov_weights
                    y_ready ss3_ready rms3_ready result_ready result_stored""".split():
            sem[n] = ctx.enter_context(nc.semaphore(n))
        unit_full = [ctx.enter_context(nc.semaphore(f"unit_full{i}")) for i in range(4)]
        w_full = [ctx.enter_context(nc.semaphore(f"w_full{i}")) for i in range(4)]

        AUX = ["zw", "za", "g", "kk", "vt", "s0", "s1a", "s1b", "tok", "bonus", "pt0", "pt1", "pt2", "pv"]

        def aux(name):
            n = AUX.index(name)
            full, free = ("auxa_full", "auxa_free") if n % 2 == 0 else ("auxb_full", "auxb_free")
            b = 0 if n % 2 == 0 else 2
            return PS[:, b:b + 2, :].rearrange("p a n -> p (a n)"), sem[full], sem[free], n // 2

        block = ctx.enter_context(nc.Block())

        @block.sync
        def _(sp):
            sp.dma_start(x3[:, :, :], A["x"][0].rearrange("(a p) d -> p a d", p=P)).then_inc(sem["x_loaded"], 16)
            row = 0
            for name, n in VECS:
                src = A[name]
                if name == "c":
                    src = src[0]
                elif name == "rwkv_r_k":
                    src = src.rearrange("h n -> (h n)")
                sp.dma_start(colrows[row:row + n, :], src.rearrange("(a b) -> a b", b=P)).then_inc(sem["vecs_loaded"], 16)
                row += n
            bias = A["b_ada"].rearrange("(v g n) -> g v n", v=6, g=4)
            for g in range(4):
                sp.dma_start(bada0[32 * g:32 * g + 32, :].rearrange("p (v n) -> p v n", v=2),
                             bias[g:g + 1, 0:2, :].broadcast_to([32, 2, 256])).then_inc(sem["bada_loaded"], 16)

            def load_unit(u):
                if u >= 4:
                    sp.wait_ge(sem["unit_free"], u - 3)
                kind, c0, w = LOADS[u]
                name = dict(ada="w_ada", wa="w_branch_a", wb="w_branch_b", out="w_out").get(kind, "w_in")
                src = A[name][c0:c0 + 512, :] if w == D else A[name][:, c0:c0 + w]
                k = src.shape[0] // P
                sp.dma_start(unit(u)[:, 0:k * w].rearrange("p (k n) -> p k n", k=k),
                             src.rearrange("(k p) n -> p k n", p=P)).then_inc(unit_full[u % 4], 16)

            for u in range(4):
                load_unit(u)
            sp.dma_start(w2, A["rwkv_w2"]).then_inc(sem["lora_loaded"], 16)
            sp.dma_start(a2, A["rwkv_a2"]).then_inc(sem["lora_loaded"], 16)
            sp.dma_start(g2, A["rwkv_g2"]).then_inc(sem["lora_loaded"], 16)
            sp.dma_start(rw, A["router_w"].rearrange("(k p) e -> p k e", p=P)).then_inc(sem["router_loaded"], 16)
            sp.dma_start(rbias, A["router_b"].rearrange("(a e) -> a e", a=1).broadcast_to([P, NE])).then_inc(sem["router_loaded"], 16)
            for g in range(4):
                sp.dma_start(modrest[32 * g:32 * g + 32, :, :], bias[g:g + 1, 2:6, :].broadcast_to([32, 4, 256])).then_inc(sem["bada_rest_loaded"], 16)
            for u in range(4, N_UNITS):
                load_unit(u)

            WEIGHTS = [A["exp_w_gate"], A["exp_w_up"], A["exp_w_down"]]
            DONE = [sem["gate_done"], sem["up_done"], sem["down_done"]]

            def load_matrix(e, kind, slot):
                sp.dma_start(ring[:, slot, :].rearrange("p (k n) -> p k n", k=KC),
                             WEIGHTS[kind][bass.ds(e, 1), :, :].rearrange("a (k p) n -> p (a k) n", p=P)).then_inc(w_full[slot], 16)

            sp.wait_ge(sem["yf_ready"], 1)
            load_matrix(0, 2, 2)
            load_matrix(1, 0, 3)
            sp.wait_ge(sem["unit_free"], N_UNITS)
            load_matrix(0, 0, 0)
            load_matrix(0, 1, 1)
            with sp.Fori(0, 7) as i:
                for q in range(4, 16):
                    sp.wait_ge(DONE[(q - 4) % 3], 4 * i + (q - 4) // 3 + 1)
                    load_matrix(4 * i + q // 3, q % 3, q % 4)
            for m in range(88, 96):
                sp.wait_ge(DONE[(m - 4) % 3], (m - 4) // 3 + 1)
                load_matrix(m // 3, m % 3, m % 4)

            def load_turn(c, used):
                e = sp.value_load(TURN_EI[0:1, bass.ds(c, 1)], min_val=0, max_val=NE - 1)
                for kind in range(3):
                    s, n = used[kind]
                    sp.wait_ge(s, n)
                    sp.dma_start(ring[:, kind, :].rearrange("p (k n) -> p k n", k=KC),
                                 WEIGHTS[kind][bass.ds(e, 1), :, :].rearrange("a (k p) n -> p (a k) n", p=P)).then_inc(w_full[kind], 16)

            sp.wait_ge(sem["turns_listed"], 1)
            turns = sp.value_load(N_TURNS[0:1, 0:1], min_val=0, max_val=MAX_TURNS)
            with sp.If(turns > 0):
                load_turn(0, ((DONE[2], NE - 1), (DONE[0], NE), (DONE[1], NE)))
                with sp.If(turns > 1):
                    with sp.Fori(1, turns) as c:
                        load_turn(c, ((sem["ov_gate"], c), (sem["ov_up"], c), (sem["ov_down"], c)))

            sp.wait_ge(sem["result_ready"], 1)
            sp.dma_start(out[0, 0:P, :], x3[:, 0, :]).then_inc(sem["result_stored"], 16)
            sp.wait_ge(sem["result_ready"], 2)
            sp.dma_start(out[0, P:T, :], x3[:, 1, :]).then_inc(sem["result_stored"], 16)
            sp.wait_ge(sem["result_stored"], 32)

        @block.gpsimd
        def _(pool):
            n = [0]

            def link(ins):
                n[0] += 1
                ins.then_inc(sem["pool_chain"], 1)
                pool.wait_ge(sem["pool_chain"], n[0])

            link(nc.gpsimd.memset(ident, 1.0))
            link(nc.gpsimd.affine_select(out=ident, in_=ident, compare_op=ALU.is_equal, fill=0.0, base=0,
                                         pattern=[[-1, P]], channel_multiplier=1))
            pool.sem_inc(sem["ident_ready"], 1)
            link(nc.gpsimd.memset(ones, 1.0))
            link(nc.gpsimd.memset(QK_t[64:128, 0:1024], 0.0))
            link(nc.gpsimd.memset(GAB_t[0:64, 2048:3072], 0.0))
            link(nc.gpsimd.memset(same, 1.0))
            for i in range(7):
                b = 1 << i
                v = same[:, i, :].rearrange("p (n b) -> p n b", b=b)
                link(nc.gpsimd.affine_select(out=v, in_=v, compare_op=ALU.is_ge, fill=0.0, base=0,
                                             pattern=[[-b, P // b], [0, b]], channel_multiplier=1))
                link(nc.gpsimd.affine_select(out=v, in_=v, compare_op=ALU.is_ge, fill=0.0, base=b - 1,
                                             pattern=[[b, P // b], [0, b]], channel_multiplier=-1))
            link(nc.gpsimd.tensor_copy(blk, same[:, 6, :]))
            for m, base, f, p in ((maskU[:, 0, :], -1, 1, -1), (maskU[:, 1, :], 0, 1, -1), (maskL, -1, -1, 1)):
                link(nc.gpsimd.affine_select(out=m, in_=ones, compare_op=ALU.is_ge, fill=0.0, base=base,
                                             pattern=[[f, P]], channel_multiplier=p))
            link(nc.gpsimd.memset(negmask, 0.0))
            link(nc.gpsimd.affine_select(out=negmask, in_=negmask, compare_op=ALU.is_ge, fill=NEG, base=0,
                                         pattern=[[-1, P]], channel_multiplier=1))
            link(nc.gpsimd.tensor_tensor(lmask, same[:, 1:8, :], same[:, 0:7, :], ALU.subtract))
            link(nc.gpsimd.tensor_tensor(lmask0L, lmask[:, 0, :], maskL, ALU.mult))
            link(nc.gpsimd.tensor_tensor(lmask, lmask, maskU[:, 0:1, :].broadcast_to([P, 7, P]), ALU.mult))
            link(nc.gpsimd.iota(iota64, pattern=[[1, 64]], base=0, channel_multiplier=0,
                                allow_small_or_imprecise_dtypes=True))
            link(nc.gpsimd.iota(iota32, pattern=[[1, 32]], base=0, channel_multiplier=0,
                                allow_small_or_imprecise_dtypes=True))
            pool.sem_inc(sem["consts_ready"], 1)

            pool.wait_ge(sem["xT_done"], 4)
            link(nc.gpsimd.memset(ARz[0:64, :, 1, :, :], 0.0))
            nc.gpsimd.memset(ARz[64:128, :, 0, :, :], 0.0).then_inc(sem["zeros_ready"], 1)
            pool.wait_ge(sem["zeros_ready"], 1)

            pool.wait_ge(sem["auxa_free"], AUX.index("g") // 2 + 1)
            pool.wait_ge(sem["auxb_free"], AUX.index("bonus") // 2 + 1)
            b4 = lambda name: over(col(name, 0, 4), T)
            link(nc.gpsimd.tensor_tensor(BON, BON, b4("rwkv_ln_b"), ALU.add))
            link(nc.gpsimd.tensor_tensor(BON, BON, pairs(Gf), ALU.mult))
            nc.gpsimd.tensor_tensor(pairs(Gf), pairs(Gf), b4("rwkv_ln_w"), ALU.mult).then_inc(sem["gate_folded"], 1)

            for c in range(TT):
                for q in range(HP):
                    hs = slice(2 * q, 2 * q + 2)
                    pool.wait_ge(sem["bk_read"], HP * c + q + 1)
                    if c and q == 0:
                        pool.wait_ge(sem["u_full"], 1)
                    link(nc.gpsimd.tensor_tensor(Nm[:, hs, :], BK[:, hs, 0, 0, :], lmask[:, 0:1, :].broadcast_to([P, 2, P]), ALU.mult))
                    nc.gpsimd.tensor_tensor(Nm[:, hs, :], Nm[:, hs, :], ident.unsqueeze(1).broadcast_to([P, 2, P]), ALU.add).then_inc(sem["n_init"], 1)
                if c == 0:
                    pool.wait_ge(sem["x_full"], HP)
                    link(nc.gpsimd.tensor_copy(ARz[0:64, :, 0], AR1[0:64]))
                    nc.gpsimd.tensor_copy(ARz[64:128, :, 1], AR1[64:128]).then_inc(sem["ar_next"], 1)
                    pool.wait_ge(sem["ar_next"], 1)

            pool.wait_ge(sem["mod_read"], 4)
            pool.dma_start(scratch.rearrange("a n -> (a n)").rearrange("(v g n) -> g v n", v=4, g=4), modrest[0:P:32, :, :]).then_inc(sem["scratch_written"], 16)
            pool.wait_ge(sem["scratch_written"], 16)
            pool.wait_ge(sem["s_full"], 1)
            pool.wait_ge(sem["auxb_full"], AUX.index("pv") // 2 + 1)
            for dst, r in ((gate1b, 0), (shift2b, 2), (scale2b, 4)):
                src = scratch[r:r + 2, :].rearrange("(o a) n -> o (a n)", o=1)
                pool.dma_start(dst, src.broadcast_to([P, D])).then_inc(sem["mod_bcast"], 16)
            pool.wait_ge(sem["auxb_free"], AUX.index("bonus") // 2 + 1)
            pool.dma_start(norm2b, A["norm2_g"].rearrange("(a n) -> a n", a=1).broadcast_to([P, D])).then_inc(sem["norm2_loaded"], 16)
            pool.wait_ge(sem["y_read"], TT)
            nc.gpsimd.memset(modrow[:, 0:T], 0.0).then_inc(sem["comb_cleared"], 1)
            pool.wait_ge(sem["z_read"], KC)
            for j in range(3):
                rows = slice(32 * j, 32 * j + 32)
                pool.dma_start(biasraw[rows, 0:D], A["exp_b_gate"]).then_inc(sem["bias_loaded"], 16)
                pool.dma_start(biasraw[rows, D:2 * D], A["exp_b_up"]).then_inc(sem["bias_loaded"], 16)
            pool.dma_start(bdown[0:NE], A["exp_b_down"]).then_inc(sem["bias_loaded"], 16)
            for j in range(3):
                link(nc.gpsimd.tensor_copy(eye3[32 * j:32 * j + 32, :], ident[0:32, 0:32]))
            pool.wait_ge(sem["bias_loaded"], 16 * 7)
            pool.wait_ge(sem["scale2_ready"], 1)
            rest = lambda rows: link(nc.gpsimd.tensor_tensor(biasraw[rows], biasraw[rows], bias3[rows], ALU.subtract))
            take = lambda rows: link(nc.gpsimd.tensor_copy(bias3[rows], biasraw[rows]))
            take(slice(0, 96))
            rest(slice(0, 96))
            take(slice(32, 64))
            take(slice(64, 96))
            rest(slice(64, 96))
            take(slice(64, 96))
            def select(k, e):
                nc.gpsimd.tensor_copy(selb[0:96, k, :], eye3[0:96, bass.ds(e, 1)].broadcast_to([96, SLOTS])).then_inc(sem["sel_ready"], 1)

            for k in range(2):
                select(k, k)
            pool.sem_inc(sem["bias_ready"], 1)
            pool.wait_ge(sem["logits_full"], TT)
            pool.dma_start(gate2b, scratch[6:8, :].rearrange("(o a) n -> o (a n)", o=1).broadcast_to([P, D])).then_inc(sem["late_loaded"], 16)
            pool.dma_start(normfb, A["normf_g"].rearrange("(a n) -> a n", a=1).broadcast_to([P, D])).then_inc(sem["late_loaded"], 16)
            with pool.Fori(1, PAIRS) as p:
                for k in range(2):
                    pool.wait_ge(sem["up_done"], 2 * p + k - 1)
                    select(k, 2 * p + k)

            def select_expert(c):
                e = pool.value_load(TURN_EI[0:1, bass.ds(c, 1)], min_val=0, max_val=NE - 1)
                nc.gpsimd.tensor_copy(selb[0:96, 0, :], eye3[0:96, bass.ds(e, 1)].broadcast_to([96, SLOTS])).then_inc(sem["ov_sel"], 1)

            pool.wait_ge(sem["turns_listed"], 1)
            turns = pool.value_load(N_TURNS[0:1, 0:1], min_val=0, max_val=MAX_TURNS)
            with pool.If(turns > 0):
                pool.wait_ge(sem["up_done"], NE)
                select_expert(0)
                with pool.If(turns > 1):
                    with pool.Fori(1, turns) as c:
                        pool.wait_ge(sem["ov_up"], c)
                        select_expert(c)

        @block.scalar
        def _(act):
            n = [0]

            def link(ins):
                n[0] += 1
                ins.then_inc(sem["act_chain"], 1)
                act.wait_ge(sem["act_chain"], n[0])

            act.wait_ge(sem["ss_ready"], 1)
            nc.scalar.activation(rstd, ss, ACT.Sqrt).then_inc(sem["rms_ready"], 1)
            act.wait_ge(sem["cols_ready"], 1)
            nc.scalar.activation(sigc, col("c", 0, 8), ACT.Sigmoid).then_inc(sem["sigc_ready"], 1)

            act.wait_ge(sem["modcols_read"], 1)
            for k in range(4, KC):
                act.wait_ge(sem["xT_done"], k // 2 + 1)
                nc.scalar.activation(hT[:, k, :], PS[:, 2 + k // 2, (k % 2) * T:(k % 2) * T + T], ACT.Identity,
                                     bias=sh1c[:, k:k + 1], scale=s1c[:, k:k + 1]).then_inc(sem["hT_act"], 1)

            def read_tiles(a, b):
                for i in range(a, b):
                    kind, u, c0, j = TILES[i]
                    src = PS[:, 4 + i % 4, 0:T]
                    if kind in BY_VECTOR:
                        continue
                    act.wait_ge(sem["tile_done"], i + 1)
                    if kind in ("r", "k", "v", "lora"):
                        dst, f = PR[:, j, 1:257], ACT.Copy
                    elif kind == "q":
                        nc.scalar.activation(Qz[0][0:64, j, :], src[0:64], ACT.Copy)
                        src, dst, f = src[64:128], Qz[1][64:128, j, :], ACT.Copy
                    elif kind == "km":
                        dst, f = QK[:, j, :], ACT.Copy
                    elif kind == "vm":
                        src, dst, f = PS[:, 4 + i % 4, :], VM[:, j, :], ACT.Copy
                    elif kind == "R":
                        src, dst, f = PS[:, 4 + i % 4, :], Rs, ACT.Copy
                    else:
                        dst, f = GAB[:, j, :], ACT.Sigmoid
                    nc.scalar.activation(dst, src, f).then_inc(sem["tile_read"], 1)

            def read_aux(name, dst, f=ACT.Copy, biases=None, **kw):
                ps, full, free, uses = aux(name)
                act.wait_ge(full, uses + 1)
                if biases is None:
                    last = nc.scalar.activation(dst, ps, f, **kw)
                else:
                    for q in range(HP):
                        last = nc.scalar.activation(dst[:, T * q:T * q + T], ps[:, T * q:T * q + T], f, bias=biases(q))
                last.then_inc(free, 1)

            read_tiles(0, 6)
            act.wait_ge(sem["lora_shifted"], 1)
            nc.scalar.activation(PR[0:64, 12, 1:257], PR[0:64, 12, 1:257], ACT.Tanh)
            nc.scalar.activation(PR[:, 13, 1:257], PR[:, 13, 1:257], ACT.Sigmoid).then_inc(sem["lora_act"], 1)
            read_tiles(6, AFTER_LORA)
            read_aux("zw", SIGf, ACT.Sigmoid, lambda q: col("rwkv_w0", q))
            read_aux("za", Af, ACT.Sigmoid, lambda q: col("rwkv_a0", q))
            read_tiles(AFTER_LORA, AFTER_R)
            read_aux("g", Gf)
            read_aux("kk", NRMf, ACT.Sqrt)
            act.wait_ge(sem["cum_ready"], 1)
            nc.scalar.activation(E1f, Ccf, ACT.Exp, scale=-LAM)
            nc.scalar.activation(DIFf, DIFf, ACT.Exp, scale=-LAM)
            nc.scalar.activation(decay_end, dsum, ACT.Exp, scale=-LAM)
            nc.scalar.activation(E2f, Ccf, ACT.Exp, scale=LAM).then_inc(sem["decays"], 1)
            read_tiles(AFTER_R, AFTER_Q)
            read_aux("vt", VTf)
            read_tiles(AFTER_Q, AFTER_V)
            read_aux("tok", WG[:, :])
            read_tiles(AFTER_V, AFTER_V + 3)
            act.wait_ge(sem["att_centred"], 1)
            nc.scalar.activation(att, att, ACT.Exp, scale=SCALE).then_inc(sem["att_exp"], 1)
            read_tiles(AFTER_V + 3, AFTER_PT)
            for b in range(3):
                read_aux(f"pt{b}", PT[:, b].rearrange("p h t -> p (h t)"))
            read_tiles(AFTER_PT, AFTER_PV)
            read_aux("pv", QK_t[:, 0:1024])
            read_tiles(AFTER_PV, AT_CHUNK[0])
            for c in range(TT):
                read_tiles(AT_CHUNK[c], AT_CHUNK[c] + 5)
                act.wait_ge(sem["u_full"], c + 1)
                nc.scalar.activation(Us, PS[:, 0, :], ACT.Copy).then_inc(sem["u_read"], 1)
                read_tiles(AT_CHUNK[c] + 5, AT_CHUNK[c] + 6)
                act.wait_ge(sem["y_full"], c + 1)
                nc.scalar.activation(YTf.rearrange("p (q t) -> p q t", q=HP)[:, :, P * c:P * c + P],
                                     PS[:, 2, :].rearrange("p (q t) -> p q t", q=HP), ACT.Copy).then_inc(sem["y_read"], 1)
                read_tiles(AT_CHUNK[c] + 6, AT_CHUNK[c] + 7)
            act.wait_ge(sem["gn_var"], 1)
            nc.scalar.activation(SIGf, PS[:, 2:4, :].rearrange("p a n -> p (a n)"), ACT.Sqrt, bias=eps_gn, scale=1.0 / HD).then_inc(sem["gn_std"], 1)

            for a in range(TT):
                act.wait_ge(sem["ss2_ready"], a + 1)
                nc.scalar.activation(rstd2[:, a:a + 1], ss2[:, a:a + 1], ACT.Sqrt).then_inc(sem["rms2_ready"], 1)
                for b in range(2):
                    act.wait_ge(sem["h2T_full"], 2 * a + b + 1)
                    nc.scalar.activation(h2T[:, 4 * b:4 * b + 4, P * a:P * a + P], PS[:, 2 * a + b, :].rearrange("p (k t) -> p k t", k=4), ACT.Copy).then_inc(sem["h2T_read"], 1)
            act.wait_ge(sem["top_ready"], 1)
            nc.scalar.activation(EX, EX, ACT.Exp).then_inc(sem["top_exp"], 1)
            act.wait_ge(sem["comb_cleared"], 1)
            act.wait_ge(sem["combT_full"], 1)
            nc.scalar.activation(combT[0:NE], PS[0:NE, 2, 0:T], ACT.Copy).then_inc(sem["combT_ready"], 1)

            act.sem_inc(sem["hidT_read"], 1)
            act.sem_inc(sem["out_read"], 1)
            with act.Fori(0, PAIRS // 2) as i:
                for pp in range(2):
                    p = 2 * i + pp
                    act.wait_ge(sem["pt_full"], p + 1)
                    nc.scalar.activation(PWT[:, pp, :], PS[:, 0, 0:T], ACT.Copy).then_inc(sem["pt_read"], 1)
                    act.wait_ge(sem["gather_full"], p + 1)
                    nc.scalar.activation(xe[:, pp].rearrange("p k s -> p (k s)"), PS[:, 1:3, :].rearrange("p a n -> p (a n)"), ACT.Copy).then_inc(sem["gather_read"], 1)
                    for k in range(2):
                        e = 2 * p + k
                        act.wait_ge(sem["t1_ready"], e + 1)
                        nc.scalar.activation(sg, t1, ACT.Sigmoid, scale=ALPHA).then_inc(sem["sg_ready"], 1)
                        for h in range(2):
                            act.wait_ge(sem["hidT_full"], 2 * e + h + 1)
                            nc.scalar.activation(hidT[:, 2 * h:2 * h + 2, :].rearrange("p q s -> p (q s)"),
                                                 PS[:, 0, T * h:T * h + T], ACT.Copy).then_inc(sem["hidT_read"], 1)
                        act.wait_ge(sem["down_done"], e + 1)
                        nc.scalar.activation(OUTe[64 * k:64 * k + 64, 0:512], PS[0:64, 3, :], ACT.Copy).then_inc(sem["out_read"], 1)
            act.wait_ge(sem["turns_listed"], 1)
            turns = act.value_load(N_TURNS[0:1, 0:1], min_val=0, max_val=MAX_TURNS)
            with act.If(turns > 0):
                with act.Fori(0, turns) as c:
                    act.wait_ge(sem["ov_gather"], c + 1)
                    nc.scalar.activation(PWT[:, 0, :], PS[:, 0, 0:T], ACT.Copy)
                    nc.scalar.activation(xe[:, 0].rearrange("p k s -> p (k s)"), PS[:, 1:3, :].rearrange("p a n -> p (a n)"), ACT.Copy).then_inc(sem["ov_copied"], 1)
                    act.wait_ge(sem["ov_t1"], c + 1)
                    nc.scalar.activation(sg, t1, ACT.Sigmoid, scale=ALPHA).then_inc(sem["ov_sg"], 1)
                    act.wait_ge(sem["ov_hidT"], c + 1)
                    nc.scalar.activation(hidT.rearrange("p q s -> p (q s)"), PS[:, 0, :], ACT.Copy).then_inc(sem["ov_hidTc"], 1)
            act.wait_ge(sem["ss3_ready"], 1)
            nc.scalar.activation(rstd3, ss3, ACT.Sqrt).then_inc(sem["rms3_ready"], 1)

        @block.vector
        def _(dve):
            n = [0]
            V = nc.vector

            def link(ins):
                n[0] += 1
                ins.then_inc(sem["dve_chain"], 1)
                dve.wait_ge(sem["dve_chain"], n[0])

            b4 = lambda name: over(col(name, 0, 4), T)

            def read_tiles(a, b):
                for i in range(a, b):
                    kind, _, _, j = TILES[i]
                    if kind in BY_VECTOR:
                        dve.wait_ge(sem["tile_done"], i + 1)
                    if kind == "mod":
                        V.tensor_tensor(modrest[:, j, :], PS[:, 4 + i % 4, 0:T], modrest[:, j, :], ALU.add).then_inc(sem["mod_read"], 1)
                    elif kind == "yb":
                        dve.wait_ge(sem["tile_read"], reads(tile_at("gb", 8 + j) + 1))
                        V.tensor_tensor(GAB[:, 8 + j, :], PS[:, 4 + i % 4, 0:T], GAB[:, 8 + j, :], ALU.mult).then_inc(sem["yb_read"], 1)

            r4, k4, v4 = PR[:, 0:4, 1:257], PR[:, 4:8, 1:257], PR[:, 8:12, 1:257]

            V.memset(PR[:, :, 0:1], 0.0)
            V.memset(eps_gn, GN_EPS)

            dve.wait_ge(sem["x_loaded"], 16)
            for a in range(TT):
                link(V.tensor_tensor_reduce(out=xn[:, a, :], in0=x3[:, a, :], in1=x3[:, a, :], scale=1.0, scalar=0.0,
                                            op0=ALU.mult, op1=ALU.add, accum_out=ss[:, a:a + 1]))
            V.tensor_scalar(ss, ss, 1.0 / D, RMS_EPS, ALU.mult, ALU.add).then_inc(sem["ss_ready"], 1)
            dve.wait_ge(sem["rms_ready"], 1)
            link(V.reciprocal(rstd, rstd))
            for a in range(TT):
                V.tensor_scalar(xn[:, a, :], x3[:, a, :], rstd[:, a:a + 1], None, ALU.mult).then_inc(sem["xn_ready"], 1)
            dve.wait_ge(sem["cols_done"], 1)
            V.tensor_copy(cols[:, 0:NVEC], PS[:, 0, 0:NVEC]).then_inc(sem["cols_ready"], 1)
            dve.wait_ge(sem["cols_ready"], 1)
            dve.wait_ge(sem["sigc_ready"], 1)
            V.tensor_tensor(scr, over(col("c", 0, 8), 32), over(sigc, 32), ALU.mult).then_inc(sem["scr_ready"], 1)
            dve.wait_ge(sem["bada_loaded"], 64)
            for v in range(2):
                dve.wait_ge(sem["mod_done"], v + 1)
                V.tensor_tensor(modrow[:, T * v:T * v + T], PS[:, 1 + 6 * v, 0:T], bada0[:, T * v:T * v + T], ALU.add).then_inc(sem["modrow_ready"], 1)
            dve.wait_ge(sem["modcols_done"], 1)
            turned = PS[:, 6, :].rearrange("p (v j g r) -> p v g j r", v=2, j=2, r=32)
            V.tensor_copy(sh1c.rearrange("p (g j) -> p g j", j=2), turned[:, 0, :, :, 0])
            V.scalar_tensor_tensor(out=s1c.rearrange("p (g j) -> p g j", j=2), in0=turned[:, 1, :, :, 0], scalar=1.0,
                                   in1=col("norm1_g", 0, 8).rearrange("p (g j) -> p g j", j=2),
                                   op0=ALU.add, op1=ALU.mult).then_inc(sem["modcols_read"], 1)
            dve.wait_ge(sem["modcols_read"], 1)
            for k in range(4):
                dve.wait_ge(sem["xT_done"], k // 2 + 1)
                V.tensor_scalar(hT[:, k, :], PS[:, 2 + k // 2, (k % 2) * T:(k % 2) * T + T], s1c[:, k:k + 1],
                                sh1c[:, k:k + 1], ALU.mult, ALU.add).then_inc(sem["hT_dve"], 1)

            def shift(j0, nj, signal=None):
                dif = VTf[:, 0:T * nj].rearrange("p (j t) -> p j t", j=nj)
                link(V.tensor_tensor(dif, PR[:, j0:j0 + nj, 0:T], PR[:, j0:j0 + nj, 1:257], ALU.subtract))
                for j in range(nj):
                    ins = V.scalar_tensor_tensor(out=PR[:, j0 + j, 1:257], in0=dif[:, j, :], scalar=col("rwkv_mu", j0 + j),
                                                 in1=PR[:, j0 + j, 1:257], op0=ALU.mult, op1=ALU.add)
                if signal:
                    ins.then_inc(sem[signal], 1)
                else:
                    link(ins)

            dve.wait_ge(sem["tile_read"], 2)
            shift(12, 2, "lora_shifted")
            dve.wait_ge(sem["lora_shifted"], 1)
            dve.wait_ge(sem["tile_read"], 6)
            shift(4, 4)
            link(V.tensor_tensor(pairs(KKf), k4, b4("rwkv_k_k"), ALU.mult))
            V.tensor_tensor(SQf, KKf, KKf, ALU.mult).then_inc(sem["kk_sq"], 1)
            dve.wait_ge(sem["tile_read"], 10)
            shift(0, 4)
            dve.wait_ge(sem["consts_ready"], 1)
            dve.wait_ge(sem["auxa_free"], 1)
            for q in range(2 * HP):
                last = V.tensor_tensor_scan(Cf[:, P * q:P * q + P], ones, SIGf[:, P * q:P * q + P], 0.0, ALU.mult, ALU.add)
            link(last)
            C8 = Cf.rearrange("p (j t) -> p j t", t=P)
            link(V.tensor_tensor(Ccf.rearrange("p (j t) -> p j t", t=P), C8,
                                 C8[:, :, MID:MID + 1].broadcast_to([P, 2 * HP, P]), ALU.subtract))
            C4 = Ccf.rearrange("p (q c t) -> p q c t", q=HP, c=TT)
            R4 = Cf.rearrange("p (q c t) -> p q c t", q=HP, c=TT)
            V.tensor_tensor(dsum.unsqueeze(2), C4[:, :, 0, P - 1:P], R4[:, :, 1, MID:MID + 1], ALU.add)
            V.tensor_tensor(DIFf, Ccf, SIGf, ALU.subtract).then_inc(sem["cum_ready"], 1)
            dve.wait_ge(sem["auxb_free"], 1)
            link(V.scalar_tensor_tensor(out=pairs(VTf), in0=pairs(Af), scalar=-1.0, in1=b4("rwkv_k_a"), op0=ALU.add, op1=ALU.mult))
            link(V.scalar_tensor_tensor(out=k4, in0=pairs(VTf), scalar=1.0, in1=k4, op0=ALU.add, op1=ALU.mult))
            dve.wait_ge(sem["auxb_free"], 2)
            link(V.tensor_scalar(NRMf, NRMf, 1e-12, None, ALU.max))
            link(V.reciprocal(NRMf, NRMf))
            link(V.tensor_tensor(KKf, KKf, NRMf, ALU.mult))
            link(V.tensor_tensor(Bf, KKf, Af, ALU.mult))
            dve.wait_ge(sem["tile_read"], 14)
            shift(8, 4, "v_shifted")
            dve.wait_ge(sem["decays"], 1)
            c4 = lambda a: a.rearrange("p (q c t) -> p q c t", q=HP, c=TT)
            for c, rows, dst in ((0, slice(0, 64), ARz[:, :, 0]), (0, slice(64, 128), ARz[:, :, 1]), (1, slice(0, P), AR1)):
                V.tensor_tensor(dst[rows, :, 1, :], PR[rows, 0:4, 1 + P * c:1 + P * c + P], c4(E1f)[rows, :, c, :], ALU.mult)
                V.scalar_tensor_tensor(out=dst[rows, :, 0, :], in0=c4(KKf)[rows, :, c, :], scalar=-1.0, in1=c4(DIFf)[rows, :, c, :],
                                       op0=ALU.mult, op1=ALU.mult)
            V.tensor_tensor(pairs(K2f), k4, pairs(E2f), ALU.mult)
            V.tensor_tensor(Bf, Bf, E2f, ALU.mult).then_inc(sem["ar_ready"], 1)
            dve.wait_ge(sem["ar_ready"], 1)
            link(V.tensor_tensor(r4, r4, k4, ALU.mult))
            V.tensor_tensor(r4, r4, b4("rwkv_r_k"), ALU.mult).then_inc(sem["bon_ready"], 1)

            ps, full, free, uses = aux("s0")
            dve.wait_ge(full, uses + 1)
            V.tensor_tensor(att[:, :, 0:P], heads(ps), negmask.unsqueeze(1).broadcast_to([P, RH, P]), ALU.add).then_inc(free, 1)
            for name, h0 in (("s1a", 0), ("s1b", 4)):
                ps, full, free, uses = aux(name)
                s = ps.rearrange("p (i q t) -> p i q t", i=2, q=2)
                dst = att.rearrange("p (i q) t -> p i q t", i=2)[:, :, h0 // 2:h0 // 2 + 2, :]
                dve.wait_ge(full, uses + 1)
                V.tensor_copy(dst[:, :, :, P:2 * P], s[:, :, :, 0:P])
                for i in range(2):
                    last = V.tensor_tensor(dst[:, i, :, 2 * P:3 * P], s[:, i, :, P:T], negmask.unsqueeze(1).broadcast_to([P, 2, P]), ALU.add)
                last.then_inc(free, 1)
            dve.wait_ge(sem["auxb_free"], 4)
            dve.wait_ge(sem["auxa_free"], 4)
            parts = ((att[:, :, 0:P], 0, P), (att[:, :, P:3 * P], RH, 2 * P))
            for a, m, w in parts:
                last = V.tensor_reduce(mx[:, m:m + RH], a, AX_X, ALU.max)
            link(last)
            for a, m, w in parts:
                last = V.tensor_tensor(a, a, over(mx[:, m:m + RH], w), ALU.subtract)
            last.then_inc(sem["att_centred"], 1)
            ps, full, free, uses = aux("bonus")
            dve.wait_ge(full, uses + 1)
            V.tensor_tensor(BON, pairs(ps), v4, ALU.mult).then_inc(free, 1)
            dve.wait_ge(sem["att_exp"], 1)
            for a, m, w in parts:
                last = V.tensor_reduce(sums[:, m:m + RH], a, AX_X, ALU.add)
            link(last)
            link(V.reciprocal(sums, sums))
            for a, m, w in parts:
                last = V.tensor_tensor(a, a, over(sums[:, m:m + RH], w), ALU.mult)
            last.then_inc(sem["att_ready"], 1)
            dve.wait_ge(sem["bada_rest_loaded"], 64)
            read_tiles(0, AT_CHUNK[0])

            steps = 0
            for c in range(TT):
                for q in range(HP):
                    u = HP * c + q
                    dve.wait_ge(sem["bk_full"], u + 1)
                    V.tensor_tensor(BK[:, 2 * q:2 * q + 2].rearrange("p i j a t -> p i j (a t)"),
                                    PS[:, 0:2, :].rearrange("p j (i t) -> p i j t", i=2),
                                    maskU_t[:, :].unsqueeze(1).unsqueeze(1).broadcast_to([P, 2, 2, T]), ALU.mult).then_inc(sem["bk_read"], 1)
                    dve.wait_ge(sem["x_full"], u + 1)
                    V.tensor_tensor(XS[:, 2 * q:2 * q + 2, :], PS[:, 2:4, 0:P],
                                    maskL.unsqueeze(1).broadcast_to([P, 2, P]), ALU.mult).then_inc(sem["x_read"], 1)
                dve.wait_ge(sem["x_read"], HP * (c + 1))
                link(V.tensor_tensor(Mm, XS, lmask0L.unsqueeze(1).broadcast_to([P, RH, P]), ALU.mult))
                V.tensor_tensor(Mm, Mm, ident.unsqueeze(1).broadcast_to([P, RH, P]), ALU.add).then_inc(sem["m_init"], 1)
                dve.wait_ge(sem["n_init"], HP * (c + 1))
                for k in range(1, 7):
                    seq = [(w, g) for w in ("TNM" if k < 6 else "TN") for g in range(2)]
                    for what, g in seq:
                        if what == "N" and g == 0 and k % 2 == 0:
                            read_tiles(AT_CHUNK[c] + k // 2 + 1, AT_CHUNK[c] + k // 2 + 2)
                        assert steps == level_index(c, k, what, g)
                        dve.wait_ge(sem["level_done"], steps + 1)
                        hs = slice(4 * g, 4 * g + 4)
                        ps = PS[:, 2 * g + (what != "M"), :].rearrange("p (h t) -> p h t", h=4)
                        if what == "T":
                            ins = V.tensor_tensor(TL[:, hs, :], ps, lmask[:, k:k + 1, :].broadcast_to([P, 4, P]), ALU.mult)
                        else:
                            m = Mm if what == "M" else Nm
                            ins = V.tensor_tensor(m[:, hs, :], m[:, hs, :], ps, ALU.add)
                        ins.then_inc(sem["level_read"], 1)
                        steps += 1
                read_tiles(AT_CHUNK[c] + 5, AT_CHUNK[c] + 6)
                if c == 0:
                    dve.wait_ge(sem["s_full"], 1)
                    V.tensor_tensor(S1, PS[:, 3, 0:T].rearrange("p (q d) -> p q d", q=HP), over(decay_end, HD), ALU.mult).then_inc(sem["s_read"], 1)
                read_tiles(AT_CHUNK[c] + 6, AT_CHUNK[c] + 7)

            dve.wait_ge(sem["gn_mean"], 1)
            YC, SQ2 = KKf, Bf
            link(V.scalar_tensor_tensor(out=YC, in0=PS[:, 0:2, :].rearrange("p a n -> p (a n)"), scalar=-1.0 / HD, in1=YTf,
                                        op0=ALU.mult, op1=ALU.add))
            link(V.tensor_tensor(SQ2, YC, YC, ALU.mult))
            dve.sem_inc(sem["gn_c"], 1)
            dve.wait_ge(sem["gate_folded"], 1)
            link(V.tensor_tensor(YC, YC, Gf, ALU.mult))
            read_tiles(AFTER_CHUNKS, AFTER_CHUNKS + 3)
            dve.wait_ge(sem["gn_std"], 1)
            link(V.reciprocal(SIGf, SIGf))
            link(V.tensor_tensor(YC, YC, SIGf, ALU.mult))
            V.tensor_tensor(YF, pairs(YC), BON, ALU.add).then_inc(sem["yf_ready"], 1)
            read_tiles(AFTER_CHUNKS + 3, len(TILES))

            za = PR_t[:, 1028:1540].rearrange("p (i t) -> p i t", i=2)
            dve.wait_ge(sem["yf_ready"], 1)
            dve.wait_ge(sem["yb_read"], KC)
            for m in range(KC):
                dve.wait_ge(sem["z_full"], m + 1)
                link(V.tensor_tensor(za[:, m % 2, :], PS[:, m % 4, 0:T], GAB[:, m, :], ALU.mult))
                V.tensor_tensor(zT[:, m, :], za[:, m % 2, :], GAB[:, 8 + m, :], ALU.add).then_inc(sem["z_read"], 1)

            dve.wait_ge(sem["mod_bcast"], 48)
            dve.wait_ge(sem["norm2_loaded"], 16)
            dve.wait_ge(sem["z_read"], KC)
            V.scalar_tensor_tensor(out=scale2b, in0=scale2b, scalar=1.0, in1=norm2b, op0=ALU.add, op1=ALU.mult).then_inc(sem["scale2_ready"], 1)
            dve.wait_ge(sem["scale2_ready"], 1)
            mixed = PR_t[:, 0:2048].rearrange("p (a d) -> p a d", a=TT)
            for a in range(TT):
                for h in range(2):
                    s = slice(512 * h, 512 * h + 512)
                    dve.wait_ge(sem["mix_done"], 2 * a + h + 1)
                    link(V.tensor_tensor(mixed[:, a, s], PS[:, 4 + 2 * a + h, :], gate1b[:, s], ALU.mult))
                    link(V.tensor_tensor(x3[:, a, s], x3[:, a, s], mixed[:, a, s], ALU.add))
                    link(V.tensor_tensor_reduce(out=mixed[:, a, s], in0=x3[:, a, s], in1=x3[:, a, s], scale=1.0, scalar=0.0,
                                                op0=ALU.mult, op1=ALU.add, accum_out=ss2half[:, a, h:h + 1]))
                link(V.tensor_tensor(ss2[:, a:a + 1], ss2half[:, a, 0:1], ss2half[:, a, 1:2], ALU.add))
                V.tensor_scalar(ss2[:, a:a + 1], ss2[:, a:a + 1], 1.0 / D, RMS_EPS, ALU.mult, ALU.add).then_inc(sem["ss2_ready"], 1)
                dve.wait_ge(sem["rms2_ready"], a + 1)
                link(V.reciprocal(rstd2[:, a:a + 1], rstd2[:, a:a + 1]))
                for h in range(2):
                    s = slice(512 * h, 512 * h + 512)
                    link(V.scalar_tensor_tensor(out=h2[:, a, s], in0=x3[:, a, s], scalar=rstd2[:, a:a + 1], in1=scale2b[:, s],
                                                op0=ALU.mult, op1=ALU.mult))
                    V.tensor_tensor(h2[:, a, s], h2[:, a, s], shift2b[:, s], ALU.add).then_inc(sem["h2_ready"], 1)
            dve.wait_ge(sem["h2_ready"], 2 * TT)

            V.memset(COMB, 0.0)
            V.memset(POS, 0.0)
            V.memset(PWT[:, 1, :], 0.0)
            V.memset(OUTe, 0.0).then_inc(sem["prologue"], 1)
            dve.wait_ge(sem["prologue"], 1)
            dve.wait_ge(sem["router_loaded"], 32)
            for a in range(TT):
                dve.wait_ge(sem["logits_full"], a + 1)
                link(V.tensor_tensor(L2[:, a, :], PS[:, 2 * a, 0:NE], rbias, ALU.add))
                link(V.max(M8[:, a, :], L2[:, a, :]))
                link(V.max_index(IX[:, a, :], M8[:, a, :], L2[:, a, :]))
            V.tensor_copy(IXF, IX[:, :, 0:TOPK])
            V.tensor_tensor(EX, M8[:, :, 0:TOPK], M8[:, :, 0:1].broadcast_to([P, 2, TOPK]), ALU.subtract).then_inc(sem["top_ready"], 1)
            dve.wait_ge(sem["top_ready"], 1)
            for a in range(TT):
                last = V.tensor_tensor(OH[:, a], iota32.unsqueeze(1).broadcast_to([P, TOPK, NE]), over(IXF[:, a, :], NE), ALU.is_equal)
            link(last)
            V.tensor_reduce(MSK, OH.rearrange("p a k e -> p a e k"), AX_X, ALU.add).then_inc(sem["chosen_ready"], 1)
            dve.wait_ge(sem["top_exp"], 1)
            link(V.tensor_reduce(SM, EX, AX_X, ALU.add))
            link(V.reciprocal(SM, SM))
            link(V.tensor_tensor(EX, EX, over(SM, TOPK), ALU.mult))
            for a in range(TT):
                last = V.tensor_tensor(OH[:, a], OH[:, a], over(EX[:, a, :], NE), ALU.mult)
            link(last)
            V.tensor_reduce(COMB[:, :, 0:NE], OH.rearrange("p a k e -> p a e k"), AX_X, ALU.add).then_inc(sem["comb_ready"], 1)
            dve.wait_ge(sem["pos_full"], 1)
            link(V.scalar_tensor_tensor(out=POS[:, :, 0:NE], in0=PS[:, 1, 0:64].rearrange("p (a e) -> p a e", a=2), scalar=1.0,
                                        in1=MSK, op0=ALU.add, op1=ALU.mult))
            link(V.tensor_scalar(POS, POS, -1.0, None, ALU.add))
            V.tensor_copy(CNT, PS[:, 1, 64:96])

            def one_hot(b, p):
                pos = POS[:, :, bass.ds(2 * p, 2)].unsqueeze(3).broadcast_to([P, TT, 2, SLOTS])
                comb = COMB[:, :, bass.ds(2 * p, 2)].unsqueeze(3).broadcast_to([P, TT, 2, SLOTS])
                gathering = P1[:, b].rearrange("p a (k s) -> p a k s", k=2)
                weighted = PW[:, b].rearrange("p a (k s) -> p a k s", k=2)
                for a in range(TT):
                    last = V.tensor_tensor(gathering[:, a], iota64.unsqueeze(1).broadcast_to([P, 2, SLOTS]), pos[:, a], ALU.is_equal)
                last.then_inc(sem["gathering_ready"], 1)
                dve.wait_ge(sem["gathering_ready"], p + 1)
                for a in range(TT):
                    last = V.tensor_tensor(weighted[:, a], gathering[:, a], comb[:, a], ALU.mult)
                last.then_inc(sem["weighted_ready"], 1)

            one_hot(0, 0)
            dve.sem_inc(sem["up_read"], 1)
            dve.sem_inc(sem["out_read_b"], 1)

            for t in range(MORE):
                last = V.tensor_scalar(TAKEN[:, NE * t:NE * t + NE], CNT, float(SLOTS * (t + 1)), None, ALU.is_gt)
            link(last)
            link(V.tensor_tensor_scan(RANK, ones[:, 0:MORE * NE], TAKEN, 0.0, ALU.mult, ALU.add))
            V.tensor_copy(N_TURNS, RANK[:, MORE * NE - 1:MORE * NE])
            link(V.tensor_tensor(TAKEN, TAKEN, RANK, ALU.mult))
            link(V.tensor_scalar(TAKEN, TAKEN, -1.0, None, ALU.add))
            flat = LISTING.rearrange("p l t e -> p l (t e)")
            for i in range(2):
                part = slice(MAX_TURNS // 2 * i, MAX_TURNS // 2 * (i + 1))
                link(V.tensor_tensor(flat, over(iota64[:, part], MORE * NE), TAKEN.unsqueeze(1).broadcast_to([P, MAX_TURNS // 2, MORE * NE]), ALU.is_equal))
                link(V.tensor_reduce(TURN3[:, part, :], LISTING, AX_X, ALU.add))
                for t in range(MORE):
                    last = V.tensor_tensor(LISTING[:, :, t, :], LISTING[:, :, t, :], iota32.unsqueeze(1).broadcast_to([P, MAX_TURNS // 2, NE]), ALU.mult)
                link(last)
                link(V.tensor_reduce(TURN_E[:, part], flat, AX_X, ALU.add))
            link(V.scalar_tensor_tensor(out=TURN_BASE, in0=TURN3[:, :, 1], scalar=2.0, in1=TURN3[:, :, 0], op0=ALU.mult, op1=ALU.add))
            link(V.scalar_tensor_tensor(out=TURN_BASE, in0=TURN3[:, :, 2], scalar=3.0, in1=TURN_BASE, op0=ALU.mult, op1=ALU.add))
            link(V.tensor_scalar(TURN_BASE, TURN_BASE, float(SLOTS), None, ALU.mult))
            V.tensor_copy(TURN_EI, TURN_E).then_inc(sem["turns_listed"], 1)
            with dve.Fori(0, PAIRS // 2) as i:
                for pp in range(2):
                    p = 2 * i + pp
                    for k in range(2):
                        e = 2 * p + k
                        dve.wait_ge(sem["gate_done"], e + 1)
                        V.tensor_scalar(t1, PS[:, 0, :], LIMIT, None, ALU.min).then_inc(sem["t1_ready"], 1)
                        dve.wait_ge(sem["sg_ready"], e + 1)
                        V.tensor_tensor(t1, t1, sg, ALU.mult)
                        for h in range(2):
                            s = slice(T * h, T * h + T)
                            dve.wait_ge(sem["up_done" if h else "up_half_done"], e + 1)
                            V.tensor_scalar(u_sb[:, s], PS[:, 1 + h, 0:T], LIMIT, -LIMIT, ALU.min, ALU.max).then_inc(sem["up_read"], 1)
                            dve.wait_ge(sem["up_read"], 2 * e + h + 2)
                            V.scalar_tensor_tensor(out=hid[:, s], in0=u_sb[:, s], scalar=1.0, in1=t1[:, s],
                                                   op0=ALU.add, op1=ALU.mult).then_inc(sem["hid_ready"], 1)
                        if k == 1:
                            one_hot(1 - pp, p + 1)
                        dve.wait_ge(sem["down_done"], e + 1)
                        V.tensor_copy(OUTe[64 * k:64 * k + 64, 512:1024], PS[64:128, 3, :]).then_inc(sem["out_read_b"], 1)

            turns = dve.value_load(N_TURNS[0:1, 0:1], min_val=0, max_val=MAX_TURNS)
            with dve.If(turns > 0):
                dve.wait_ge(sem["weighted_ready"], PAIRS + 1)
                V.memset(P1[:, 0], 0.0)
                V.memset(PW[:, 0], 0.0)
                with dve.Fori(0, turns) as c:
                    e = dve.value_load(TURN_EI[0:1, bass.ds(c, 1)], min_val=0, max_val=NE - 1)
                    V.tensor_copy(OVC, COMB[:, :, bass.ds(e, 1)].rearrange("p a o -> p (a o)"))
                    V.tensor_tensor(OVP, POS[:, :, bass.ds(e, 1)].rearrange("p a o -> p (a o)"),
                                    TURN_BASE[:, bass.ds(c, 1)].broadcast_to([P, TT]), ALU.subtract).then_inc(sem["ov_place"], 1)
                    dve.wait_ge(sem["ov_place"], c + 1)
                    for a in range(TT):
                        last = V.tensor_tensor(P1[:, 0, a, 0:SLOTS], iota64, OVP[:, a:a + 1].broadcast_to([P, SLOTS]), ALU.is_equal)
                    last.then_inc(sem["ov_gathering"], 1)
                    dve.wait_ge(sem["ov_gathering"], c + 1)
                    for a in range(TT):
                        last = V.tensor_scalar(PW[:, 0, a, 0:SLOTS], P1[:, 0, a, 0:SLOTS], OVC[:, a:a + 1], None, ALU.mult)
                    last.then_inc(sem["ov_onehot"], 1)
                    dve.wait_ge(sem["ov_gate"], c + 1)
                    V.tensor_scalar(t1, PS[:, 0, :], LIMIT, None, ALU.min).then_inc(sem["ov_t1"], 1)
                    dve.wait_ge(sem["ov_sg"], c + 1)
                    V.tensor_tensor(t1, t1, sg, ALU.mult)
                    dve.wait_ge(sem["ov_up"], c + 1)
                    V.tensor_scalar(u_sb.rearrange("p (h n) -> p h n", h=2), PS[:, 1:3, 0:T], LIMIT, -LIMIT, ALU.min, ALU.max).then_inc(sem["ov_uread"], 1)
                    dve.wait_ge(sem["ov_uread"], c + 1)
                    V.scalar_tensor_tensor(out=hid, in0=u_sb, scalar=1.0, in1=t1, op0=ALU.add, op1=ALU.mult).then_inc(sem["ov_hid"], 1)
                    dve.wait_ge(sem["ov_down"], c + 1)
                    V.tensor_copy(OUTe[0:64, 0:512], PS[0:64, 3, :])
                    V.tensor_copy(OUTe[0:64, 512:1024], PS[64:128, 3, :]).then_inc(sem["ov_out"], 1)

            dve.wait_ge(sem["y_ready"], 1)
            dve.wait_ge(sem["late_loaded"], 32)
            gy = GAB_t[:, 2048:4096]
            for a in range(TT):
                for h in range(2):
                    s = slice(512 * h, 512 * h + 512)
                    last = V.tensor_tensor(gy[:, D * a + 512 * h:D * a + 512 * h + 512], PS[:, 4 + 2 * a + h, :], gate2b[:, s], ALU.mult)
            link(last)
            link(V.tensor_tensor(x_sb[:, :], x_sb[:, :], gy, ALU.add))
            for a in range(TT):
                link(V.tensor_tensor_reduce(out=gy[:, D * a:D * a + D], in0=x3[:, a, :], in1=x3[:, a, :], scale=1.0, scalar=0.0,
                                            op0=ALU.mult, op1=ALU.add, accum_out=ss3[:, a:a + 1]))
            V.tensor_scalar(ss3, ss3, 1.0 / D, RMS_EPS, ALU.mult, ALU.add).then_inc(sem["ss3_ready"], 1)
            dve.wait_ge(sem["rms3_ready"], 1)
            link(V.reciprocal(rstd3, rstd3))
            for a in range(TT):
                V.scalar_tensor_tensor(out=x3[:, a, :], in0=x3[:, a, :], scalar=rstd3[:, a:a + 1], in1=normfb,
                                       op0=ALU.mult, op1=ALU.mult).then_inc(sem["result_ready"], 1)

        @block.tensor
        def _(pe):
            M = nc.tensor

            pe.wait_ge(sem["ident_ready"], 1)
            pe.wait_ge(sem["vecs_loaded"], 16 * len(VECS))
            M.transpose(PS[:, 0, 0:NVEC], colrows[0:NVEC, :], ident[0:NVEC, 0:NVEC]).then_inc(sem["cols_done"], 1)
            for b in range(4):
                for k in (2 * b, 2 * b + 1):
                    for a in range(TT):
                        pe.wait_ge(sem["xn_ready"], a + 1)
                        c0 = (k % 2) * T + a * P
                        last = M.transpose(PS[:, 2 + b, c0:c0 + P], xn[:, a, P * k:P * k + P], ident)
                last.then_inc(sem["xT_done"], 1)

            def full(n):
                pe.wait_ge(unit_full[n % 4], 16 * (n // 4 + 1))

            def modulate(n, bank, c0, part=(0, KC)):
                full(n)
                full(n + 1)
                for k in range(*part):
                    for g in range(4):
                        w = unit(n + g // 2).rearrange("p (k n) -> p k n", k=KC)
                        last = M.matmul(PS[32 * g:32 * g + 32, bank, c0:c0 + T], scr[:, k, :], w[:, k, T * (g % 2):T * (g % 2) + T],
                                        start=(k == 0), stop=(k == KC - 1), tile_position=(0, 32 * g))
                return last

            pe.wait_ge(sem["scr_ready"], 1)
            for v in range(2):
                modulate(2 * v, 1 + 6 * v, 0).then_inc(sem["mod_done"], 1)
                pe.wait_ge(sem["mod_done"], v + 1)
                pe.sem_inc(sem["unit_free"], 2)
            for j in range(4):
                pe.wait_ge(sem["modrow_ready"], j // 2 + 1)
                last = M.transpose(PS[:, 6, P * j:P * j + P], modrow[:, P * j:P * j + P], ident)
            last.then_inc(sem["modcols_done"], 1)

            def tile(i, part=(0, KC)):
                kind, n, c0, j = TILES[i]
                if i == 0:
                    pe.wait_ge(sem["hT_dve"], 4)
                    pe.wait_ge(sem["hT_act"], 4)
                if i >= 4 and part[0] == 0:
                    before = TILES[i - 4][0]
                    if before in BY_VECTOR:
                        pe.wait_ge(sem[before + "_read"], TILES[i - 4][3] + 1)
                    else:
                        pe.wait_ge(sem["tile_read"], reads(i - 3))
                if kind == "mod":
                    last = modulate(n, 4 + i % 4, 0, part)
                elif kind == "R":
                    c = j
                    for h in range(RH):
                        for half in range(2):
                            t = slice(64 * half, 64 * half + 64)
                            o = PS[t, 4 + i % 4, HD * h:HD * h + HD]
                            last = M.matmul(o, BK[:, h, 1, 0, t], VT[:, c, HD * h:HD * h + HD], start=True, stop=(c == 0))
                            if c:
                                last = M.matmul(o, ARz[:, h // 2, h % 2, 0, t], S1[:, h // 2, :], start=False, stop=True)
                else:
                    full(n)
                    k_all = 4 if kind == "yb" else KC
                    steps = range(part[0] * k_all // KC, part[1] * k_all // KC)
                    w = unit(n)[:, 0:k_all * LOADS[n][2]].rearrange("p (k n) -> p k n", k=k_all)
                    for k in steps:
                        if kind == "vm":
                            last = M.matmul(PS[:, 4 + i % 4, :], hT[:, k, P * j:P * j + P], w[:, k, :], start=(k == 0), stop=(k == k_all - 1))
                        else:
                            x = YB if kind == "yb" else hT
                            last = M.matmul(PS[:, 4 + i % 4, 0:T], w[:, k, c0:c0 + P], x[:, k, :], start=(k == 0), stop=(k == k_all - 1))
                if part[1] < KC:
                    return
                last.then_inc(sem["tile_done"], 1)
                if kind != "R" and not any(t[1] == n for t in TILES[i + 1:]):
                    pe.wait_ge(sem["tile_done"], i + 1)
                    pe.sem_inc(sem["unit_free"], 2 if kind == "mod" else 1)

            def begin(name):
                ps, full, free, uses = aux(name)
                if uses:
                    pe.wait_ge(free, uses)
                return ps, full

            def run(i, to):
                for j in range(i, to):
                    tile(j)

            run(0, AFTER_LORA)
            pe.wait_ge(sem["lora_loaded"], 48)
            pe.wait_ge(sem["lora_act"], 1)
            for name, w, x in (("zw", w2, PR[0:64, 12, 1:257]), ("za", a2, PR[64:128, 12, 1:257])):
                ps, done = begin(name)
                for q in range(HP):
                    last = M.matmul(ps[:, T * q:T * q + T], w[:, P * q:P * q + P], x, start=True, stop=True)
                last.then_inc(done, 1)
            run(AFTER_LORA, AFTER_R)
            ps, done = begin("g")
            for q in range(HP):
                last = M.matmul(ps[:, T * q:T * q + T], g2[:, P * q:P * q + P], PR[:, 13, 1:257], start=True, stop=True)
            last.then_inc(done, 1)
            ps, done = begin("kk")
            pe.wait_ge(sem["consts_ready"], 1)
            pe.wait_ge(sem["kk_sq"], 1)
            for h in range(2):
                last = M.matmul(ps[:, 512 * h:512 * h + 512], blk, SQf[:, 512 * h:512 * h + 512], start=True, stop=True)
            last.then_inc(done, 1)
            run(AFTER_R, AFTER_Q)
            ps, done = begin("vt")
            pe.wait_ge(sem["v_shifted"], 1)
            for c in range(TT):
                for q in range(HP):
                    last = M.transpose(ps[:, 512 * c + P * q:512 * c + P * q + P], PR[:, 8 + q, 1 + P * c:1 + P * c + P], ident)
            last.then_inc(done, 1)
            run(AFTER_Q, AFTER_K)
            pe.wait_ge(sem["zeros_ready"], 1)
            pe.wait_ge(sem["tile_read"], reads(tile_at("km", 7) + 1))
            ps, done = begin("s0")
            for h in range(RH):
                last = M.matmul(ps[:, P * place(h):P * place(h) + P], Qz[h % 2][:, h // 2, 0:P], QK[:, 4 + h // 2, 0:P], start=True, stop=True)
            last.then_inc(done, 1)
            for name, h0 in (("s1a", 0), ("s1b", 4)):
                ps, done = begin(name)
                for h in range(h0, h0 + 4):
                    c0 = 512 * (h % 2) + T * ((h - h0) // 2)
                    last = M.matmul(ps[:, c0:c0 + T], Qz[h % 2][:, h // 2, P:T], QK[:, 4 + h // 2, :], start=True, stop=True)
                last.then_inc(done, 1)
            run(AFTER_K, AFTER_V)
            ps, done = begin("tok")
            pe.wait_ge(sem["ar_ready"], 1)
            for i, src in enumerate((Bf, K2f)):
                for q in range(HP):
                    last = M.transpose(ps[:, 512 * i + P * q:512 * i + P * q + P], src[:, T * q:T * q + P], ident)
            last.then_inc(done, 1)
            ps, done = begin("bonus")
            pe.wait_ge(sem["bon_ready"], 1)
            for q in range(HP):
                last = M.matmul(ps[:, T * q:T * q + T], blk, PR[:, q, 1:257], start=True, stop=True)
            last.then_inc(done, 1)
            run(AFTER_V, AFTER_PT)
            pe.wait_ge(sem["att_ready"], 1)
            for b in range(3):
                ps, done = begin(f"pt{b}")
                for h in range(RH):
                    last = M.transpose(ps[:, P * h:P * h + P], att[:, h, P * b:P * b + P], ident)
                last.then_inc(done, 1)
            run(AFTER_PT, AFTER_PV)
            ps, done = begin("pv")
            pe.wait_ge(sem["auxa_free"], AUX.index("pt2") // 2 + 1)
            pe.wait_ge(sem["tile_read"], reads(AFTER_V))
            for h in range(RH):
                r = slice(64 * (h % 2), 64 * (h % 2) + 64)
                c0 = T * (h // 2)
                v = slice(HD * h, HD * h + HD)
                M.matmul(ps[r, c0:c0 + P], VM[:, 0, v], PT[:, 0, place(h), :], start=True, stop=True)
                M.matmul(ps[r, c0 + P:c0 + T], VM[:, 0, v], PT[:, 1, place(h), :], start=True, stop=False)
                last = M.matmul(ps[r, c0 + P:c0 + T], VM[:, 1, v], PT[:, 2, place(h), :], start=False, stop=True)
            last.then_inc(done, 1)
            run(AFTER_PV, AT_CHUNK[0])

            B4 = Bf.rearrange("p (q c t) -> p q c t", q=HP, c=TT)
            K4 = K2f.rearrange("p (q c t) -> p q c t", q=HP, c=TT)
            pe.wait_ge(sem["auxa_free"], 7)
            pe.wait_ge(sem["auxb_free"], 7)
            for c in range(TT):
                at = AT_CHUNK[c]
                half = ((0, KC // 2), (KC // 2, KC))
                if c:
                    pe.wait_ge(sem["y_read"], c)
                    pe.wait_ge(sem["s_read"], c)
                    pe.wait_ge(sem["ar_next"], c)
                for q in range(HP):
                    u = HP * c + q
                    if u:
                        pe.wait_ge(sem["bk_read"], u)
                    for j, src in enumerate((B4, K4)):
                        last = M.matmul(PS[:, j, :], src[:, q, c, :], ARz[:, q].rearrange("p i a t -> p (i a t)"), start=True, stop=True)
                    last.then_inc(sem["bk_full"], 1)
                    if u:
                        pe.wait_ge(sem["x_read"], u)
                    for i in range(2):
                        last = M.matmul(PS[:, 2 + i, 0:P], ARz[:, q, i, 0, :], B4[:, q, c, :], start=True, stop=True)
                    last.then_inc(sem["x_full"], 1)
                    if q < 3:
                        tile(at, ((0, 3), (3, 6), (6, 8))[q])
                pe.wait_ge(sem["bk_read"], HP * (c + 1))
                tile(at + 1)
                pe.wait_ge(sem["x_read"], HP * (c + 1))
                for k in range(1, 7):
                    for g in range(2):
                        if k > 1:
                            pe.wait_ge(sem["level_read"], level_index(c, k - 1, "N", g) + 1)
                        else:
                            pe.wait_ge(sem["n_init"], HP * c + 2 * g + 2)
                        for h in range(4 * g, 4 * g + 4):
                            last = M.matmul(PS[:, 2 * g + 1, P * (h % 4):P * (h % 4) + P], XS[:, h, :], Nm[:, h, :], start=True, stop=True)
                        last.then_inc(sem["level_done"], 1)
                    tile(at + 2 + (k - 1) // 2, half[(k - 1) % 2])
                    if k == 1:
                        pe.wait_ge(sem["m_init"], c + 1)
                    for what in ("NM" if k < 6 else "N"):
                        for g in range(2):
                            pe.wait_ge(sem["level_read"], level_index(c, k, "T", g) + 1)
                            for h in range(4 * g, 4 * g + 4):
                                lhsT, rhs = (TL, Mm) if what == "M" else (Mm, TL)
                                last = M.matmul(PS[:, 2 * g + (what == "N"), P * (h % 4):P * (h % 4) + P], lhsT[:, h, :], rhs[:, h, :],
                                                start=True, stop=True)
                            last.then_inc(sem["level_done"], 1)
                tile(at + 5, half[0])
                pe.wait_ge(sem["level_read"], level_index(c, 6, "N", 1) + 1)
                pe.wait_ge(sem["tile_read"], reads(AT_CHUNK[c] + 2))
                for h in range(RH):
                    v = slice(HD * h, HD * h + HD)
                    for i in range(2):
                        t = slice(64 * i, 64 * i + 64)
                        last = M.matmul(PS[t, 0, v], Nm[:, h, t], Rs[:, v], start=True, stop=True)
                last.then_inc(sem["u_full"], 1)
                tile(at + 5, half[1])
                pe.wait_ge(sem["u_read"], c + 1)
                for h in range(RH):
                    v = slice(HD * h, HD * h + HD)
                    r = slice(64 * (h % 2), 64 * (h % 2) + 64)
                    o = PS[r, 2, P * (h // 2):P * (h // 2) + P]
                    M.matmul(o, Us[:, v], BK[:, h, 0, 1, :], start=True, stop=False)
                    last = M.matmul(o, VT[:, c, v], BK[:, h, 1, 1, :], start=False, stop=(c == 0))
                    if c:
                        last = M.matmul(o, S1[:, h // 2, :], ARz[:, h // 2, h % 2, 1, :], start=False, stop=True)
                last.then_inc(sem["y_full"], 1)
                if c == 0:
                    for h in range(RH):
                        v = slice(HD * h, HD * h + HD)
                        o = PS[64 * (h % 2):64 * (h % 2) + 64, 3, HD * (h // 2):HD * (h // 2) + HD]
                        M.matmul(o, Btok[:, v], Us[:, v], start=True, stop=False)
                        last = M.matmul(o, Ktok[:, v], VT[:, 0, v], start=False, stop=True)
                    last.then_inc(sem["s_full"], 1)
                tile(at + 6)

            pe.wait_ge(sem["y_read"], TT)
            for h in range(2):
                last = M.matmul(PS[:, h, :], blk, YTf[:, 512 * h:512 * h + 512], start=True, stop=True)
            last.then_inc(sem["gn_mean"], 1)
            run(AFTER_CHUNKS, AFTER_CHUNKS + 3)
            pe.wait_ge(sem["gn_c"], 1)
            for h in range(2):
                last = M.matmul(PS[:, 2 + h, :], blk, Bf[:, 512 * h:512 * h + 512], start=True, stop=True)
            last.then_inc(sem["gn_var"], 1)

            run(AFTER_CHUNKS + 3, len(TILES))

            pe.wait_ge(sem["yf_ready"], 1)
            full(U_WA)
            w = unit(U_WA).rearrange("p (k n) -> p k n", k=4)
            for m in range(KC):
                if m >= 4:
                    pe.wait_ge(sem["z_read"], m - 3)
                for q in range(HP):
                    last = M.matmul(PS[:, m % 4, 0:T], w[:, q, P * m:P * m + P], YF[:, q, :], start=(q == 0), stop=(q == HP - 1))
                last.then_inc(sem["z_full"], 1)
            pe.wait_ge(sem["yb_read"], KC)
            for a in range(TT):
                for h in range(2):
                    for k in range(KC):
                        u = U_OUT + k // 4
                        if a == h == 0:
                            if k % 4 == 0:
                                full(u)
                            pe.wait_ge(sem["z_read"], k + 1)
                        w = unit(u).rearrange("p (k n) -> p k n", k=4)
                        last = M.matmul(PS[:, 4 + 2 * a + h, :], zT[:, k, P * a:P * a + P], w[:, k % 4, 512 * h:512 * h + 512],
                                        start=(k == 0), stop=(k == KC - 1))
                    last.then_inc(sem["mix_done"], 1)
            pe.wait_ge(sem["mix_done"], 2 * TT)
            pe.sem_inc(sem["unit_free"], 3)

            pe.wait_ge(sem["router_loaded"], 32)
            for a in range(TT):
                for b in range(2):
                    pe.wait_ge(sem["h2_ready"], 2 * a + b + 1)
                    for k in range(4):
                        last = M.transpose(PS[:, 2 * a + b, P * k:P * k + P], h2[:, a, P * (4 * b + k):P * (4 * b + k) + P], ident)
                    last.then_inc(sem["h2T_full"], 1)
                pe.wait_ge(sem["h2T_read"], 2 * a + 2)
                for i in range(2):
                    t = slice(64 * i, 64 * i + 64)
                    for k in range(KC):
                        last = M.matmul(PS[t, 2 * a, 0:NE], h2T[:, k, P * a + 64 * i:P * a + 64 * i + 64], rw[:, k, :],
                                        start=(k == 0), stop=(k == KC - 1))
                last.then_inc(sem["logits_full"], 1)
            pe.wait_ge(sem["chosen_ready"], 1)
            strict = maskU[:, 0, :]
            M.matmul(PS[:, 1, 0:32], strict, MSK[:, 0, :], start=True, stop=True)
            M.matmul(PS[:, 1, 32:64], ones, MSK[:, 0, :], start=True, stop=False)
            M.matmul(PS[:, 1, 32:64], strict, MSK[:, 1, :], start=False, stop=True)
            M.matmul(PS[:, 1, 64:96], ones, MSK[:, 0, :], start=True, stop=False)
            M.matmul(PS[:, 1, 64:96], ones, MSK[:, 1, :], start=False, stop=True).then_inc(sem["pos_full"], 1)
            pe.wait_ge(sem["comb_ready"], 1)
            for a in range(TT):
                last = M.transpose(PS[0:NE, 2, P * a:P * a + P], COMB[:, a, 0:NE], ident)
            last.then_inc(sem["combT_full"], 1)
            pe.wait_ge(sem["combT_ready"], 1)
            pe.wait_ge(sem["bias_loaded"], 16 * 7)
            for a in range(TT):
                for h in range(2):
                    M.matmul(PS[:, 4 + 2 * a + h, :], combT[:, P * a:P * a + P], bdown[:, 512 * h:512 * h + 512], start=True, stop=True)

            def transpose_weights(b, done):
                for a in range(TT):
                    last = M.transpose(PS[:, 0, P * a:P * a + P], PW[:, b, a, :], ident)
                last.then_inc(sem[done], 1)

            def gather(b, done):
                for k in range(KC):
                    o = PS[:, 1 + k // 4, P * (k % 4):P * (k % 4) + P]
                    for a in range(TT):
                        last = M.matmul(o, h2[:, a, P * k:P * k + P], P1[:, b, a, :], start=(a == 0), stop=(a == TT - 1))
                last.then_inc(sem[done], 1)

            def combine(b, done):
                for a in range(TT):
                    for h in range(2):
                        last = M.matmul(PS[:, 4 + 2 * a + h, :], PWT[:, b, P * a:P * a + P], OUTe[:, 512 * h:512 * h + 512],
                                        start=False, stop=True, skip_group_check=True)
                last.then_inc(sem[done], 1)

            bias_of = {"gate": 0, "up": D}
            FILLS = 16 * 3 * NE // 4

            def project(what, slot, b, k, bank, c0, n, done, steps=range(KC + 1), sel=None):
                w = ring[:, slot, :].rearrange("p (k n) -> p k n", k=KC)
                for s in steps:
                    for h in range(2):
                        o = PS[64 * h:64 * h + 64, bank, 0:n]
                        if s < KC:
                            last = M.matmul(o, xe[:, b, s, 64 * k:64 * k + 64], w[:, s, 512 * h + c0:512 * h + c0 + n],
                                            start=(s == 0), stop=False, tile_position=(0, 64 * h))
                        else:
                            at = bias_of[what] + 512 * h + c0
                            last = M.matmul(o, selb[0:96, sel, :], bias3[0:96, at:at + n], start=False, stop=True, tile_position=(0, 64 * h))
                if done:
                    last.then_inc(sem[done], 1)

            def transpose_hidden(h):
                for q in (2 * h, 2 * h + 1):
                    last = M.transpose(PS[:, 0, P * q:P * q + P], hid[:, P * q:P * q + P], ident)
                return last

            def down(slot, qs, last_done):
                w = ring[:, slot, :].rearrange("p (k n) -> p k n", k=KC)
                for q in qs:
                    for f in range(2):
                        for h in range(2):
                            last = M.matmul(PS[64 * h:64 * h + 64, 3, :], hidT[:, q, 64 * f:64 * f + 64],
                                            w[:, 4 * f + q, 512 * h:512 * h + 512], start=(q == 0 and f == 0), stop=(q == 3 and f == 1),
                                            tile_position=(0, 64 * h))
                if last_done:
                    last.then_inc(sem[last_done], 1)

            pe.wait_ge(sem["prologue"], 1)
            pe.wait_ge(sem["bias_ready"], 1)
            with pe.Fori(0, PAIRS // 2) as i:
                for pp in range(2):
                    p = 2 * i + pp
                    pe.wait_ge(sem["weighted_ready"], p + 1)
                    pe.wait_ge(sem["hidT_read"], 4 * p + 1)
                    transpose_weights(pp, "pt_full")
                    pe.wait_ge(sem["up_read"], 4 * p + 1)
                    gather(pp, "gather_full")
                    pe.wait_ge(sem["gather_read"], p + 1)
                    for k in range(2):
                        e = 2 * p + k
                        m = 3 * (2 * pp + k)
                        fill = lambda j: 16 * (3 * i + j // 4 + 1)
                        pe.wait_ge(w_full[m % 4], fill(m))
                        if k:
                            pe.wait_ge(sem["hidT_read"], 4 * p + 3)
                        pe.wait_ge(sem["sel_ready"], e + 1)
                        project("gate", m % 4, pp, k, 0, 0, 512, "gate_done", sel=k)
                        if k == 0:
                            pe.wait_ge(sem["out_read"], 2 * p + 1)
                            pe.wait_ge(sem["out_read_b"], 2 * p + 1)
                            combine(1 - pp, "combined")
                        pe.wait_ge(w_full[(m + 1) % 4], fill(m + 1))
                        if k:
                            pe.wait_ge(sem["up_read"], 4 * p + 3)
                        project("up", (m + 1) % 4, pp, k, 1, 0, T, "up_half_done", sel=k)
                        project("up", (m + 1) % 4, pp, k, 2, T, T, None, steps=range(0, 6), sel=k)
                        pe.wait_ge(sem["hid_ready"], 2 * e + 1)
                        transpose_hidden(0).then_inc(sem["hidT_full"], 1)
                        project("up", (m + 1) % 4, pp, k, 2, T, T, "up_done", steps=range(6, KC + 1), sel=k)
                        pe.wait_ge(w_full[(m + 2) % 4], fill(m + 2))
                        pe.wait_ge(sem["hidT_read"], 2 * e + 2)
                        if k:
                            pe.wait_ge(sem["out_read"], e + 1)
                            pe.wait_ge(sem["out_read_b"], e + 1)
                        down((m + 2) % 4, (0, 1), None)
                        pe.wait_ge(sem["hid_ready"], 2 * e + 2)
                        transpose_hidden(1).then_inc(sem["hidT_full"], 1)
                        pe.wait_ge(sem["hidT_read"], 2 * e + 3)
                        down((m + 2) % 4, (2, 3), "down_done")
            pe.wait_ge(sem["out_read"], NE + 1)
            pe.wait_ge(sem["out_read_b"], NE + 1)
            combine(1, "combined")

            turns = pe.value_load(N_TURNS[0:1, 0:1], min_val=0, max_val=MAX_TURNS)
            with pe.If(turns > 0):
                with pe.Fori(0, turns) as c:
                    pe.wait_ge(sem["ov_onehot"], c + 1)
                    transpose_weights(0, "ov_weights")
                    gather(0, "ov_gather")
                    pe.wait_ge(sem["ov_copied"], c + 1)
                    pe.wait_ge(sem["ov_sel"], c + 1)
                    pe.wait_ge(w_full[0], FILLS + 16 * (c + 1))
                    project("gate", 0, 0, 0, 0, 0, 512, "ov_gate", sel=0)
                    pe.wait_ge(w_full[1], FILLS + 16 * (c + 1))
                    project("up", 1, 0, 0, 1, 0, T, None, sel=0)
                    project("up", 1, 0, 0, 2, T, T, "ov_up", sel=0)
                    pe.wait_ge(sem["ov_hid"], c + 1)
                    transpose_hidden(0)
                    transpose_hidden(1).then_inc(sem["ov_hidT"], 1)
                    pe.wait_ge(w_full[2], FILLS + 16 * (c + 1))
                    pe.wait_ge(sem["ov_hidTc"], c + 1)
                    down(2, (0, 1, 2, 3), "ov_down")
                    pe.wait_ge(sem["ov_out"], c + 1)
                    combine(0, "ov_comb")
                    pe.wait_ge(sem["ov_comb"], c + 1)
            pe.wait_ge(sem["combined"], PAIRS + 1)
            pe.sem_inc(sem["y_ready"], 1)


_INS = ["x", "c", "w_ada", "b_ada", "norm1_g", "w_in", "rwkv_mu", "rwkv_w0", "rwkv_w2", "rwkv_a0", "rwkv_a2",
        "rwkv_g2", "rwkv_k_k", "rwkv_k_a", "rwkv_r_k", "rwkv_ln_w", "rwkv_ln_b", "w_branch_a", "w_branch_b",
        "w_out", "norm2_g", "router_w", "router_b", "exp_w_gate", "exp_b_gate", "exp_w_up", "exp_b_up",
        "exp_w_down", "exp_b_down", "normf_g"]


def kernel(**inputs):
    import concourse.bacc as bacc
    import numpy as np
    from concourse.bass_utils import run_bass_kernel_spmd

    nc = bacc.Bacc("TRN2", target_bir_lowering=False, num_devices=1)
    arrays, aps = {}, {}
    for name in _INS:
        a = np.ascontiguousarray(inputs[name])
        arrays[f"in_{name}"] = a
        aps[name] = nc.dram_tensor(f"in_{name}", a.shape, mybir.dt.from_np(a.dtype), kind="ExternalInput").ap()
    out = nc.dram_tensor("out_0", (1, T, D), F32, kind="ExternalOutput").ap()
    scratch = nc.dram_tensor("mod_rows", (8, 512), F32, kind="Internal").ap()
    block_kernel(nc, aps, out, scratch)
    r = run_bass_kernel_spmd(nc, [arrays], core_ids=[0])
    return r.results[0]["out_0"]
```

```python
from contextlib import ExitStack, contextmanager

import concourse.bass as bass
from concourse import mybir

F32 = mybir.dt.float32
BF16 = mybir.dt.bfloat16
I32 = mybir.dt.int32
U32 = mybir.dt.uint32
ALU = mybir.AluOpType
ACT = mybir.ActivationFunctionType
AX_X = mybir.AxisListType.X

P = 128
D = 1024
T = 256
TT = T // P
KC = D // P
HD = 64
RH = 8
HP = RH // 2
W = RH * HD
NE = 32
TOPK = 4
SLOTS = 64
PAIRS = NE // 2
MORE = T // SLOTS - 1
MAX_TURNS = T * TOPK // SLOTS
LIMIT = 7.0
ALPHA = 1.702
RMS_EPS = 1e-5
GN_EPS = 64e-5
NEG = -1e30
LAM = 0.6065306597126334
SCALE = HD ** -0.5
MID = HD - 1

VECS = [("c", 8), ("norm1_g", 8), ("rwkv_mu", 14), ("rwkv_w0", 4), ("rwkv_a0", 4), ("rwkv_k_k", 4),
        ("rwkv_k_a", 4), ("rwkv_r_k", 4), ("rwkv_ln_w", 4), ("rwkv_ln_b", 4)]
NVEC = sum(n for _, n in VECS)

LOADS = [("ada", 512 * c, 512) for c in range(4)]
LOADS += [("lora", 3 * W, 256), ("k", W, 512), ("r", 0, 512), ("v", 2 * W, 512), ("q", 1792, 512), ("km", 2304, 512), ("vm", 2816, 512)]
for _i, (_kind, _c) in enumerate((("ga", 3328), ("ga", 3840), ("gb", 4352), ("gb", 4864))):
    LOADS += [(_kind, _c, 512)] + [("ada", 2048 + 1024 * _i + 512 * _j, 512) for _j in range(2)]
LOADS += [("wb", 0, D), ("wa", 0, D), ("out", 0, D), ("out", 512, D)]
U_WB, U_WA, U_OUT, N_UNITS = (len(LOADS) - _n for _n in (4, 3, 2, 0))
TILES = []
_next = dict(r=0, k=4, v=8, lora=12, q=0, km=4, ga=0, gb=8, mod=0)
for _u in range(4, U_WB):
    _kind, _c0, _w = LOADS[_u]
    if _kind == "vm":
        TILES += [("vm", _u, 0, c) for c in range(TT)]
    elif _kind == "ada":
        if LOADS[_u - 1][0] == "ada":
            TILES.append(("mod", _u - 1, 0, _next["mod"]))
            _next["mod"] += 1
    else:
        TILES += [(_kind, _u, 128 * j, _next[_kind] + j) for j in range(_w // 128)]
        _next[_kind] += _w // 128
TILES += [("yb", U_WB, 128 * m, m) for m in range(KC)]
AT_CHUNK = (32, 39)
for _c, _i in enumerate(AT_CHUNK):
    TILES.insert(_i + 1, ("R", None, 0, _c))
AFTER_CHUNKS = AT_CHUNK[1] + 7
AFTER_LORA, AFTER_R, AFTER_Q, AFTER_K, AFTER_V, AFTER_PT, AFTER_PV = 10, 12, 18, 23, 24, 30, 31
BY_VECTOR = ("mod", "yb")


def tile_at(kind, j):
    return [n for n, t in enumerate(TILES) if t[0] == kind and t[3] == j][0]


def reads(i, by_vector=False):
    return sum((t[0] in BY_VECTOR) == by_vector for t in TILES[:i])


def place(h):
    return (h % 2) * HP + h // 2


def level_index(c, k, what, g):
    return c * 34 + (k - 1) * 6 + {"T": 0, "N": 2, "M": 4}[what] + g


def block_kernel(nc, A, out, scratch):
    ctx = ExitStack()
    with ctx:
        def sb(name, n, dt=F32, parts=P):
            return ctx.enter_context(nc.sbuf_tensor(name, [parts, n], dt))

        ring = ctx.enter_context(nc.sbuf_tensor("ring", [P, 4, KC * D], F32))
        PS = ctx.enter_context(nc.psum_tensor("PS", [P, 8, 512], F32))

        lmask_t = sb("lmask_t", 1024)
        lmask = lmask_t[:, 0:896].rearrange("p (k t) -> p k t", k=7)
        lmask0L = lmask_t[:, 896:1024]
        ident_t = sb("ident_t", 128)
        blk_t = sb("blk_t", 128)
        ones_t = sb("ones_t", 128)
        ident, blk, ones = ident_t[:, :], blk_t[:, :], ones_t[:, :]
        maskU_t = sb("maskU_t", 256)
        maskU = maskU_t[:, :].rearrange("p (a t) -> p a t", a=2)
        maskL = sb("maskL", 128)[:, :]
        negmask = sb("negmask", 128)[:, :]
        iota64 = sb("iota64", 64)[:, :]
        iota32 = sb("iota32", 32)[:, :]
        x_sb = sb("x_sb", TT * D)
        x3 = x_sb[:, :].rearrange("p (a d) -> p a d", a=TT)
        colrows = sb("colrows", 128)
        cols = sb("cols", 64)
        scr = sb("scr", KC * 32)[:, :].rearrange("p (k m) -> p k m", k=KC)
        modrow = sb("modrow", 1536)
        hT_t = sb("hT_t", KC * T)
        hT = hT_t[:, :].rearrange("p (k t) -> p k t", k=KC)
        PR_t = sb("PR_t", 14 * 257)
        PR = PR_t[:, :].rearrange("p (j t) -> p j t", j=14)
        QK_t = sb("QK_t", 8 * T)
        QK = QK_t[:, :].rearrange("p (j t) -> p j t", j=8)
        VM_t = sb("VM_t", TT * 512)
        VM = VM_t[:, :].rearrange("p (a d) -> p a d", a=TT)
        GAB_t = sb("GAB_t", 16 * T)
        GAB = GAB_t[:, :].rearrange("p (j t) -> p j t", j=16)
        WG = sb("WG", 1024)
        rw = sb("rw", KC * NE)[:, :].rearrange("p (k e) -> p k e", k=KC)
        rbias = sb("rbias", NE)[:, :]
        small = sb("small", 96)
        eye3 = sb("eye3", 32)
        selb_t = sb("selb", 2 * SLOTS, BF16)
        selb = selb_t[:, :].rearrange("p (b s) -> p b s", b=2)

        sh1c, s1c, sigc = small[:, 0:8], small[:, 8:16], small[:, 16:24]
        ss, rstd = small[:, 24:26], small[:, 26:28]
        decay_end = small[:, 28:32]
        mx, sums = small[:, 32:48], small[:, 48:64]
        eps_gn, eps_rms = small[:, 64:65], small[:, 65:66]
        ss2, rstd2, ss3, rstd3 = small[:, 66:68], small[:, 68:70], small[:, 70:72], small[:, 72:74]
        dsum = small[:, 76:80]
        ss2half = small[:, 80:84].rearrange("p (a h) -> p a h", a=TT)
        off, v = {}, 0
        for name, n in VECS:
            off[name] = v
            v += n

        def col(name, j, n=1):
            return cols[:, off[name] + j:off[name] + j + n]

        def over(ap, n):
            return ap.unsqueeze(2).broadcast_to([ap.shape[0], ap.shape[1], n])

        def unit(u):
            return ring[:, (u % 4) // 2, (u % 2) * 4096:(u % 2) * 4096 + 4096]

        TMP = ring[:, 2:4, :].rearrange("p a n -> p (a n)")
        heads = lambda a: a.rearrange("p (h t) -> p h t", h=RH)
        pairs = lambda a: a.rearrange("p (q t) -> p q t", q=HP)
        XS, Nm, Mm = (heads(TMP[:, 1024 * i:1024 * i + 1024]) for i in range(3))
        BK = TMP[:, 3072:7168].rearrange("p (h j a t) -> p h j a t", h=RH, j=2, a=2)
        TL = BK[:, :, 0, 0, :]
        ARz = TMP[:, 7168:9216].rearrange("p (q i a t) -> p q i a t", q=HP, i=2, a=2)
        Bf, K2f, SIGf, Af, KKf, Gf, VTf = (TMP[:, 9216 + 1024 * i:10240 + 1024 * i] for i in range(7))
        VT = VTf.rearrange("p (c d) -> p c d", c=TT)
        Rs, Us = KKf[:, 0:512], KKf[:, 512:1024]
        AR1 = SIGf.rearrange("p (q a t) -> p q a t", q=HP, a=2)
        S1 = modrow[:, 0:256].rearrange("p (q d) -> p q d", q=HP)
        YTf = Af
        bada0 = TMP[:, 0:512]
        xn = TMP[:, 7168:9216].rearrange("p (a d) -> p a d", a=TT)
        same = TMP[:, 2048:3072].rearrange("p (k t) -> p k t", k=8)
        Cf, Ccf, E1f, E2f, DIFf, NRMf, SQf = (TMP[:, 1024 * i:1024 * i + 1024] for i in range(7))
        att = TMP[:, 0:3072].rearrange("p (h t) -> p h t", h=RH)
        PT = TMP[:, 3072:6144].rearrange("p (b h t) -> p b h t", b=3, h=RH)
        w2, a2, g2 = WG[:, 0:512], TMP[:, 512:1024], WG[:, 512:1024]
        Btok, Ktok = WG[:, 0:512], WG[:, 512:1024]
        YB = QK[:, 0:4, :]
        Qz = (QK[:, 0:4, :], GAB[:, 8:12, :])
        gate1b = QK_t[:, 1024:2048]
        scale2b, shift2b = VM_t[:, :], WG[:, :]
        modrest = modrow[:, 512:1536].rearrange("p (v n) -> p v n", v=4)
        YF = PR[:, 0:4, 1:257]
        BON = PR[:, 4:8, 1:257]
        norm2b = PR_t[:, 2056:3080]
        zT = GAB[:, 0:8, :]

        h2 = hT_t[:, :].rearrange("p (a d) -> p a d", a=TT)
        h2T = GAB_t[:, 0:2048].rearrange("p (k t) -> p k t", k=KC)
        gate2b, normfb = GAB_t[:, 0:1024], GAB_t[:, 1024:2048]
        xe = GAB_t[:, 2048:4096].rearrange("p (b k s) -> p b k s", b=2, k=KC)
        biasraw = GAB_t[0:96, 2048:4096]
        bias3 = norm2b.bitcast(BF16)
        bdown, gate2r = GAB_t[96:128, 3072:4096], GAB_t[96:128, 2048:3072]
        OUTe = PR_t[:, 0:1024]
        t1, u_sb, sg, hid = PR_t[:, 1024:1536], PR_t[:, 1536:2048], WG[:, 0:512], WG[:, 512:1024]
        hidT = PR_t[:, 3080:3592].rearrange("p (q s) -> p q s", q=4)
        L2, M8 = QK_t[:, 0:64].rearrange("p (a e) -> p a e", a=2), QK_t[:, 64:80].rearrange("p (a e) -> p a e", a=2)
        IX = QK_t[:, 80:96].bitcast(U32).rearrange("p (a e) -> p a e", a=2)
        IXF, EX = (QK_t[:, o:o + 8].rearrange("p (a e) -> p a e", a=2) for o in (96, 104))
        SM = QK_t[:, 112:114]
        OH = QK_t[:, 128:384].rearrange("p (a k e) -> p a k e", a=2, k=TOPK)
        MSK = QK_t[:, 384:448].rearrange("p (a e) -> p a e", a=2)
        COMB, POS = (QK_t[:, o:o + 68].rearrange("p (a e) -> p a e", a=2) for o in (448, 516))
        CNT = QK_t[:, 584:616]
        P1 = QK_t[:, 656:1168].rearrange("p (b a s) -> p b a s", b=2, a=TT)
        PW = QK_t[:, 1168:1680].rearrange("p (b a s) -> p b a s", b=2, a=TT)
        TAKEN = QK_t[:, 1680:1776].rearrange("p (t e) -> p t e", t=MORE)
        TURNSF, TURNS = QK_t[:, 1776:1809], QK_t[:, 1812:1845].bitcast(I32)
        xeF = modrow[:, 256:768].rearrange("p (k s) -> p k s", k=KC)
        P1F, PWF = (modrow[:, o:o + 256].rearrange("p (a s) -> p a s", a=TT) for o in (768, 1024))
        PWTF, OUTF = modrow[:, 1280:1536], lmask_t[:, 0:1024]
        PWT = VM_t[:, 0:512].rearrange("p (b t) -> p b t", b=2)

        sem = {}
        for n in """consts_ready x_loaded vecs_loaded bada_loaded lora_loaded router_loaded
                    ident_ready zeros_ready gate_folded comb_cleared bias_part bias_rest cum_ready ar_next
                    cols_done cols_ready sigc_ready scr_ready ss_ready rms_ready xn_ready xT_done hT_dve hT_act
                    mod_done modrow_ready modcols_done modcols_read
                    tile_done tile_read lora_shifted lora_act kk_sq decays
                    v_shifted ar_ready bon_ready att_centred att_exp att_ready yb_ready
                    auxa_full auxa_free auxb_full auxb_free
                    x_full x_read bk_full bk_read n_init m_init level_done level_read
                    u_full u_read y_full y_read s_full s_read
                    gn_mean gn_c gn_var gn_std yf_ready
                    bada_rest_loaded mod_read yb_read scratch_written mod_bcast norm2_loaded
                    z_full z_read mix_done ss2_ready rms2_ready h2_ready h2T_full h2T_read
                    logits_full top_ready top_exp scale2_ready chosen_ready comb_ready pos_full combT_full combT_ready bias_loaded late_loaded
                    pool_chain dve_chain act_chain
                    gathering_ready weighted_ready pt_full pt_read gather_full gather_read out_read combined sel_ready
                    gate_done up_half_done up_done down_done t1_ready sg_ready up_read hid_ready hidT_full hidT_read
                    prologue turns_listed
                    ov_onehot ov_gather ov_copied ov_gate ov_t1 ov_sg ov_up ov_hid ov_hidT ov_hidTc ov_down
                    ov_out ov_comb ov_place ov_gathering ov_uread
                    y_ready y_copied ss3_ready rms3_ready result_ready result_stored""".split():
            sem[n] = ctx.enter_context(nc.semaphore(n))
        unit_full = [ctx.enter_context(nc.semaphore(f"unit_full{i}")) for i in range(4)]
        down_half = [ctx.enter_context(nc.semaphore(f"down_half{i}")) for i in range(2)]
        w_full = [ctx.enter_context(nc.semaphore(f"w_full{i}")) for i in range(4)]

        AUX = ["zw", "za", "g", "kk", "vt", "s0", "s1a", "s1b", "tok", "bonus", "pt0", "pt1", "pt2", "pv"]

        def aux(name):
            n = AUX.index(name)
            full, free = ("auxa_full", "auxa_free") if n % 2 == 0 else ("auxb_full", "auxb_free")
            b = 0 if n % 2 == 0 else 2
            return PS[:, b:b + 2, :].rearrange("p a n -> p (a n)"), sem[full], sem[free], n // 2

        @contextmanager
        def further_turns(engine, e):
            engine.wait_ge(sem["turns_listed"], 1)
            first = engine.value_load(TURNS[0:1, bass.ds(e, 1)], min_val=1, max_val=MAX_TURNS)
            end = engine.value_load(TURNS[0:1, bass.ds(e + 1, 1)], min_val=1, max_val=MAX_TURNS)
            with engine.If(end > first):
                with engine.Fori(first, end) as c:
                    yield c

        block = ctx.enter_context(nc.Block())

        @block.sync
        def _(sp):
            def wait_multiplied(u):
                if u < 4:
                    sp.wait_ge(sem["mod_done"], u // 2 + 1)
                elif u < U_WA:
                    last = [i for i, (kind, n, _, _) in enumerate(TILES) if u in ((n, n + 1) if kind == "mod" else (n,))][-1]
                    sp.wait_ge(sem["tile_done"], last + 1)
                elif u == U_WA:
                    sp.wait_ge(sem["z_full"], KC)
                else:
                    sp.wait_ge(sem["mix_done"], 2 * TT)

            def load_unit(u):
                if u >= 4:
                    wait_multiplied(u - 4)
                kind, c0, w = LOADS[u]
                name = dict(ada="w_ada", wa="w_branch_a", wb="w_branch_b", out="w_out").get(kind, "w_in")
                src = A[name][c0:c0 + 512, :] if w == D else A[name][:, c0:c0 + w]
                k = src.shape[0] // P
                sp.dma_start(unit(u)[:, 0:k * w].rearrange("p (k n) -> p k n", k=k),
                             src.rearrange("(k p) n -> p k n", p=P)).then_inc(unit_full[u % 4], 16)

            load_unit(0)
            row = 0
            for name, n in VECS:
                src = A[name]
                if name == "c":
                    src = src[0]
                elif name == "rwkv_r_k":
                    src = src.rearrange("h n -> (h n)")
                sp.dma_start(colrows[row:row + n, :], src.rearrange("(a b) -> a b", b=P)).then_inc(sem["vecs_loaded"], 16)
                row += n
            load_unit(1)
            sp.dma_start(x3[:, :, :], A["x"][0].rearrange("(a p) d -> p a d", p=P)).then_inc(sem["x_loaded"], 16)
            load_unit(2)
            load_unit(3)
            bias = A["b_ada"].rearrange("(v g n) -> g v n", v=6, g=4)
            for g in range(4):
                sp.dma_start(bada0[32 * g:32 * g + 32, :].rearrange("p (v n) -> p v n", v=2),
                             bias[g:g + 1, 0:2, :].broadcast_to([32, 2, 256])).then_inc(sem["bada_loaded"], 16)
            load_unit(4)
            load_unit(5)
            sp.dma_start(w2[0:64], A["rwkv_w2"]).then_inc(sem["lora_loaded"], 16)
            sp.dma_start(a2[64:128], A["rwkv_a2"]).then_inc(sem["lora_loaded"], 16)
            sp.dma_start(g2, A["rwkv_g2"]).then_inc(sem["lora_loaded"], 16)
            sp.dma_start(rw, A["router_w"].rearrange("(k p) e -> p k e", p=P)).then_inc(sem["router_loaded"], 16)
            sp.dma_start(rbias, A["router_b"].rearrange("(a e) -> a e", a=1).broadcast_to([P, NE])).then_inc(sem["router_loaded"], 16)
            for g in range(4):
                sp.dma_start(modrest[32 * g:32 * g + 32, :, :], bias[g:g + 1, 2:6, :].broadcast_to([32, 4, 256])).then_inc(sem["bada_rest_loaded"], 16)
            for u in range(6, N_UNITS):
                load_unit(u)

            WEIGHTS = [A["exp_w_gate"], A["exp_w_up"], A["exp_w_down"]]
            DONE = [sem["gate_done"], sem["up_done"], sem["down_done"]]

            def load_matrix(e, kind, slot, odd):
                dst = ring[:, slot, :].rearrange("p (k n) -> p k n", k=KC)
                src = WEIGHTS[kind][bass.ds(e, 1), :, :].rearrange("a (k p) n -> p (a k) n", p=P)
                if kind == 2:
                    sp.dma_start(dst[:, 0:4, :], src[:, 0:4, :]).then_inc(down_half[odd], 16)
                    sp.dma_start(dst[:, 4:8, :], src[:, 4:8, :]).then_inc(w_full[slot], 16)
                else:
                    sp.dma_start(dst, src).then_inc(w_full[slot], 16)

            sp.wait_ge(sem["yf_ready"], 1)
            load_matrix(0, 2, 2, 0)
            load_matrix(1, 0, 3, 1)
            for u in (U_WB, U_WA, U_OUT + 1):
                wait_multiplied(u)
            load_matrix(0, 0, 0, 0)
            load_matrix(0, 1, 1, 0)
            FURTHER = [sem["ov_gate"], sem["ov_up"], sem["ov_down"]]
            turns = [None]

            def wait_used(e, kind):
                if kind == 0:
                    turns[0] = sp.value_load(TURNS[0:1, bass.ds(e + 1, 1)], min_val=1, max_val=MAX_TURNS)
                sp.wait_ge(DONE[kind], e + 1)
                sp.wait_ge(FURTHER[kind], turns[0])

            sp.wait_ge(sem["turns_listed"], 1)
            with sp.Fori(0, 7) as i:
                for q in range(4, 16):
                    wait_used(4 * i + (q - 4) // 3, (q - 4) % 3)
                    load_matrix(4 * i + q // 3, q % 3, q % 4, q // 3 % 2)
            for m in range(88, 96):
                wait_used((m - 4) // 3, (m - 4) % 3)
                load_matrix(m // 3, m % 3, m % 4, m // 3 % 2)

            sp.wait_ge(sem["result_ready"], 1)
            sp.dma_start(out[0, 0:P, :], x3[:, 0, :]).then_inc(sem["result_stored"], 16)
            sp.wait_ge(sem["result_ready"], 2)
            sp.dma_start(out[0, P:T, :], x3[:, 1, :]).then_inc(sem["result_stored"], 16)
            sp.wait_ge(sem["result_stored"], 32)

        @block.gpsimd
        def _(pool):
            n = [0]

            def link(ins):
                n[0] += 1
                ins.then_inc(sem["pool_chain"], 1)
                pool.wait_ge(sem["pool_chain"], n[0])

            link(nc.gpsimd.memset(ident, 1.0))
            link(nc.gpsimd.affine_select(out=ident, in_=ident, compare_op=ALU.is_equal, fill=0.0, base=0,
                                         pattern=[[-1, P]], channel_multiplier=1))
            pool.sem_inc(sem["ident_ready"], 1)
            link(nc.gpsimd.memset(ones, 1.0))
            link(nc.gpsimd.memset(QK_t[64:128, 0:1024], 0.0))
            link(nc.gpsimd.memset(GAB_t[0:64, 2048:3072], 0.0))
            link(nc.gpsimd.memset(WG[64:128, 0:512], 0.0))
            link(nc.gpsimd.memset(a2[0:64], 0.0))
            link(nc.gpsimd.memset(same, 1.0))
            for i in range(7):
                b = 1 << i
                v = same[:, i, :].rearrange("p (n b) -> p n b", b=b)
                link(nc.gpsimd.affine_select(out=v, in_=v, compare_op=ALU.is_ge, fill=0.0, base=0,
                                             pattern=[[-b, P // b], [0, b]], channel_multiplier=1))
                link(nc.gpsimd.affine_select(out=v, in_=v, compare_op=ALU.is_ge, fill=0.0, base=b - 1,
                                             pattern=[[b, P // b], [0, b]], channel_multiplier=-1))
            link(nc.gpsimd.tensor_copy(blk, same[:, 6, :]))
            for m, base, f, p in ((maskU[:, 0, :], -1, 1, -1), (maskU[:, 1, :], 0, 1, -1), (maskL, -1, -1, 1)):
                link(nc.gpsimd.affine_select(out=m, in_=ones, compare_op=ALU.is_ge, fill=0.0, base=base,
                                             pattern=[[f, P]], channel_multiplier=p))
            link(nc.gpsimd.memset(negmask, 0.0))
            link(nc.gpsimd.affine_select(out=negmask, in_=negmask, compare_op=ALU.is_ge, fill=NEG, base=0,
                                         pattern=[[-1, P]], channel_multiplier=1))
            link(nc.gpsimd.tensor_tensor(lmask, same[:, 1:8, :], same[:, 0:7, :], ALU.subtract))
            link(nc.gpsimd.tensor_tensor(lmask0L, lmask[:, 0, :], maskL, ALU.mult))
            link(nc.gpsimd.tensor_tensor(lmask, lmask, maskU[:, 0:1, :].broadcast_to([P, 7, P]), ALU.mult))
            link(nc.gpsimd.iota(iota64, pattern=[[1, 64]], base=0, channel_multiplier=0,
                                allow_small_or_imprecise_dtypes=True))
            link(nc.gpsimd.iota(iota32, pattern=[[1, 32]], base=0, channel_multiplier=0,
                                allow_small_or_imprecise_dtypes=True))
            pool.sem_inc(sem["consts_ready"], 1)

            pool.wait_ge(sem["xT_done"], 4)
            link(nc.gpsimd.memset(ARz[0:64, :, 1, :, :], 0.0))
            nc.gpsimd.memset(ARz[64:128, :, 0, :, :], 0.0).then_inc(sem["zeros_ready"], 1)
            pool.wait_ge(sem["zeros_ready"], 1)

            pool.wait_ge(sem["auxa_free"], AUX.index("g") // 2 + 1)
            pool.wait_ge(sem["auxb_free"], AUX.index("bonus") // 2 + 1)
            b4 = lambda name: over(col(name, 0, 4), T)
            link(nc.gpsimd.tensor_tensor(BON, BON, b4("rwkv_ln_b"), ALU.add))
            link(nc.gpsimd.tensor_tensor(BON, BON, pairs(Gf), ALU.mult))
            nc.gpsimd.tensor_tensor(pairs(Gf), pairs(Gf), b4("rwkv_ln_w"), ALU.mult).then_inc(sem["gate_folded"], 1)

            for c in range(TT):
                for q in range(HP):
                    hs = slice(2 * q, 2 * q + 2)
                    pool.wait_ge(sem["bk_read"], HP * c + q + 1)
                    if c and q == 0:
                        pool.wait_ge(sem["u_full"], 1)
                    link(nc.gpsimd.tensor_tensor(Nm[:, hs, :], BK[:, hs, 0, 0, :], lmask[:, 0:1, :].broadcast_to([P, 2, P]), ALU.mult))
                    nc.gpsimd.tensor_tensor(Nm[:, hs, :], Nm[:, hs, :], ident.unsqueeze(1).broadcast_to([P, 2, P]), ALU.add).then_inc(sem["n_init"], 1)
                if c == 0:
                    pool.wait_ge(sem["x_full"], HP)
                    link(nc.gpsimd.tensor_copy(ARz[0:64, :, 0], AR1[0:64]))
                    nc.gpsimd.tensor_copy(ARz[64:128, :, 1], AR1[64:128]).then_inc(sem["ar_next"], 1)
                    pool.wait_ge(sem["ar_next"], 1)

            pool.wait_ge(sem["mod_read"], 4)
            pool.dma_start(scratch.rearrange("a n -> (a n)").rearrange("(v g n) -> g v n", v=4, g=4), modrest[0:P:32, :, :]).then_inc(sem["scratch_written"], 16)
            pool.wait_ge(sem["scratch_written"], 16)
            pool.wait_ge(sem["s_full"], 1)
            pool.wait_ge(sem["auxb_full"], AUX.index("pv") // 2 + 1)
            for dst, r in ((gate1b, 0), (shift2b, 2), (scale2b, 4)):
                src = scratch[r:r + 2, :].rearrange("(o a) n -> o (a n)", o=1)
                pool.dma_start(dst, src.broadcast_to([P, D])).then_inc(sem["mod_bcast"], 16)
            pool.wait_ge(sem["auxb_free"], AUX.index("bonus") // 2 + 1)
            pool.dma_start(norm2b, A["norm2_g"].rearrange("(a n) -> a n", a=1).broadcast_to([P, D])).then_inc(sem["norm2_loaded"], 16)
            pool.wait_ge(sem["y_read"], TT)
            pool.wait_ge(sem["scratch_written"], 16)
            nc.gpsimd.memset(modrow[:, :], 0.0).then_inc(sem["comb_cleared"], 1)
            pool.wait_ge(sem["z_read"], KC)
            for j in range(3):
                rows = slice(32 * j, 32 * j + 32)
                pool.dma_start(biasraw[rows, 0:D], A["exp_b_gate"]).then_inc(sem["bias_loaded"], 16)
                pool.dma_start(biasraw[rows, D:2 * D], A["exp_b_up"]).then_inc(sem["bias_loaded"], 16)
            pool.dma_start(bdown, A["exp_b_down"]).then_inc(sem["bias_loaded"], 16)
            pool.dma_start(gate2r, scratch[6:8, :].rearrange("(o a) n -> o (a n)", o=1).broadcast_to([NE, D])).then_inc(sem["bias_loaded"], 16)
            for j in range(3):
                link(nc.gpsimd.tensor_copy(eye3[32 * j:32 * j + 32, :], ident[0:32, 0:32]))
            for n, rows in enumerate((slice(0, 96), slice(64, 96))):
                pool.wait_ge(sem["bias_part"], (1, 3)[n])
                nc.gpsimd.tensor_tensor(biasraw[rows], biasraw[rows], bias3[rows], ALU.subtract).then_inc(sem["bias_rest"], 1)
                pool.wait_ge(sem["bias_rest"], n + 1)
            def select(k, e):
                nc.gpsimd.tensor_copy(selb[0:96, k, :], eye3[0:96, bass.ds(e, 1)].broadcast_to([96, SLOTS])).then_inc(sem["sel_ready"], 1)

            for k in range(2):
                select(k, k)
            pool.wait_ge(sem["logits_full"], TT)
            pool.dma_start(gate2b, scratch[6:8, :].rearrange("(o a) n -> o (a n)", o=1).broadcast_to([P, D])).then_inc(sem["late_loaded"], 16)
            pool.dma_start(normfb, A["normf_g"].rearrange("(a n) -> a n", a=1).broadcast_to([P, D])).then_inc(sem["late_loaded"], 16)
            with pool.Fori(1, PAIRS) as p:
                for k in range(2):
                    if k == 0:
                        pool.wait_ge(sem["gather_full"], p + 1)
                    select(k, 2 * p + k)

        @block.scalar
        def _(act):
            n = [0]

            def link(ins):
                n[0] += 1
                ins.then_inc(sem["act_chain"], 1)
                act.wait_ge(sem["act_chain"], n[0])

            act.wait_ge(sem["cols_ready"], 1)
            nc.scalar.activation(sigc, col("c", 0, 8), ACT.Sigmoid).then_inc(sem["sigc_ready"], 1)
            act.wait_ge(sem["ss_ready"], 1)
            nc.scalar.activation(rstd, ss, ACT.Sqrt).then_inc(sem["rms_ready"], 1)

            act.wait_ge(sem["modcols_read"], 1)
            for k in range(4, KC):
                act.wait_ge(sem["xT_done"], k // 2 + 1)
                nc.scalar.activation(hT[:, k, :], PS[:, 2 + k // 2, (k % 2) * T:(k % 2) * T + T], ACT.Identity,
                                     bias=sh1c[:, k:k + 1], scale=s1c[:, k:k + 1]).then_inc(sem["hT_act"], 1)

            def read_tiles(a, b):
                for i in range(a, b):
                    kind, u, c0, j = TILES[i]
                    src = PS[:, 4 + i % 4, 0:T]
                    if kind in BY_VECTOR:
                        continue
                    act.wait_ge(sem["tile_done"], i + 1)
                    if kind in ("r", "k", "v", "lora"):
                        dst, f = PR[:, j, 1:257], ACT.Copy
                    elif kind == "q":
                        nc.scalar.activation(Qz[0][0:64, j, :], src[0:64], ACT.Copy)
                        src, dst, f = src[64:128], Qz[1][64:128, j, :], ACT.Copy
                    elif kind == "km":
                        dst, f = QK[:, j, :], ACT.Copy
                    elif kind == "vm":
                        src, dst, f = PS[:, 4 + i % 4, :], VM[:, j, :], ACT.Copy
                    elif kind == "R":
                        src, dst, f = PS[:, 4 + i % 4, :], Rs, ACT.Copy
                    else:
                        dst, f = GAB[:, j, :], ACT.Sigmoid
                    nc.scalar.activation(dst, src, f).then_inc(sem["tile_read"], 1)

            def read_aux(name, dst, f=ACT.Copy, biases=None, **kw):
                ps, full, free, uses = aux(name)
                act.wait_ge(full, uses + 1)
                if biases is None:
                    last = nc.scalar.activation(dst, ps, f, **kw)
                else:
                    for q in range(HP):
                        last = nc.scalar.activation(dst[:, T * q:T * q + T], ps[:, T * q:T * q + T], f, bias=biases(q))
                last.then_inc(free, 1)

            read_tiles(0, 6)
            act.wait_ge(sem["lora_shifted"], 1)
            nc.scalar.activation(PR[0:64, 12, 1:257], PR[0:64, 12, 1:257], ACT.Tanh)
            nc.scalar.activation(PR[:, 13, 1:257], PR[:, 13, 1:257], ACT.Sigmoid).then_inc(sem["lora_act"], 1)
            read_tiles(6, AFTER_LORA)
            read_aux("zw", SIGf, ACT.Sigmoid, lambda q: col("rwkv_w0", q))
            read_aux("za", Af, ACT.Sigmoid, lambda q: col("rwkv_a0", q))
            read_tiles(AFTER_LORA, AFTER_R)
            read_aux("g", Gf)
            read_aux("kk", NRMf, ACT.Sqrt)
            act.wait_ge(sem["cum_ready"], 1)
            nc.scalar.activation(E1f, Ccf, ACT.Exp, scale=-LAM)
            nc.scalar.activation(DIFf, DIFf, ACT.Exp, scale=-LAM)
            nc.scalar.activation(decay_end, dsum, ACT.Exp, scale=-LAM)
            nc.scalar.activation(E2f, Ccf, ACT.Exp, scale=LAM).then_inc(sem["decays"], 1)
            read_tiles(AFTER_R, AFTER_Q)
            read_aux("vt", VTf)
            read_tiles(AFTER_Q, AFTER_V)
            read_aux("tok", WG[:, :])
            read_tiles(AFTER_V, AFTER_V + 3)
            act.wait_ge(sem["att_centred"], 1)
            nc.scalar.activation(att, att, ACT.Exp, scale=SCALE).then_inc(sem["att_exp"], 1)
            read_tiles(AFTER_V + 3, AFTER_PT)
            for b in range(3):
                read_aux(f"pt{b}", PT[:, b].rearrange("p h t -> p (h t)"))
            read_tiles(AFTER_PT, AFTER_PV)
            read_aux("pv", QK_t[:, 0:1024])
            read_tiles(AFTER_PV, AT_CHUNK[0])
            for c in range(TT):
                read_tiles(AT_CHUNK[c], AT_CHUNK[c] + 5)
                act.wait_ge(sem["u_full"], c + 1)
                nc.scalar.activation(Us, PS[:, 0, :], ACT.Copy).then_inc(sem["u_read"], 1)
                read_tiles(AT_CHUNK[c] + 5, AT_CHUNK[c] + 6)
                act.wait_ge(sem["y_full"], c + 1)
                nc.scalar.activation(YTf.rearrange("p (q t) -> p q t", q=HP)[:, :, P * c:P * c + P],
                                     PS[:, 2, :].rearrange("p (q t) -> p q t", q=HP), ACT.Copy).then_inc(sem["y_read"], 1)
                read_tiles(AT_CHUNK[c] + 6, AT_CHUNK[c] + 7)
            act.wait_ge(sem["gn_var"], 1)
            nc.scalar.activation(SIGf, PS[:, 2:4, :].rearrange("p a n -> p (a n)"), ACT.Sqrt, bias=eps_gn, scale=1.0 / HD).then_inc(sem["gn_std"], 1)

            def take(rows):
                nc.scalar.activation(bias3[rows], biasraw[rows], ACT.Copy).then_inc(sem["bias_part"], 1)

            act.wait_ge(sem["bias_loaded"], 16 * 8)
            act.wait_ge(sem["scale2_ready"], 1)
            take(slice(0, 96))
            for a in range(TT):
                act.wait_ge(sem["ss2_ready"], a + 1)
                nc.scalar.activation(rstd2[:, a:a + 1], ss2[:, a:a + 1], ACT.Sqrt).then_inc(sem["rms2_ready"], 1)
                if a == 0:
                    act.wait_ge(sem["bias_rest"], 1)
                    take(slice(32, 64))
                    take(slice(64, 96))
                for b in range(2):
                    act.wait_ge(sem["h2T_full"], 2 * a + b + 1)
                    nc.scalar.activation(h2T[:, 4 * b:4 * b + 4, P * a:P * a + P], PS[:, 2 * a + b, :].rearrange("p (k t) -> p k t", k=4), ACT.Copy).then_inc(sem["h2T_read"], 1)
            act.wait_ge(sem["bias_rest"], 2)
            take(slice(64, 96))
            act.wait_ge(sem["top_ready"], 1)
            nc.scalar.activation(EX, EX, ACT.Exp).then_inc(sem["top_exp"], 1)
            act.wait_ge(sem["prologue"], 1)
            act.wait_ge(sem["combT_full"], 1)
            nc.scalar.activation(PWT[0:NE, 1, :], PS[0:NE, 2, 0:T], ACT.Copy).then_inc(sem["combT_ready"], 1)

            act.sem_inc(sem["hidT_read"], 1)
            with act.Fori(0, PAIRS // 2) as i:
                for pp in range(2):
                    p = 2 * i + pp
                    act.wait_ge(sem["pt_full"], p + 1)
                    nc.scalar.activation(PWT[:, pp, :], PS[:, 0, 0:T], ACT.Copy).then_inc(sem["pt_read"], 1)
                    act.wait_ge(sem["gather_full"], p + 1)
                    nc.scalar.activation(xe[:, pp].rearrange("p k s -> p (k s)"), PS[:, 1:3, :].rearrange("p a n -> p (a n)"), ACT.Copy).then_inc(sem["gather_read"], 1)
                    for k in range(2):
                        e = 2 * p + k
                        act.wait_ge(sem["t1_ready"], e + 1)
                        nc.scalar.activation(sg, t1, ACT.Sigmoid, scale=ALPHA).then_inc(sem["sg_ready"], 1)
                        for h in range(2):
                            act.wait_ge(sem["hidT_full"], 2 * e + h + 1)
                            nc.scalar.activation(hidT[:, 2 * h:2 * h + 2, :].rearrange("p q s -> p (q s)"),
                                                 PS[:, 0, T * h:T * h + T], ACT.Copy).then_inc(sem["hidT_read"], 1)
                        with further_turns(act, e) as c:
                            act.wait_ge(sem["ov_gather"], c)
                            nc.scalar.activation(PWTF, PS[:, 0, 0:T], ACT.Copy)
                            nc.scalar.activation(xeF, PS[:, 1:3, :].rearrange("p b (k t) -> p (b k) t", t=P)[:, :, 0:SLOTS], ACT.Copy).then_inc(sem["ov_copied"], 1)
                            act.wait_ge(sem["ov_t1"], c)
                            nc.scalar.activation(sg, t1, ACT.Sigmoid, scale=ALPHA).then_inc(sem["ov_sg"], 1)
                            act.wait_ge(sem["ov_hidT"], c)
                            nc.scalar.activation(hidT.rearrange("p q s -> p (q s)"), PS[:, 0, :], ACT.Copy).then_inc(sem["ov_hidTc"], 1)
            for a in range(TT):
                act.wait_ge(sem["y_ready"], a + 1)
                nc.scalar.activation(x3[:, a, :], PS[:, 4 + 2 * a:6 + 2 * a, :].rearrange("p h n -> p (h n)"), ACT.Copy).then_inc(sem["y_copied"], 1)
            for a in range(TT):
                act.wait_ge(sem["ss3_ready"], a + 1)
                nc.scalar.activation(rstd3[:, a:a + 1], ss3[:, a:a + 1], ACT.Sqrt).then_inc(sem["rms3_ready"], 1)

        @block.vector
        def _(dve):
            n = [0]
            V = nc.vector

            def link(ins):
                n[0] += 1
                ins.then_inc(sem["dve_chain"], 1)
                dve.wait_ge(sem["dve_chain"], n[0])

            b4 = lambda name: over(col(name, 0, 4), T)

            def read_tiles(a, b):
                for i in range(a, b):
                    kind, _, _, j = TILES[i]
                    if kind in BY_VECTOR:
                        dve.wait_ge(sem["tile_done"], i + 1)
                    if kind == "mod":
                        V.tensor_tensor(modrest[:, j, :], PS[:, 4 + i % 4, 0:T], modrest[:, j, :], ALU.add).then_inc(sem["mod_read"], 1)
                    elif kind == "yb":
                        dve.wait_ge(sem["tile_read"], reads(tile_at("gb", 8 + j) + 1))
                        V.tensor_tensor(GAB[:, 8 + j, :], PS[:, 4 + i % 4, 0:T], GAB[:, 8 + j, :], ALU.mult).then_inc(sem["yb_read"], 1)

            r4, k4, v4 = PR[:, 0:4, 1:257], PR[:, 4:8, 1:257], PR[:, 8:12, 1:257]

            V.memset(PR[:, :, 0:1], 0.0)
            V.memset(eps_gn, GN_EPS)

            dve.wait_ge(sem["cols_done"], 1)
            V.tensor_copy(cols[:, 0:NVEC], PS[:, 0, 0:NVEC]).then_inc(sem["cols_ready"], 1)
            dve.wait_ge(sem["cols_ready"], 1)
            dve.wait_ge(sem["sigc_ready"], 1)
            V.tensor_tensor(scr, over(col("c", 0, 8), 32), over(sigc, 32), ALU.mult).then_inc(sem["scr_ready"], 1)
            dve.wait_ge(sem["x_loaded"], 16)
            for a in range(TT):
                link(V.tensor_tensor_reduce(out=xn[:, a, :], in0=x3[:, a, :], in1=x3[:, a, :], scale=1.0, scalar=0.0,
                                            op0=ALU.mult, op1=ALU.add, accum_out=ss[:, a:a + 1]))
            V.tensor_scalar(ss, ss, 1.0 / D, RMS_EPS, ALU.mult, ALU.add).then_inc(sem["ss_ready"], 1)
            dve.wait_ge(sem["rms_ready"], 1)
            link(V.reciprocal(rstd, rstd))
            for a in range(TT):
                V.tensor_scalar(xn[:, a, :], x3[:, a, :], rstd[:, a:a + 1], None, ALU.mult).then_inc(sem["xn_ready"], 1)
            dve.wait_ge(sem["bada_loaded"], 64)
            for v in range(2):
                dve.wait_ge(sem["mod_done"], v + 1)
                V.tensor_tensor(modrow[:, T * v:T * v + T], PS[:, 1 + 6 * v, 0:T], bada0[:, T * v:T * v + T], ALU.add).then_inc(sem["modrow_ready"], 1)
            dve.wait_ge(sem["modcols_done"], 1)
            turned = PS[:, 6, :].rearrange("p (v j g r) -> p v g j r", v=2, j=2, r=32)
            V.tensor_copy(sh1c.rearrange("p (g j) -> p g j", j=2), turned[:, 0, :, :, 0])
            V.scalar_tensor_tensor(out=s1c.rearrange("p (g j) -> p g j", j=2), in0=turned[:, 1, :, :, 0], scalar=1.0,
                                   in1=col("norm1_g", 0, 8).rearrange("p (g j) -> p g j", j=2),
                                   op0=ALU.add, op1=ALU.mult).then_inc(sem["modcols_read"], 1)
            dve.wait_ge(sem["modcols_read"], 1)
            for k in range(4):
                dve.wait_ge(sem["xT_done"], k // 2 + 1)
                V.tensor_scalar(hT[:, k, :], PS[:, 2 + k // 2, (k % 2) * T:(k % 2) * T + T], s1c[:, k:k + 1],
                                sh1c[:, k:k + 1], ALU.mult, ALU.add).then_inc(sem["hT_dve"], 1)

            def shift(j0, nj, signal=None):
                dif = VTf[:, 0:T * nj].rearrange("p (j t) -> p j t", j=nj)
                link(V.tensor_tensor(dif, PR[:, j0:j0 + nj, 0:T], PR[:, j0:j0 + nj, 1:257], ALU.subtract))
                for j in range(nj):
                    ins = V.scalar_tensor_tensor(out=PR[:, j0 + j, 1:257], in0=dif[:, j, :], scalar=col("rwkv_mu", j0 + j),
                                                 in1=PR[:, j0 + j, 1:257], op0=ALU.mult, op1=ALU.add)
                if signal:
                    ins.then_inc(sem[signal], 1)
                else:
                    link(ins)

            dve.wait_ge(sem["tile_read"], 2)
            shift(12, 2, "lora_shifted")
            dve.wait_ge(sem["lora_shifted"], 1)
            dve.wait_ge(sem["tile_read"], 6)
            shift(4, 4)
            link(V.tensor_tensor(pairs(KKf), k4, b4("rwkv_k_k"), ALU.mult))
            V.tensor_tensor(SQf, KKf, KKf, ALU.mult).then_inc(sem["kk_sq"], 1)
            dve.wait_ge(sem["tile_read"], 10)
            shift(0, 4)
            dve.wait_ge(sem["consts_ready"], 1)
            dve.wait_ge(sem["auxa_free"], 1)
            dve.wait_ge(sem["auxb_free"], 1)
            for q in range(2 * HP):
                last = V.tensor_tensor_scan(Cf[:, P * q:P * q + P], ones, SIGf[:, P * q:P * q + P], 0.0, ALU.mult, ALU.add)
            link(last)
            C8 = Cf.rearrange("p (j t) -> p j t", t=P)
            link(V.tensor_tensor(Ccf.rearrange("p (j t) -> p j t", t=P), C8,
                                 C8[:, :, MID:MID + 1].broadcast_to([P, 2 * HP, P]), ALU.subtract))
            C4 = Ccf.rearrange("p (q c t) -> p q c t", q=HP, c=TT)
            R4 = Cf.rearrange("p (q c t) -> p q c t", q=HP, c=TT)
            V.tensor_tensor(dsum.unsqueeze(2), C4[:, :, 0, P - 1:P], R4[:, :, 1, MID:MID + 1], ALU.add)
            V.tensor_tensor(DIFf, Ccf, SIGf, ALU.subtract).then_inc(sem["cum_ready"], 1)
            link(V.scalar_tensor_tensor(out=pairs(VTf), in0=pairs(Af), scalar=-1.0, in1=b4("rwkv_k_a"), op0=ALU.add, op1=ALU.mult))
            link(V.scalar_tensor_tensor(out=k4, in0=pairs(VTf), scalar=1.0, in1=k4, op0=ALU.add, op1=ALU.mult))
            dve.wait_ge(sem["auxb_free"], 2)
            link(V.tensor_scalar(NRMf, NRMf, 1e-12, None, ALU.max))
            link(V.reciprocal(NRMf, NRMf))
            link(V.tensor_tensor(KKf, KKf, NRMf, ALU.mult))
            link(V.tensor_tensor(Bf, KKf, Af, ALU.mult))
            dve.wait_ge(sem["tile_read"], 14)
            shift(8, 4, "v_shifted")
            dve.wait_ge(sem["decays"], 1)
            c4 = lambda a: a.rearrange("p (q c t) -> p q c t", q=HP, c=TT)
            for c, rows, dst in ((0, slice(0, 64), ARz[:, :, 0]), (0, slice(64, 128), ARz[:, :, 1]), (1, slice(0, P), AR1)):
                V.tensor_tensor(dst[rows, :, 1, :], PR[rows, 0:4, 1 + P * c:1 + P * c + P], c4(E1f)[rows, :, c, :], ALU.mult)
                V.scalar_tensor_tensor(out=dst[rows, :, 0, :], in0=c4(KKf)[rows, :, c, :], scalar=-1.0, in1=c4(DIFf)[rows, :, c, :],
                                       op0=ALU.mult, op1=ALU.mult)
            V.tensor_tensor(pairs(K2f), k4, pairs(E2f), ALU.mult)
            V.tensor_tensor(Bf, Bf, E2f, ALU.mult).then_inc(sem["ar_ready"], 1)
            dve.wait_ge(sem["ar_ready"], 1)
            link(V.tensor_tensor(r4, r4, k4, ALU.mult))
            V.tensor_tensor(r4, r4, b4("rwkv_r_k"), ALU.mult).then_inc(sem["bon_ready"], 1)

            ps, full, free, uses = aux("s0")
            dve.wait_ge(full, uses + 1)
            V.tensor_tensor(att[:, :, 0:P], heads(ps), negmask.unsqueeze(1).broadcast_to([P, RH, P]), ALU.add).then_inc(free, 1)
            for name, h0 in (("s1a", 0), ("s1b", 4)):
                ps, full, free, uses = aux(name)
                s = ps.rearrange("p (i q t) -> p i q t", i=2, q=2)
                dst = att.rearrange("p (i q) t -> p i q t", i=2)[:, :, h0 // 2:h0 // 2 + 2, :]
                dve.wait_ge(full, uses + 1)
                V.tensor_copy(dst[:, :, :, P:2 * P], s[:, :, :, 0:P])
                for i in range(2):
                    last = V.tensor_tensor(dst[:, i, :, 2 * P:3 * P], s[:, i, :, P:T], negmask.unsqueeze(1).broadcast_to([P, 2, P]), ALU.add)
                last.then_inc(free, 1)
            dve.wait_ge(sem["auxb_free"], 4)
            dve.wait_ge(sem["auxa_free"], 4)
            parts = ((att[:, :, 0:P], 0, P), (att[:, :, P:3 * P], RH, 2 * P))
            for a, m, w in parts:
                last = V.tensor_reduce(mx[:, m:m + RH], a, AX_X, ALU.max)
            link(last)
            for a, m, w in parts:
                last = V.tensor_tensor(a, a, over(mx[:, m:m + RH], w), ALU.subtract)
            last.then_inc(sem["att_centred"], 1)
            ps, full, free, uses = aux("bonus")
            dve.wait_ge(full, uses + 1)
            V.tensor_tensor(BON, pairs(ps), v4, ALU.mult).then_inc(free, 1)
            dve.wait_ge(sem["att_exp"], 1)
            for a, m, w in parts:
                last = V.tensor_reduce(sums[:, m:m + RH], a, AX_X, ALU.add)
            link(last)
            link(V.reciprocal(sums, sums))
            for a, m, w in parts:
                last = V.tensor_tensor(a, a, over(sums[:, m:m + RH], w), ALU.mult)
            last.then_inc(sem["att_ready"], 1)
            dve.wait_ge(sem["bada_rest_loaded"], 64)
            read_tiles(0, AT_CHUNK[0])

            steps = 0
            for c in range(TT):
                for q in range(HP):
                    u = HP * c + q
                    dve.wait_ge(sem["bk_full"], u + 1)
                    V.tensor_tensor(BK[:, 2 * q:2 * q + 2].rearrange("p i j a t -> p i j (a t)"),
                                    PS[:, 0:2, :].rearrange("p j (i t) -> p i j t", i=2),
                                    maskU_t[:, :].unsqueeze(1).unsqueeze(1).broadcast_to([P, 2, 2, T]), ALU.mult).then_inc(sem["bk_read"], 1)
                    dve.wait_ge(sem["x_full"], u + 1)
                    V.tensor_tensor(XS[:, 2 * q:2 * q + 2, :], PS[:, 2:4, 0:P],
                                    maskL.unsqueeze(1).broadcast_to([P, 2, P]), ALU.mult).then_inc(sem["x_read"], 1)
                read_tiles(AT_CHUNK[c], AT_CHUNK[c] + 1)
                dve.wait_ge(sem["x_read"], HP * (c + 1))
                link(V.tensor_tensor(Mm, XS, lmask0L.unsqueeze(1).broadcast_to([P, RH, P]), ALU.mult))
                V.tensor_tensor(Mm, Mm, ident.unsqueeze(1).broadcast_to([P, RH, P]), ALU.add).then_inc(sem["m_init"], 1)
                dve.wait_ge(sem["n_init"], HP * (c + 1))
                for k in range(1, 7):
                    seq = [(w, g) for w in ("TNM" if k < 6 else "TN") for g in range(2)]
                    for what, g in seq:
                        if what == "N" and g == 0 and k % 2 == 0:
                            read_tiles(AT_CHUNK[c] + k // 2 + 1, AT_CHUNK[c] + k // 2 + 2)
                        assert steps == level_index(c, k, what, g)
                        dve.wait_ge(sem["level_done"], steps + 1)
                        hs = slice(4 * g, 4 * g + 4)
                        ps = PS[:, 2 * g + (what != "M"), :].rearrange("p (h t) -> p h t", h=4)
                        if what == "T":
                            ins = V.tensor_tensor(TL[:, hs, :], ps, lmask[:, k:k + 1, :].broadcast_to([P, 4, P]), ALU.mult)
                        else:
                            m = Mm if what == "M" else Nm
                            ins = V.tensor_tensor(m[:, hs, :], m[:, hs, :], ps, ALU.add)
                        ins.then_inc(sem["level_read"], 1)
                        steps += 1
                read_tiles(AT_CHUNK[c] + 5, AT_CHUNK[c] + 6)
                if c == 0:
                    dve.wait_ge(sem["s_full"], 1)
                    V.tensor_tensor(S1, PS[:, 3, 0:T].rearrange("p (q d) -> p q d", q=HP), over(decay_end, HD), ALU.mult).then_inc(sem["s_read"], 1)
                read_tiles(AT_CHUNK[c] + 6, AT_CHUNK[c] + 7)

            dve.wait_ge(sem["gn_mean"], 1)
            YC, SQ2 = KKf, Bf
            link(V.scalar_tensor_tensor(out=YC, in0=PS[:, 0:2, :].rearrange("p a n -> p (a n)"), scalar=-1.0 / HD, in1=YTf,
                                        op0=ALU.mult, op1=ALU.add))
            link(V.tensor_tensor(SQ2, YC, YC, ALU.mult))
            dve.sem_inc(sem["gn_c"], 1)
            dve.wait_ge(sem["gate_folded"], 1)
            link(V.tensor_tensor(YC, YC, Gf, ALU.mult))
            read_tiles(AFTER_CHUNKS, AFTER_CHUNKS + 2)
            dve.wait_ge(sem["gn_std"], 1)
            link(V.reciprocal(SIGf, SIGf))
            read_tiles(AFTER_CHUNKS + 2, AFTER_CHUNKS + 4)
            link(V.tensor_tensor(YC, YC, SIGf, ALU.mult))
            V.tensor_tensor(YF, pairs(YC), BON, ALU.add).then_inc(sem["yf_ready"], 1)
            read_tiles(AFTER_CHUNKS + 4, len(TILES))

            za = PR_t[:, 1028:1540].rearrange("p (i t) -> p i t", i=2)
            dve.wait_ge(sem["yf_ready"], 1)
            dve.wait_ge(sem["yb_read"], KC)
            for m in range(KC):
                dve.wait_ge(sem["z_full"], m + 1)
                link(V.tensor_tensor(za[:, m % 2, :], PS[:, m % 4, 0:T], GAB[:, m, :], ALU.mult))
                V.tensor_tensor(zT[:, m, :], za[:, m % 2, :], GAB[:, 8 + m, :], ALU.add).then_inc(sem["z_read"], 1)

            dve.wait_ge(sem["mod_bcast"], 48)
            dve.wait_ge(sem["norm2_loaded"], 16)
            dve.wait_ge(sem["z_read"], KC)
            V.scalar_tensor_tensor(out=scale2b, in0=scale2b, scalar=1.0, in1=norm2b, op0=ALU.add, op1=ALU.mult).then_inc(sem["scale2_ready"], 1)
            dve.wait_ge(sem["scale2_ready"], 1)
            mixed = PR_t[:, 0:2048].rearrange("p (a d) -> p a d", a=TT)
            for a in range(TT):
                for h in range(2):
                    s = slice(512 * h, 512 * h + 512)
                    dve.wait_ge(sem["mix_done"], 2 * a + h + 1)
                    link(V.tensor_tensor(mixed[:, a, s], PS[:, 4 + 2 * a + h, :], gate1b[:, s], ALU.mult))
                    link(V.tensor_tensor(x3[:, a, s], x3[:, a, s], mixed[:, a, s], ALU.add))
                    link(V.tensor_tensor_reduce(out=mixed[:, a, s], in0=x3[:, a, s], in1=x3[:, a, s], scale=1.0, scalar=0.0,
                                                op0=ALU.mult, op1=ALU.add, accum_out=ss2half[:, a, h:h + 1]))
                link(V.tensor_tensor(ss2[:, a:a + 1], ss2half[:, a, 0:1], ss2half[:, a, 1:2], ALU.add))
                V.tensor_scalar(ss2[:, a:a + 1], ss2[:, a:a + 1], 1.0 / D, RMS_EPS, ALU.mult, ALU.add).then_inc(sem["ss2_ready"], 1)
                V.tensor_tensor(h2[:, a, :], x3[:, a, :], scale2b, ALU.mult)
                dve.wait_ge(sem["rms2_ready"], a + 1)
                link(V.reciprocal(rstd2[:, a:a + 1], rstd2[:, a:a + 1]))
                for h in range(2):
                    s = slice(512 * h, 512 * h + 512)
                    V.scalar_tensor_tensor(out=h2[:, a, s], in0=h2[:, a, s], scalar=rstd2[:, a:a + 1], in1=shift2b[:, s],
                                           op0=ALU.mult, op1=ALU.add).then_inc(sem["h2_ready"], 1)
            dve.wait_ge(sem["h2_ready"], 2 * TT)

            V.memset(COMB, 0.0)
            V.memset(POS, 0.0)
            V.memset(PWT[:, 1, :], 0.0)
            link(V.memset(OUTe, 0.0))
            dve.wait_ge(sem["bias_loaded"], 16 * 8)
            V.tensor_tensor(OUTe[0:NE, :], bdown, gate2r, ALU.mult).then_inc(sem["prologue"], 1)
            dve.wait_ge(sem["prologue"], 1)
            dve.wait_ge(sem["router_loaded"], 32)
            for a in range(TT):
                dve.wait_ge(sem["logits_full"], a + 1)
                link(V.tensor_tensor(L2[:, a, :], PS[:, 2 * a, 0:NE], rbias, ALU.add))
                link(V.max(M8[:, a, :], L2[:, a, :]))
                link(V.max_index(IX[:, a, :], M8[:, a, :], L2[:, a, :]))
            V.tensor_copy(IXF, IX[:, :, 0:TOPK])
            V.tensor_tensor(EX, M8[:, :, 0:TOPK], M8[:, :, 0:1].broadcast_to([P, 2, TOPK]), ALU.subtract).then_inc(sem["top_ready"], 1)
            dve.wait_ge(sem["top_ready"], 1)
            for a in range(TT):
                last = V.tensor_tensor(OH[:, a], iota32.unsqueeze(1).broadcast_to([P, TOPK, NE]), over(IXF[:, a, :], NE), ALU.is_equal)
            link(last)
            V.tensor_reduce(MSK, OH.rearrange("p a k e -> p a e k"), AX_X, ALU.add).then_inc(sem["chosen_ready"], 1)
            dve.wait_ge(sem["top_exp"], 1)
            link(V.tensor_reduce(SM, EX, AX_X, ALU.add))
            link(V.reciprocal(SM, SM))
            link(V.tensor_tensor(EX, EX, over(SM, TOPK), ALU.mult))
            for a in range(TT):
                last = V.tensor_tensor(OH[:, a], OH[:, a], over(EX[:, a, :], NE), ALU.mult)
            link(last)
            V.tensor_reduce(COMB[:, :, 0:NE], OH.rearrange("p a k e -> p a e k"), AX_X, ALU.add).then_inc(sem["comb_ready"], 1)
            dve.wait_ge(sem["pos_full"], 1)
            link(V.scalar_tensor_tensor(out=POS[:, :, 0:NE], in0=PS[:, 1, 0:64].rearrange("p (a e) -> p a e", a=2), scalar=1.0,
                                        in1=MSK, op0=ALU.add, op1=ALU.mult))
            link(V.tensor_scalar(POS, POS, -1.0, None, ALU.add))
            V.tensor_copy(CNT, PS[:, 1, 64:96])

            def one_hot(b, p):
                pos = POS[:, :, bass.ds(2 * p, 2)].unsqueeze(3).broadcast_to([P, TT, 2, SLOTS])
                comb = COMB[:, :, bass.ds(2 * p, 2)].unsqueeze(3).broadcast_to([P, TT, 2, SLOTS])
                gathering = P1[:, b].rearrange("p a (k s) -> p a k s", k=2)
                weighted = PW[:, b].rearrange("p a (k s) -> p a k s", k=2)
                for a in range(TT):
                    last = V.tensor_tensor(gathering[:, a], iota64.unsqueeze(1).broadcast_to([P, 2, SLOTS]), pos[:, a], ALU.is_equal)
                last.then_inc(sem["gathering_ready"], 1)
                dve.wait_ge(sem["gathering_ready"], p + 1)
                for a in range(TT):
                    last = V.tensor_tensor(weighted[:, a], gathering[:, a], comb[:, a], ALU.mult)
                last.then_inc(sem["weighted_ready"], 1)

            def gated_out(dst):
                V.tensor_tensor(dst[:, 0:512], PS[0:64, 3, :], gate2b[0:64, 0:512], ALU.mult)
                return V.tensor_tensor(dst[:, 512:1024], PS[64:128, 3, :], gate2b[64:128, 512:1024], ALU.mult)

            one_hot(0, 0)
            dve.sem_inc(sem["up_read"], 1)
            dve.sem_inc(sem["out_read"], 1)

            for t in range(MORE):
                last = V.tensor_scalar(TAKEN[:, t, :], CNT, float(SLOTS * (t + 1)), None, ALU.is_gt)
            link(last)
            link(V.tensor_reduce(CNT, TAKEN.rearrange("p t e -> p e t"), AX_X, ALU.add))
            link(V.memset(TURNSF[:, 0:1], 0.0))
            link(V.tensor_tensor_scan(TURNSF[:, 1:NE + 1], ones[:, 0:NE], CNT, 0.0, ALU.mult, ALU.add))
            link(V.tensor_scalar(TURNSF, TURNSF, 1.0, None, ALU.add))
            V.tensor_copy(TURNS, TURNSF).then_inc(sem["turns_listed"], 1)
            with dve.Fori(0, PAIRS // 2) as i:
                for pp in range(2):
                    p = 2 * i + pp
                    for k in range(2):
                        e = 2 * p + k
                        dve.wait_ge(sem["gate_done"], e + 1)
                        V.tensor_scalar(t1, PS[:, 0, :], LIMIT, None, ALU.min).then_inc(sem["t1_ready"], 1)
                        dve.wait_ge(sem["sg_ready"], e + 1)
                        V.tensor_tensor(t1, t1, sg, ALU.mult)
                        for h in range(2):
                            s = slice(T * h, T * h + T)
                            dve.wait_ge(sem["up_done" if h else "up_half_done"], e + 1)
                            V.tensor_scalar(u_sb[:, s], PS[:, 1 + h, 0:T], LIMIT, -LIMIT, ALU.min, ALU.max).then_inc(sem["up_read"], 1)
                            dve.wait_ge(sem["up_read"], 2 * e + h + 2)
                            V.scalar_tensor_tensor(out=hid[:, s], in0=u_sb[:, s], scalar=1.0, in1=t1[:, s],
                                                   op0=ALU.add, op1=ALU.mult).then_inc(sem["hid_ready"], 1)
                        if k == 1:
                            one_hot(1 - pp, p + 1)
                        dve.wait_ge(sem["down_done"], e + 1)
                        if pp == k == 0:
                            dve.wait_ge(sem["late_loaded"], 32)
                        gated_out(OUTe[64 * k:64 * k + 64, :]).then_inc(sem["out_read"], 1)
                        with further_turns(dve, e) as c:
                            V.tensor_scalar(POS[:, :, bass.ds(e, 1)], POS[:, :, bass.ds(e, 1)], -float(SLOTS), None, ALU.add).then_inc(sem["ov_place"], 1)
                            dve.wait_ge(sem["ov_place"], c)
                            for a in range(TT):
                                last = V.tensor_tensor(P1F[:, a, 0:SLOTS], iota64, POS[:, a, bass.ds(e, 1)].broadcast_to([P, SLOTS]), ALU.is_equal)
                            last.then_inc(sem["ov_gathering"], 1)
                            dve.wait_ge(sem["ov_gathering"], c)
                            for a in range(TT):
                                last = V.tensor_tensor(PWF[:, a, 0:SLOTS], P1F[:, a, 0:SLOTS], COMB[:, a, bass.ds(e, 1)].broadcast_to([P, SLOTS]), ALU.mult)
                            last.then_inc(sem["ov_onehot"], 1)
                            dve.wait_ge(sem["ov_gate"], c + 1)
                            V.tensor_scalar(t1, PS[:, 0, :], LIMIT, None, ALU.min).then_inc(sem["ov_t1"], 1)
                            dve.wait_ge(sem["ov_sg"], c)
                            V.tensor_tensor(t1, t1, sg, ALU.mult)
                            dve.wait_ge(sem["ov_up"], c + 1)
                            V.tensor_scalar(u_sb.rearrange("p (h n) -> p h n", h=2), PS[:, 1:3, 0:T], LIMIT, -LIMIT, ALU.min, ALU.max).then_inc(sem["ov_uread"], 1)
                            dve.wait_ge(sem["ov_uread"], c)
                            V.scalar_tensor_tensor(out=hid, in0=u_sb, scalar=1.0, in1=t1, op0=ALU.add, op1=ALU.mult).then_inc(sem["ov_hid"], 1)
                            dve.wait_ge(sem["ov_down"], c + 1)
                            gated_out(OUTF[0:64, :]).then_inc(sem["ov_out"], 1)

            gy = GAB_t[:, 2048:4096].rearrange("p (a d) -> p a d", a=TT)
            for a in range(TT):
                dve.wait_ge(sem["y_copied"], a + 1)
                link(V.tensor_tensor_reduce(out=gy[:, a, :], in0=x3[:, a, :], in1=x3[:, a, :], scale=1.0, scalar=0.0,
                                            op0=ALU.mult, op1=ALU.add, accum_out=ss3[:, a:a + 1]))
                V.tensor_scalar(ss3[:, a:a + 1], ss3[:, a:a + 1], 1.0 / D, RMS_EPS, ALU.mult, ALU.add).then_inc(sem["ss3_ready"], 1)
            for a in range(TT):
                dve.wait_ge(sem["rms3_ready"], a + 1)
                link(V.reciprocal(rstd3[:, a:a + 1], rstd3[:, a:a + 1]))
                V.scalar_tensor_tensor(out=x3[:, a, :], in0=x3[:, a, :], scalar=rstd3[:, a:a + 1], in1=normfb,
                                       op0=ALU.mult, op1=ALU.mult).then_inc(sem["result_ready"], 1)

        @block.tensor
        def _(pe):
            M = nc.tensor

            def keep_warm(n, bank):
                for _ in range(n):
                    M.matmul(PS[:, bank, 0:P], ident, ident, start=True, stop=True)

            pe.wait_ge(sem["ident_ready"], 1)
            pe.wait_ge(sem["vecs_loaded"], 16 * len(VECS))
            M.transpose(PS[:, 0, 0:NVEC], colrows[0:NVEC, :], ident[0:NVEC, 0:NVEC]).then_inc(sem["cols_done"], 1)
            def full(n):
                pe.wait_ge(unit_full[n % 4], 16 * (n // 4 + 1))

            def modulate(n, bank, c0, part=(0, KC)):
                for step in range(2 * part[0], 2 * part[1]):
                    i, k = step // KC, step % KC
                    if k == 0:
                        full(n + i)
                    w = unit(n + i).rearrange("p (k n) -> p k n", k=KC)
                    for g in (2 * i, 2 * i + 1):
                        last = M.matmul(PS[32 * g:32 * g + 32, bank, c0:c0 + T], scr[:, k, :], w[:, k, T * (g % 2):T * (g % 2) + T],
                                        start=(k == 0), stop=(k == KC - 1), tile_position=(0, 32 * g))
                return last

            pe.wait_ge(sem["scr_ready"], 1)
            for v in range(2):
                modulate(2 * v, 1 + 6 * v, 0).then_inc(sem["mod_done"], 1)
                for b in range(4 if v == 0 else 0):
                    for k in (2 * b, 2 * b + 1):
                        for a in range(TT):
                            pe.wait_ge(sem["xn_ready"], a + 1)
                            c0 = (k % 2) * T + a * P
                            last = M.transpose(PS[:, 2 + b, c0:c0 + P], xn[:, a, P * k:P * k + P], ident)
                    last.then_inc(sem["xT_done"], 1)
            for j in range(4):
                pe.wait_ge(sem["modrow_ready"], j // 2 + 1)
                last = M.transpose(PS[:, 6, P * j:P * j + P], modrow[:, P * j:P * j + P], ident)
            last.then_inc(sem["modcols_done"], 1)
            keep_warm(8, 7)

            def tile(i, part=(0, KC)):
                kind, n, c0, j = TILES[i]
                if i == 0:
                    pe.wait_ge(sem["hT_dve"], 4)
                    pe.wait_ge(sem["hT_act"], 4)
                if i >= 4 and part[0] == 0:
                    before = TILES[i - 4][0]
                    if before in BY_VECTOR:
                        pe.wait_ge(sem[before + "_read"], TILES[i - 4][3] + 1)
                    else:
                        pe.wait_ge(sem["tile_read"], reads(i - 3))
                if kind == "mod":
                    last = modulate(n, 4 + i % 4, 0, part)
                elif kind == "R":
                    c = j
                    for h in range(RH):
                        for half in range(2):
                            t = slice(64 * half, 64 * half + 64)
                            o = PS[t, 4 + i % 4, HD * h:HD * h + HD]
                            last = M.matmul(o, BK[:, h, 1, 0, t], VT[:, c, HD * h:HD * h + HD], start=True, stop=(c == 0))
                            if c:
                                last = M.matmul(o, ARz[:, h // 2, h % 2, 0, t], S1[:, h // 2, :], start=False, stop=True)
                else:
                    full(n)
                    k_all = 4 if kind == "yb" else KC
                    steps = range(part[0] * k_all // KC, part[1] * k_all // KC)
                    w = unit(n)[:, 0:k_all * LOADS[n][2]].rearrange("p (k n) -> p k n", k=k_all)
                    for k in steps:
                        if kind == "vm":
                            last = M.matmul(PS[:, 4 + i % 4, :], hT[:, k, P * j:P * j + P], w[:, k, :], start=(k == 0), stop=(k == k_all - 1))
                        else:
                            x = YB if kind == "yb" else hT
                            last = M.matmul(PS[:, 4 + i % 4, 0:T], w[:, k, c0:c0 + P], x[:, k, :], start=(k == 0), stop=(k == k_all - 1))
                if part[1] < KC:
                    return
                last.then_inc(sem["tile_done"], 1)

            def begin(name):
                ps, full, free, uses = aux(name)
                if uses:
                    pe.wait_ge(free, uses)
                return ps, full

            def run(i, to):
                for j in range(i, to):
                    tile(j)

            run(0, AFTER_LORA)
            pe.wait_ge(sem["lora_loaded"], 48)
            pe.wait_ge(sem["lora_act"], 1)
            pe.wait_ge(sem["zeros_ready"], 1)
            for name, w in (("zw", w2), ("za", a2)):
                ps, done = begin(name)
                for q in range(HP):
                    last = M.matmul(ps[:, T * q:T * q + T], w[:, P * q:P * q + P], PR[:, 12, 1:257], start=True, stop=True)
                last.then_inc(done, 1)
            run(AFTER_LORA, AFTER_R)
            ps, done = begin("g")
            for q in range(HP):
                last = M.matmul(ps[:, T * q:T * q + T], g2[:, P * q:P * q + P], PR[:, 13, 1:257], start=True, stop=True)
            last.then_inc(done, 1)
            ps, done = begin("kk")
            pe.wait_ge(sem["consts_ready"], 1)
            pe.wait_ge(sem["kk_sq"], 1)
            for h in range(2):
                last = M.matmul(ps[:, 512 * h:512 * h + 512], blk, SQf[:, 512 * h:512 * h + 512], start=True, stop=True)
            last.then_inc(done, 1)
            run(AFTER_R, AFTER_Q)
            ps, done = begin("vt")
            pe.wait_ge(sem["v_shifted"], 1)
            for c in range(TT):
                for q in range(HP):
                    last = M.transpose(ps[:, 512 * c + P * q:512 * c + P * q + P], PR[:, 8 + q, 1 + P * c:1 + P * c + P], ident)
            last.then_inc(done, 1)
            run(AFTER_Q, AFTER_K)
            pe.wait_ge(sem["zeros_ready"], 1)
            pe.wait_ge(sem["tile_read"], reads(tile_at("km", 7) + 1))
            ps, done = begin("s0")
            for h in range(RH):
                last = M.matmul(ps[:, P * place(h):P * place(h) + P], Qz[h % 2][:, h // 2, 0:P], QK[:, 4 + h // 2, 0:P], start=True, stop=True)
            last.then_inc(done, 1)
            for name, h0 in (("s1a", 0), ("s1b", 4)):
                ps, done = begin(name)
                for h in range(h0, h0 + 4):
                    c0 = 512 * (h % 2) + T * ((h - h0) // 2)
                    last = M.matmul(ps[:, c0:c0 + T], Qz[h % 2][:, h // 2, P:T], QK[:, 4 + h // 2, :], start=True, stop=True)
                last.then_inc(done, 1)
            run(AFTER_K, AFTER_V)
            ps, done = begin("tok")
            pe.wait_ge(sem["ar_ready"], 1)
            for i, src in enumerate((Bf, K2f)):
                for q in range(HP):
                    last = M.transpose(ps[:, 512 * i + P * q:512 * i + P * q + P], src[:, T * q:T * q + P], ident)
            last.then_inc(done, 1)
            ps, done = begin("bonus")
            pe.wait_ge(sem["bon_ready"], 1)
            for q in range(HP):
                last = M.matmul(ps[:, T * q:T * q + T], blk, PR[:, q, 1:257], start=True, stop=True)
            last.then_inc(done, 1)
            run(AFTER_V, AFTER_PT)
            pe.wait_ge(sem["att_ready"], 1)
            for b in range(3):
                ps, done = begin(f"pt{b}")
                for h in range(RH):
                    last = M.transpose(ps[:, P * h:P * h + P], att[:, h, P * b:P * b + P], ident)
                last.then_inc(done, 1)
            run(AFTER_PT, AFTER_PV)
            ps, done = begin("pv")
            pe.wait_ge(sem["auxa_free"], AUX.index("pt2") // 2 + 1)
            pe.wait_ge(sem["tile_read"], reads(AFTER_V))
            for h in range(RH):
                r = slice(64 * (h % 2), 64 * (h % 2) + 64)
                c0 = T * (h // 2)
                v = slice(HD * h, HD * h + HD)
                M.matmul(ps[r, c0:c0 + P], VM[:, 0, v], PT[:, 0, place(h), :], start=True, stop=True)
                M.matmul(ps[r, c0 + P:c0 + T], VM[:, 0, v], PT[:, 1, place(h), :], start=True, stop=False)
                last = M.matmul(ps[r, c0 + P:c0 + T], VM[:, 1, v], PT[:, 2, place(h), :], start=False, stop=True)
            last.then_inc(done, 1)
            run(AFTER_PV, AT_CHUNK[0])

            B4 = Bf.rearrange("p (q c t) -> p q c t", q=HP, c=TT)
            K4 = K2f.rearrange("p (q c t) -> p q c t", q=HP, c=TT)
            pe.wait_ge(sem["auxa_free"], 7)
            pe.wait_ge(sem["auxb_free"], 7)
            for c in range(TT):
                at = AT_CHUNK[c]
                half = ((0, KC // 2), (KC // 2, KC))
                if c:
                    pe.wait_ge(sem["y_read"], c)
                    pe.wait_ge(sem["s_read"], c)
                    pe.wait_ge(sem["ar_next"], c)
                for q in range(HP):
                    u = HP * c + q
                    if u:
                        pe.wait_ge(sem["bk_read"], u)
                    for j, src in enumerate((B4, K4)):
                        last = M.matmul(PS[:, j, :], src[:, q, c, :], ARz[:, q].rearrange("p i a t -> p (i a t)"), start=True, stop=True)
                    last.then_inc(sem["bk_full"], 1)
                    if u:
                        pe.wait_ge(sem["x_read"], u)
                    for i in range(2):
                        last = M.matmul(PS[:, 2 + i, 0:P], ARz[:, q, i, 0, :], B4[:, q, c, :], start=True, stop=True)
                    last.then_inc(sem["x_full"], 1)
                    if q < 3:
                        tile(at, ((0, 3), (3, 6), (6, 8))[q])
                pe.wait_ge(sem["bk_read"], HP * (c + 1))
                tile(at + 1)
                pe.wait_ge(sem["x_read"], HP * (c + 1))
                for k in range(1, 7):
                    for g in range(2):
                        if k > 1:
                            pe.wait_ge(sem["level_read"], level_index(c, k - 1, "N", g) + 1)
                        else:
                            pe.wait_ge(sem["n_init"], HP * c + 2 * g + 2)
                        for h in range(4 * g, 4 * g + 4):
                            last = M.matmul(PS[:, 2 * g + 1, P * (h % 4):P * (h % 4) + P], XS[:, h, :], Nm[:, h, :], start=True, stop=True)
                        last.then_inc(sem["level_done"], 1)
                    tile(at + 2 + (k - 1) // 2, half[(k - 1) % 2])
                    if k == 1:
                        pe.wait_ge(sem["m_init"], c + 1)
                    for what in ("NM" if k < 6 else "N"):
                        for g in range(2):
                            pe.wait_ge(sem["level_read"], level_index(c, k, "T", g) + 1)
                            for h in range(4 * g, 4 * g + 4):
                                lhsT, rhs = (TL, Mm) if what == "M" else (Mm, TL)
                                last = M.matmul(PS[:, 2 * g + (what == "N"), P * (h % 4):P * (h % 4) + P], lhsT[:, h, :], rhs[:, h, :],
                                                start=True, stop=True)
                            last.then_inc(sem["level_done"], 1)
                tile(at + 5, half[0])
                pe.wait_ge(sem["level_read"], level_index(c, 6, "N", 1) + 1)
                pe.wait_ge(sem["tile_read"], reads(AT_CHUNK[c] + 2))
                for h in range(RH):
                    v = slice(HD * h, HD * h + HD)
                    for i in range(2):
                        t = slice(64 * i, 64 * i + 64)
                        last = M.matmul(PS[t, 0, v], Nm[:, h, t], Rs[:, v], start=True, stop=True)
                last.then_inc(sem["u_full"], 1)
                tile(at + 5, half[1])
                pe.wait_ge(sem["u_read"], c + 1)
                for h in range(RH):
                    v = slice(HD * h, HD * h + HD)
                    r = slice(64 * (h % 2), 64 * (h % 2) + 64)
                    o = PS[r, 2, P * (h // 2):P * (h // 2) + P]
                    M.matmul(o, Us[:, v], BK[:, h, 0, 1, :], start=True, stop=False)
                    last = M.matmul(o, VT[:, c, v], BK[:, h, 1, 1, :], start=False, stop=(c == 0))
                    if c:
                        last = M.matmul(o, S1[:, h // 2, :], ARz[:, h // 2, h % 2, 1, :], start=False, stop=True)
                last.then_inc(sem["y_full"], 1)
                if c == 0:
                    for h in range(RH):
                        v = slice(HD * h, HD * h + HD)
                        o = PS[64 * (h % 2):64 * (h % 2) + 64, 3, HD * (h // 2):HD * (h // 2) + HD]
                        M.matmul(o, Btok[:, v], Us[:, v], start=True, stop=False)
                        last = M.matmul(o, Ktok[:, v], VT[:, 0, v], start=False, stop=True)
                    last.then_inc(sem["s_full"], 1)
                tile(at + 6)

            pe.wait_ge(sem["y_read"], TT)
            for h in range(2):
                last = M.matmul(PS[:, h, :], blk, YTf[:, 512 * h:512 * h + 512], start=True, stop=True)
            last.then_inc(sem["gn_mean"], 1)
            run(AFTER_CHUNKS, AFTER_CHUNKS + 2)
            pe.wait_ge(sem["gn_c"], 1)
            for h in range(2):
                last = M.matmul(PS[:, 2 + h, :], blk, Bf[:, 512 * h:512 * h + 512], start=True, stop=True)
            last.then_inc(sem["gn_var"], 1)

            run(AFTER_CHUNKS + 2, len(TILES))

            pe.wait_ge(sem["yf_ready"], 1)
            full(U_WA)
            w = unit(U_WA).rearrange("p (k n) -> p k n", k=4)
            for m in range(KC):
                if m >= 4:
                    pe.wait_ge(sem["z_read"], m - 3)
                for q in range(HP):
                    last = M.matmul(PS[:, m % 4, 0:T], w[:, q, P * m:P * m + P], YF[:, q, :], start=(q == 0), stop=(q == HP - 1))
                last.then_inc(sem["z_full"], 1)
            pe.wait_ge(sem["yb_read"], KC)
            for a in range(TT):
                for h in range(2):
                    for k in range(KC):
                        u = U_OUT + k // 4
                        if a == h == 0:
                            if k % 4 == 0:
                                full(u)
                            pe.wait_ge(sem["z_read"], k + 1)
                        w = unit(u).rearrange("p (k n) -> p k n", k=4)
                        last = M.matmul(PS[:, 4 + 2 * a + h, :], zT[:, k, P * a:P * a + P], w[:, k % 4, 512 * h:512 * h + 512],
                                        start=(k == 0), stop=(k == KC - 1))
                    last.then_inc(sem["mix_done"], 1)

            pe.wait_ge(sem["router_loaded"], 32)
            pe.wait_ge(sem["comb_cleared"], 1)
            pe.wait_ge(sem["bias_loaded"], 16 * 8)
            for a in range(TT):
                for b in range(2):
                    pe.wait_ge(sem["h2_ready"], 2 * a + b + 1)
                    for k in range(4):
                        last = M.transpose(PS[:, 2 * a + b, P * k:P * k + P], h2[:, a, P * (4 * b + k):P * (4 * b + k) + P], ident)
                    last.then_inc(sem["h2T_full"], 1)
                if a == 0:
                    keep_warm(3, 3)
                pe.wait_ge(sem["h2T_read"], 2 * a + 2)
                for i in range(2):
                    t = slice(64 * i, 64 * i + 64)
                    for k in range(KC):
                        last = M.matmul(PS[t, 2 * a, 0:NE], h2T[:, k, P * a + 64 * i:P * a + 64 * i + 64], rw[:, k, :],
                                        start=(k == 0), stop=(k == KC - 1))
                last.then_inc(sem["logits_full"], 1)
                for h in range(2):
                    M.matmul(PS[:, 4 + 2 * a + h, :], ident, x3[:, a, 512 * h:512 * h + 512], start=True, stop=True)
                if a == 1:
                    keep_warm(2, 3)
            pe.wait_ge(sem["chosen_ready"], 1)
            strict = maskU[:, 0, :]
            M.matmul(PS[:, 1, 0:32], strict, MSK[:, 0, :], start=True, stop=True)
            M.matmul(PS[:, 1, 32:64], ones, MSK[:, 0, :], start=True, stop=False)
            M.matmul(PS[:, 1, 32:64], strict, MSK[:, 1, :], start=False, stop=True)
            M.matmul(PS[:, 1, 64:96], ones, MSK[:, 0, :], start=True, stop=False)
            M.matmul(PS[:, 1, 64:96], ones, MSK[:, 1, :], start=False, stop=True).then_inc(sem["pos_full"], 1)
            keep_warm(2, 3)
            pe.wait_ge(sem["comb_ready"], 1)
            for a in range(TT):
                last = M.transpose(PS[0:NE, 2, P * a:P * a + P], COMB[:, a, 0:NE], ident)
            last.then_inc(sem["combT_full"], 1)

            def transpose_weights(weighted):
                for a in range(TT):
                    last = M.transpose(PS[:, 0, P * a:P * a + P], weighted[:, a, :], ident)
                return last

            def gather(gathering, done):
                for k in range(KC):
                    o = PS[:, 1 + k // 4, P * (k % 4):P * (k % 4) + P]
                    for a in range(TT):
                        last = M.matmul(o, h2[:, a, P * k:P * k + P], gathering[:, a, :], start=(a == 0), stop=(a == TT - 1))
                last.then_inc(sem[done], 1)

            def combine(weighted, expert_out, done, tell_each=False):
                for a in range(TT):
                    for h in range(2):
                        last = M.matmul(PS[:, 4 + 2 * a + h, :], weighted[:, P * a:P * a + P], expert_out[:, 512 * h:512 * h + 512],
                                        start=False, stop=True, skip_group_check=True)
                    if tell_each or a == TT - 1:
                        last.then_inc(sem[done], 1)

            quarters = lambda a: a.rearrange("p (j h n) -> p j h n", j=2, h=2)
            bias_of = {"gate": quarters(bias3[:, 0:D]), "up": quarters(bias3[:, D:2 * D])}

            def project(what, slot, x, bank, c0, n, done, steps=range(KC + 1), sel=None):
                w = ring[:, slot, :].rearrange("p (k n) -> p k n", k=KC)
                js = slice(c0 // T, (c0 + n) // T)
                for s in steps:
                    for h in range(2):
                        o = PS[64 * h:64 * h + 64, bank, 0:n]
                        if s < KC:
                            last = M.matmul(o, x[:, s, :], quarters(w[:, s, :])[:, js, h, :], start=(s == 0), stop=False, tile_position=(0, 64 * h))
                        else:
                            last = M.matmul(o, selb[0:96, sel, :], bias_of[what][0:96, js, h, :], start=False, stop=True, tile_position=(0, 64 * h))
                if done:
                    last.then_inc(sem[done], 1)

            def transpose_hidden(h):
                for q in (2 * h, 2 * h + 1):
                    last = M.transpose(PS[:, 0, P * q:P * q + P], hid[:, P * q:P * q + P], ident)
                return last

            def down(slot, qs, last_done):
                w = ring[:, slot, :].rearrange("p (k n) -> p k n", k=KC)
                for q in qs:
                    for f in range(2):
                        for h in range(2):
                            last = M.matmul(PS[64 * h:64 * h + 64, 3, :], hidT[:, q, 64 * f:64 * f + 64],
                                            w[:, 4 * (q // 2) + 2 * f + q % 2, 512 * h:512 * h + 512], start=(q == 0 and f == 0), stop=(q == 3 and f == 1),
                                            tile_position=(0, 64 * h))
                if last_done:
                    last.then_inc(sem[last_done], 1)

            pe.wait_ge(sem["combT_ready"], 1)
            pe.wait_ge(sem["bias_part"], 4)
            for name in ("ov_gate", "ov_up", "ov_down"):
                pe.sem_inc(sem[name], 1)
            with pe.Fori(0, PAIRS // 2) as i:
                for pp in range(2):
                    p = 2 * i + pp
                    pe.wait_ge(sem["weighted_ready"], p + 1)
                    pe.wait_ge(sem["hidT_read"], 4 * p + 1)
                    transpose_weights(PW[:, pp]).then_inc(sem["pt_full"], 1)
                    pe.wait_ge(sem["up_read"], 4 * p + 1)
                    gather(P1[:, pp], "gather_full")
                    pe.wait_ge(sem["gather_read"], p + 1)
                    for k in range(2):
                        e = 2 * p + k
                        m = 3 * (2 * pp + k)
                        x = xe[:, pp, :, 64 * k:64 * k + 64]
                        fill = lambda j: 16 * (3 * i + j // 4 + 1)
                        pe.wait_ge(w_full[m % 4], fill(m))
                        if k:
                            pe.wait_ge(sem["hidT_read"], 4 * p + 3)
                        pe.wait_ge(sem["sel_ready"], e + 1)
                        project("gate", m % 4, x, 0, 0, 512, "gate_done", sel=k)
                        if k == 0:
                            pe.wait_ge(sem["out_read"], 2 * p + 1)
                            combine(PWT[:, 1 - pp], OUTe, "combined")
                        pe.wait_ge(w_full[(m + 1) % 4], fill(m + 1))
                        if k:
                            pe.wait_ge(sem["up_read"], 4 * p + 3)
                        project("up", (m + 1) % 4, x, 1, 0, T, "up_half_done", sel=k)
                        project("up", (m + 1) % 4, x, 2, T, T, None, steps=range(0, 6), sel=k)
                        pe.wait_ge(sem["hid_ready"], 2 * e + 1)
                        transpose_hidden(0).then_inc(sem["hidT_full"], 1)
                        project("up", (m + 1) % 4, x, 2, T, T, "up_done", steps=range(6, KC + 1), sel=k)
                        pe.wait_ge(down_half[k], 16 * (p + 1))
                        pe.wait_ge(sem["hidT_read"], 2 * e + 2)
                        if k:
                            pe.wait_ge(sem["out_read"], e + 1)
                        down((m + 2) % 4, (0, 1), None)
                        pe.wait_ge(sem["hid_ready"], 2 * e + 2)
                        transpose_hidden(1).then_inc(sem["hidT_full"], 1)
                        pe.wait_ge(w_full[(m + 2) % 4], fill(m + 2))
                        pe.wait_ge(sem["hidT_read"], 2 * e + 3)
                        down((m + 2) % 4, (2, 3), "down_done")
                        with further_turns(pe, e) as c:
                            pe.wait_ge(sem["ov_onehot"], c)
                            transpose_weights(PWF)
                            gather(P1F, "ov_gather")
                            pe.wait_ge(sem["ov_copied"], c)
                            project("gate", m % 4, xeF, 0, 0, 512, "ov_gate", sel=k)
                            project("up", (m + 1) % 4, xeF, 1, 0, T, None, sel=k)
                            project("up", (m + 1) % 4, xeF, 2, T, T, "ov_up", sel=k)
                            pe.wait_ge(sem["ov_hid"], c)
                            transpose_hidden(0)
                            transpose_hidden(1).then_inc(sem["ov_hidT"], 1)
                            pe.wait_ge(sem["ov_hidTc"], c)
                            pe.wait_ge(sem["out_read"], e + 2)
                            down((m + 2) % 4, (0, 1, 2, 3), "ov_down")
                            pe.wait_ge(sem["ov_out"], c)
                            combine(PWTF, OUTF, "ov_comb")
            pe.wait_ge(sem["out_read"], NE + 1)
            combine(PWT[:, 1], OUTe, "y_ready", tell_each=True)


_INS = ["x", "c", "w_ada", "b_ada", "norm1_g", "w_in", "rwkv_mu", "rwkv_w0", "rwkv_w2", "rwkv_a0", "rwkv_a2",
        "rwkv_g2", "rwkv_k_k", "rwkv_k_a", "rwkv_r_k", "rwkv_ln_w", "rwkv_ln_b", "w_branch_a", "w_branch_b",
        "w_out", "norm2_g", "router_w", "router_b", "exp_w_gate", "exp_b_gate", "exp_w_up", "exp_b_up",
        "exp_w_down", "exp_b_down", "normf_g"]


def kernel(**inputs):
    import concourse.bacc as bacc
    import numpy as np
    from concourse.bass_utils import run_bass_kernel_spmd

    nc = bacc.Bacc("TRN2", target_bir_lowering=False, num_devices=1)
    arrays, aps = {}, {}
    for name in _INS:
        a = np.ascontiguousarray(inputs[name])
        arrays[f"in_{name}"] = a
        aps[name] = nc.dram_tensor(f"in_{name}", a.shape, mybir.dt.from_np(a.dtype), kind="ExternalInput").ap()
    out = nc.dram_tensor("out_0", (1, T, D), F32, kind="ExternalOutput").ap()
    scratch = nc.dram_tensor("mod_rows", (8, 512), F32, kind="Internal").ap()
    block_kernel(nc, aps, out, scratch)
    r = run_bass_kernel_spmd(nc, [arrays], core_ids=[0])
    return r.results[0]["out_0"]
```
